# Optimizing a Trainium2 kernel written in Bass

```python
import jax, jax.numpy as jnp
from jax import lax
import numpy as np

D_MODEL = 1024
BATCH = 1
SEQ = 256
DEPTH = 1

CHUNK = 64
HEAD_DIM = 64
ATT_WIDTH = D_MODEL // 2
ATT_HEADS = ATT_WIDTH // HEAD_DIM
LEFT_CHUNKS = 8
BAND = LEFT_CHUNKS + 1
MAX_LEFT_REL = 128
REL_TABLE = MAX_LEFT_REL + CHUNK
RWKV_HEAD = 64
RWKV_WIDTH = D_MODEL - ATT_WIDTH
RWKV_HEADS = RWKV_WIDTH // RWKV_HEAD
DECAY_LORA = 64
AAA_LORA = 64
GATE_LORA = 128
RWKV_COLS = 3 * RWKV_WIDTH + DECAY_LORA + AAA_LORA + GATE_LORA
IN_COLS = 3 * ATT_WIDTH + RWKV_COLS
MIX_WIDTH = ATT_WIDTH + RWKV_WIDTH
LN_X_EPS = 64e-5
N_EXPERTS = 32
TOP_K = 4
D_EXPERT = D_MODEL
SWIGLU_ALPHA = 1.702
SWIGLU_LIMIT = 7.0
MOE_BLOCK = 256
NORM_EPS = 1e-6

kernel_name = "hymba_chunkattn_rwkv7_moe_block"

def rms_norm(x, g):
    xf = x.astype(jnp.float32)
    y = xf * lax.rsqrt(jnp.mean(xf * xf, axis=-1, keepdims=True) + NORM_EPS)
    return (y * g.astype(jnp.float32)).astype(x.dtype)

def chunk_band_attention(q, k, v, rel_bias):
    B, S = q.shape[:2]
    NC = S // CHUNK

    def to_chunks(t):
        return t.reshape(B, NC, CHUNK, ATT_HEADS, HEAD_DIM).transpose(0, 3, 1, 2, 4)

    qc = to_chunks(q) * (HEAD_DIM ** -0.5)
    pad = ((0, 0), (0, 0), (LEFT_CHUNKS, 0), (0, 0), (0, 0))
    kp = jnp.pad(to_chunks(k), pad)
    vp = jnp.pad(to_chunks(v), pad)
    scores = jnp.stack(
        [jnp.einsum('bhncd,bhnkd->bhnck', qc, kp[:, :, j:j + NC]) for j in range(BAND)],
        axis=-2).astype(jnp.float32)
    qi = jnp.arange(CHUNK)[:, None, None]
    bj = jnp.arange(BAND)[None, :, None]
    kc = jnp.arange(CHUNK)[None, None, :]
    rel = (bj - LEFT_CHUNKS) * CHUNK + kc - qi
    idx = jnp.clip(rel, -MAX_LEFT_REL, CHUNK - 1) + MAX_LEFT_REL
    bias = rel_bias[:, idx].astype(jnp.float32)
    valid = (jnp.arange(NC)[:, None] + jnp.arange(BAND)[None, :]) >= LEFT_CHUNKS
    scores = jnp.where(valid[None, None, :, None, :, None],
                       scores + bias[None, :, None],
                       jnp.finfo(jnp.float32).min)
    probs = jax.nn.softmax(scores.reshape(B, ATT_HEADS, NC, CHUNK, BAND * CHUNK), axis=-1)
    probs = probs.reshape(scores.shape).astype(v.dtype)
    out = jnp.einsum('bhnck,bhnkd->bhncd', probs[..., 0, :], vp[:, :, 0:NC])
    for j in range(1, BAND):
        out = out + jnp.einsum('bhnck,bhnkd->bhncd', probs[..., j, :], vp[:, :, j:j + NC])
    return out.transpose(0, 2, 3, 1, 4).reshape(B, S, ATT_WIDTH)

def rwkv7_scan(r, w, k, v, kk, a):
    B, S, H, N = r.shape

    def step(state, inp):
        r_t, w_t, k_t, v_t, kk_t, a_t = inp
        sa = jnp.einsum('bhvk,bhk->bhv', state, -kk_t)
        state = (state * w_t[:, :, None, :]
                 + sa[..., None] * (kk_t * a_t)[:, :, None, :]
                 + v_t[..., None] * k_t[:, :, None, :])
        y = jnp.einsum('bhvk,bhk->bhv', state, r_t)
        return state, y

    xs = tuple(jnp.moveaxis(t, 1, 0) for t in (r, w, k, v, kk, a))
    state0 = jnp.zeros((B, H, N, N), jnp.float32)
    _, ys = lax.scan(step, state0, xs)
    return jnp.moveaxis(ys, 0, 1)

def rwkv7_mixer(p, mu, w0, w_decay_up, a0, w_aaa_up, w_gate_up, k_k, k_a, r_k, ln_g, ln_b):
    B, S, _ = p.shape
    f32 = jnp.float32
    prev = jnp.pad(p, ((0, 0), (1, 0), (0, 0)))[:, :S]
    p = p + (prev - p) * mu
    C = RWKV_WIDTH
    r, k, v, wd, ad, gd = jnp.split(
        p, [C, 2 * C, 3 * C, 3 * C + DECAY_LORA, 3 * C + DECAY_LORA + AAA_LORA], axis=-1)
    w_logit = (w0 + jnp.tanh(wd) @ w_decay_up).astype(f32)
    decay = jnp.exp(-jnp.exp(-jax.nn.softplus(-w_logit) - 0.5))
    a = jax.nn.sigmoid((a0 + ad @ w_aaa_up).astype(f32))
    g = jax.nn.sigmoid(gd) @ w_gate_up

    def heads(t):
        return t.reshape(B, S, RWKV_HEADS, RWKV_HEAD).astype(f32)

    r, k, v, decay, a = heads(r), heads(k), heads(v), heads(decay), heads(a)
    kk = k * k_k.astype(f32)
    kk = kk / jnp.maximum(jnp.linalg.norm(kk, axis=-1, keepdims=True), 1e-12)
    k = k * (1.0 + (a - 1.0) * k_a.astype(f32))
    y = rwkv7_scan(r, decay, k, v, kk, a)
    mean = jnp.mean(y, axis=-1, keepdims=True)
    var = jnp.mean(jnp.square(y - mean), axis=-1, keepdims=True)
    y = ((y - mean) * lax.rsqrt(var + LN_X_EPS)).reshape(B, S, C)
    y = y * ln_g.astype(f32) + ln_b.astype(f32)
    bonus = jnp.sum(r * k * r_k.astype(f32), axis=-1, keepdims=True) * v
    y = (y + bonus.reshape(B, S, C)) * g.astype(f32)
    return y.astype(p.dtype)

def moe_ffn(xn, w_router, b_router, w_up, b_up, w_down, b_down):
    B, S, D = xn.shape
    T = B * S
    xf = xn.reshape(T, D)
    logits = (xf @ w_router).astype(jnp.float32) + b_router.astype(jnp.float32)
    top_vals, top_idx = lax.top_k(logits, TOP_K)
    gates = jax.nn.softmax(top_vals, axis=-1).astype(xn.dtype)
    A = T * TOP_K
    e_flat = top_idx.reshape(A).astype(jnp.int32)
    t_flat = jnp.repeat(jnp.arange(T, dtype=jnp.int32), TOP_K)
    g_flat = gates.reshape(A)
    counts = jnp.bincount(e_flat, length=N_EXPERTS).astype(jnp.int32)
    padded = (counts + MOE_BLOCK - 1) // MOE_BLOCK * MOE_BLOCK
    pad_end = jnp.cumsum(padded)
    pad_start = pad_end - padded
    start = jnp.cumsum(counts) - counts
    order = jnp.argsort(e_flat)
    e_sorted = e_flat[order]
    dest = pad_start[e_sorted] + jnp.arange(A, dtype=jnp.int32) - start[e_sorted]
    n_blocks = -(-A // MOE_BLOCK) + N_EXPERTS
    n_rows = n_blocks * MOE_BLOCK
    row_tok = jnp.full((n_rows,), T, jnp.int32).at[dest].set(t_flat[order])
    row_gate = jnp.zeros((n_rows,), xn.dtype).at[dest].set(g_flat[order])
    blk_start = jnp.arange(n_blocks, dtype=jnp.int32) * MOE_BLOCK
    blk_expert = jnp.minimum(jnp.searchsorted(pad_end, blk_start, side='right'), N_EXPERTS - 1)
    x_pad = jnp.concatenate([xf, jnp.zeros((1, D), xf.dtype)], axis=0)

    def expert_block(args):
        tok, gate, e = args
        h = x_pad[tok] @ w_up[e] + b_up[e]
        h_glu = jnp.minimum(h[:, :D_EXPERT], SWIGLU_LIMIT)
        h_lin = jnp.clip(h[:, D_EXPERT:], -SWIGLU_LIMIT, SWIGLU_LIMIT)
        act = h_glu * jax.nn.sigmoid(SWIGLU_ALPHA * h_glu) * (h_lin + 1.0)
        return (act @ w_down[e] + b_down[e]) * gate[:, None]

    y_rows = lax.map(expert_block, (row_tok.reshape(n_blocks, MOE_BLOCK),
                                    row_gate.reshape(n_blocks, MOE_BLOCK),
                                    blk_expert))
    y = jax.ops.segment_sum(y_rows.reshape(n_rows, D), row_tok, num_segments=T + 1)[:T]
    return y.reshape(B, S, D).astype(xn.dtype)

def setup_inputs(seed: int = 0) -> dict:
    key = jax.random.key(seed)
    ks = jax.random.split(key, 32)
    L = DEPTH

    def nrm(k, shape, scale):
        return jax.random.normal(k, shape, jnp.float32) * scale

    return {
        "x": nrm(ks[0], (BATCH, SEQ, D_MODEL), 1.0),
        "norm1_g": 1.0 + nrm(ks[1], (L, D_MODEL), 0.01),
        "w_in": nrm(ks[2], (L, D_MODEL, IN_COLS), D_MODEL ** -0.5),
        "tshift_mu": jax.random.uniform(ks[3], (L, RWKV_COLS), jnp.float32),
        "q_norm_g": 1.0 + nrm(ks[4], (L, HEAD_DIM), 0.01),
        "k_norm_g": 1.0 + nrm(ks[5], (L, HEAD_DIM), 0.01),
        "rel_bias": nrm(ks[6], (L, ATT_HEADS, REL_TABLE), 0.5),
        "w0": nrm(ks[7], (L, RWKV_WIDTH), 0.5),
        "w_decay_up": nrm(ks[8], (L, DECAY_LORA, RWKV_WIDTH), 0.5 * DECAY_LORA ** -0.5),
        "a0": nrm(ks[9], (L, RWKV_WIDTH), 0.5),
        "w_aaa_up": nrm(ks[10], (L, AAA_LORA, RWKV_WIDTH), 0.5 * AAA_LORA ** -0.5),
        "w_gate_up": nrm(ks[11], (L, GATE_LORA, RWKV_WIDTH), GATE_LORA ** -0.5),
        "k_k": 1.0 + nrm(ks[12], (L, RWKV_HEADS, RWKV_HEAD), 0.1),
        "k_a": 1.0 + nrm(ks[13], (L, RWKV_HEADS, RWKV_HEAD), 0.1),
        "r_k": nrm(ks[14], (L, RWKV_HEADS, RWKV_HEAD), 0.1),
        "ln_x_g": 1.0 + nrm(ks[15], (L, RWKV_WIDTH), 0.01),
        "ln_x_b": nrm(ks[16], (L, RWKV_WIDTH), 0.01),
        "w_out": nrm(ks[17], (L, MIX_WIDTH, D_MODEL), MIX_WIDTH ** -0.5),
        "norm2_g": 1.0 + nrm(ks[18], (L, D_MODEL), 0.01),
        "w_router": nrm(ks[19], (L, D_MODEL, N_EXPERTS), D_MODEL ** -0.5),
        "b_router": nrm(ks[20], (L, N_EXPERTS), 0.01),
        "w_up": nrm(ks[21], (L, N_EXPERTS, D_MODEL, 2 * D_EXPERT), D_MODEL ** -0.5),
        "b_up": nrm(ks[22], (L, N_EXPERTS, 2 * D_EXPERT), 0.01),
        "w_down": nrm(ks[23], (L, N_EXPERTS, D_EXPERT, D_MODEL), D_EXPERT ** -0.5),
        "b_down": nrm(ks[24], (L, N_EXPERTS, D_MODEL), 0.01),
    }

def reference(x, norm1_g, w_in, tshift_mu, q_norm_g, k_norm_g, rel_bias, w0, w_decay_up,
              a0, w_aaa_up, w_gate_up, k_k, k_a, r_k, ln_x_g, ln_x_b, w_out, norm2_g,
              w_router, b_router, w_up, b_up, w_down, b_down):
    B, S, _ = x.shape
    for l in range(DEPTH):
        h = rms_norm(x, norm1_g[l])
        proj = h @ w_in[l]
        aq, ak, av, p_rwkv = jnp.split(proj, [ATT_WIDTH, 2 * ATT_WIDTH, 3 * ATT_WIDTH], axis=-1)
        q = rms_norm(aq.reshape(B, S, ATT_HEADS, HEAD_DIM), q_norm_g[l])
        k = rms_norm(ak.reshape(B, S, ATT_HEADS, HEAD_DIM), k_norm_g[l])
        v = av.reshape(B, S, ATT_HEADS, HEAD_DIM)
        att = chunk_band_attention(q, k, v, rel_bias[l])
        rwk = rwkv7_mixer(p_rwkv, tshift_mu[l], w0[l], w_decay_up[l], a0[l], w_aaa_up[l],
                          w_gate_up[l], k_k[l], k_a[l], r_k[l], ln_x_g[l], ln_x_b[l])
        x = x + (jnp.concatenate([att, rwk], axis=-1) @ w_out[l]).astype(x.dtype)
        x = x + moe_ffn(rms_norm(x, norm2_g[l]), w_router[l], b_router[l], w_up[l], b_up[l],
                        w_down[l], b_down[l])
    return x


_drawn_inputs = setup_inputs


def setup_inputs(seed=0):
    import zlib

    import numpy as np

    out = dict(_drawn_inputs(seed))
    spreads = {}
    factors = {'q_norm_g': 6.223,
     'k_norm_g': 7.005,
     'ln_x_g': 3.427,
     'ln_x_b': 3.012,
     'b_up': 8.0,
     'b_down': 8.0}
    for name, (base, spread) in spreads.items():
        noise = np.random.default_rng([zlib.crc32(name.encode()), seed]).standard_normal(out[name].shape)
        drawn = base * np.exp(spread * noise) if base else spread * noise
        out[name] = __import__('jax').numpy.asarray(drawn.astype(out[name].dtype))
    for name, factor in factors.items():
        out[name] = (out[name] * factor).astype(out[name].dtype)
    return out
```

```python
from contextlib import ExitStack

import concourse.bass as bass
from concourse import mybir

P = 128
F32 = mybir.dt.float32
U32 = mybir.dt.uint32
I32 = mybir.dt.int32
ALU = mybir.AluOpType
ACT = mybir.ActivationFunctionType
AX = mybir.AxisListType

D = 1024
T = 256
TT = T // P
KD = D // P
H = 8
NP = H // 2
HD = 64
W = H * HD
NRW = 14
NC = 32
NQ = P // NC
NS = H * TT
E = 32
CAP = 64
EXP_M05 = 0.6065306597126334
NEG = -3.0e38
CST = 1328
SLOT = 2048
PRE_SLOTS = 7
MOE_SLOTS = 12

TOP_K = 4
ALPHA, LIMIT = 1.702, 7.0
RW_GROUPS = [6, 2, 3, 0, 1, 4, 5]
AT_GROUPS = [0, 1, 2, 3, 4, 5]


def slot_of(n):
    return n % PRE_SLOTS


def set_of(h, tt):
    return (h % 2) * NS // 2 + (h // 2) * TT + tt


def hybrid_block(nc, x, norm1_g, w_in, tshift_mu, q_norm_g, k_norm_g, rel_bias, w0, w_decay_up,
                 a0, w_aaa_up, w_gate_up, k_k, k_a, r_k, ln_x_g, ln_x_b, w_out, norm2_g,
                 w_router, b_router, w_up, b_up, w_down, b_down, out):
    with ExitStack() as ctx:
        def sb(name, shape, dt=F32):
            return ctx.enter_context(nc.sbuf_tensor(name, shape, dt))

        def sem(name):
            return ctx.enter_context(nc.semaphore(name))

        ring = sb("ring", [P, PRE_SLOTS * SLOT])
        xs = sb("xs", [P, TT, D])
        cst = sb("cst", [P, CST])
        arena_cols = 34850
        arena = sb("arena", [P, arena_cols])
        bank = [ctx.enter_context(nc.psum_tensor(f"bank{i}", [P, 512], F32)) for i in range(8)]

        class Area:
            def __init__(self, t, start, end):
                self.t, self.at, self.end = t, start, end

            def take(self, *dims):
                n = 1
                for d in dims:
                    n *= d
                a = self.t[:, self.at:self.at + n]
                self.at += n
                assert self.at <= self.end, (self.at, self.end)
                if len(dims) > 1:
                    names = "abcde"[:len(dims)]
                    a = a.rearrange(f"p ({' '.join(names)}) -> p {' '.join(names)}",
                                    **{n_: d_ for n_, d_ in zip(names[1:], dims[1:])})
                return a

        c = Area(cst, 0, CST)
        ident = c.take(P)
        half_ones = c.take(P)
        gmask = c.take(2, P)
        blk = c.take(NQ, NC)
        id64 = c.take(HD)
        keep = c.take(T)
        eps = c.take(4)
        nought = c.take(P)
        zeroed = c.at
        vec = c.take(60)
        stat = c.take(100)
        (V_G1, V_MU, V_W0, V_A0, V_KK, V_KA, V_RK, V_LG, V_LB, V_QG, V_KG) = (
            0, 8, 22, 26, 30, 34, 38, 42, 46, 50, 51)
        NVEC = 52

        a = Area(arena, 0, arena_cols)
        ar = a.take(NP * TT, 2, P)
        be = a.take(NP, T)
        ka = a.take(NP, T)
        bend = a.take(NP, T)
        kend = a.take(NP, T)
        gate = a.take(NP, T)
        bonus = a.take(NP, T)
        lora = a.take(2, T)
        pend = a.take(NP, T // NC)
        ht_at = a.at
        wu = a.take(H, P)
        rr = a.take(H, P)
        ht = Area(arena, ht_at, a.at).take(KD, T)
        vtok_at = a.at
        vtok = a.take(TT, W)
        rt = a.take(NP, P)
        st = a.take(NP, NQ + 1, HD)
        mt = a.take(NP, NQ, HD)
        qk_sq = Area(arena, vtok_at, a.at).take(4 * W)
        yy_at = a.at
        yy = a.take(NP, T)
        z = Area(arena, yy_at, a.at)
        lora_w = z.take(T)
        lora_a = z.take(T)
        lora_g = z.take(T)
        rows = z.take(P)
        e0 = a.at
        sg = a.take(NP, T)
        ls = a.take(NP, T)
        tm2 = a.take(NP, T)
        aa = a.take(NP, T)
        kk = a.take(NP, T)
        tmp = a.take(NP, T)
        mr = a.take(NP, T)
        mk = a.take(NP, T)
        mv = a.take(NP, T)
        raw = a.take(2, T + 1)
        dd = a.take(2, T)
        z = Area(arena, e0, e0 + 3 * NP * T)
        prob = z.take(NC, NC)
        xt = z.take(NC // 2, NC)
        xtmp = z.take(NC // 2, NC)
        acol = z.take(NS, NC)
        dt = z.take(NS, NC)
        bbd = Area(arena, e0, e0 + 2048).take(H, NQ, HD)
        z = Area(arena, e0 + 3 * NP * T, a.at)
        gm = z.take(H, 4, P)
        ttb = z.take(H, P)
        kbd = z.take(H, NQ, HD)
        tmpn = gm[:, 2:4, :, :].rearrange("p h g t -> p (h g t)").rearrange("p (b t) -> p b t", b=NP)
        sqy = gm[:, 0:2, :, :].rearrange("p h g t -> p (h g t)").rearrange("p (b t) -> p b t", b=NP)
        qk_at = a.at
        qk = a.take(TT, 2, W)
        htok = Area(arena, qk_at, a.at).take(TT, D)
        sc = Area(arena, qk_at, a.at).take(4, 3 * P)
        pt = a.take(2, 3 * P)
        qt = a.take(NP, T)
        kt = a.take(NP, T)
        va = a.take(TT, W)
        eb = a.take(H, T)
        at_at = a.at
        at = a.take(NP, T)
        z = Area(arena, at_at, a.at)
        wup = z.take(W)
        wgu = z.take(W)

        z = Area(arena, 0, NP * TT * 2 * P + 4 * NP * T)
        xn = z.take(TT, D)
        eb_up = z.take(2 * D)
        eb_dn = z.take(D)
        g2 = z.take(D)
        moe_at = z.at
        z = Area(arena, yy_at - KD * E - 4, yy_at)
        wr = z.take(KD, E)
        br = z.take(1)
        z = Area(arena, moe_at, yy_at - KD * E - 4)
        xnt = z.take(KD, T)
        z = Area(arena, moe_at, z.end)
        xg = z.take(512)
        xgt = z.take(4, P)
        glu = z.take(512)
        sig = z.take(512)
        z.take(2)
        lin = z.take(512)
        acts = z.take(512)
        actt = z.take(4, P)
        ye = z.take(512)
        sct = z.take(2, TT, P)
        pick = z.take(TT, CAP)
        gated = z.take(TT, 4, CAP)
        chosen = z.take(CAP)
        lgt = z.take(T)
        logits = z.take(TT, E)
        top = z.take(TT, 8)
        topn = z.take(TT)
        tope = z.take(TT, TOP_K)
        tops = z.take(TT)
        topi = z.take(TT, TOP_K)
        hot = z.take(TT * TOP_K, E)
        hotg = z.take(TT * TOP_K, E)
        member = z.take(TT, E)
        gates = z.take(TT, E)
        place = z.take(TT, E + 1)
        counts = z.take(E)
        most = z.take(1)
        iota = z.take(CAP)
        before = z.take(P)
        ones = z.take(P)
        slot_at = ([(ring, j * SLOT) for j in range(PRE_SLOTS)]
                   + [(arena, qk_at + j * SLOT) for j in range(3)]
                   + [(arena, e0 + j * SLOT) for j in range(2)])
        assert qk_at + 3 * SLOT <= at_at
        topi_u = sb("topi_u", [P, TT, 8], U32)
        most_u = sb("most_u", [P, 1], U32)
        iota_i = sb("iota_i", [P, CAP], I32)

        bias_d = nc.dram_tensor("bias_scratch", (H, 384), F32, kind="Internal").ap()
        skew_d = nc.dram_tensor("skew_scratch", (P, H * 384), F32, kind="Internal").ap()
        acol_d = nc.dram_tensor("acol_scratch", (P, NS * NC), F32, kind="Internal").ap()
        inv_d = nc.dram_tensor("inv_scratch", (P, NC * NC // 2), F32, kind="Internal").ap()

        x_in = [sem(f"x_in{i}") for i in range(TT)]
        rows_in = sem("rows_in")
        lora_in = sem("lora_in")
        slot_full = [sem(f"slot_full{i}") for i in range(PRE_SLOTS)]
        act_chain = sem("act_chain")
        vec_chain = sem("vec_chain")
        pool_chain = sem("pool_chain")
        consts = sem("consts")
        bias_ext = sem("bias_ext")
        bias_dram = sem("bias_dram")
        bias_in = sem("bias_in")
        bias_ok = sem("bias_ok")
        rms_root = sem("rms_root")
        h_tok = sem("h_tok")
        rows_ps = sem("rows_ps")
        vec_ok = sem("vec_ok")
        ht_ps = sem("ht_ps")
        ht_ok = sem("ht_ok")
        proj_ps = sem("proj_ps")
        proj_out = sem("proj_out")
        mixed = sem("mixed")
        lora_act = sem("lora_act")
        lora_ps = sem("lora_ps")
        lora_out = sem("lora_out")
        kk_ok = sem("kk_ok")
        kk_sq = sem("kk_sq")
        kk_ps = sem("kk_ps")
        kk_root = sem("kk_root")
        ls_ok = sem("ls_ok")
        shifted = sem("shifted")
        exps = sem("exps")
        alpha_beta = sem("alpha_beta")
        rank_ok = sem("rank_ok")
        bonus_in = sem("bonus_in")
        bonus_ps = sem("bonus_ps")
        elem_ok = sem("elem_ok")
        ends_ok = sem("ends_ok")
        acol_ps = sem("acol_ps")
        acol_ok = sem("acol_ok")
        acol_dram = sem("acol_dram")
        prob_in = sem("prob_in")
        xt_zero = sem("xt_zero")
        inv_ok = sem("inv_ok")
        inv_dram = sem("inv_dram")
        dt_in = sem("dt_in")
        qk_sqd = sem("qk_sqd")
        qk_sum = sem("qk_sum")
        qk_root = sem("qk_root")
        qk_ok = sem("qk_ok")
        qkt_ps = sem("qkt_ps")
        qkt_ok = sem("qkt_ok")
        sc_ps = sem("sc_ps")
        sc_max = sem("sc_max")
        sc_exp = sem("sc_exp")
        probs_ok = sem("probs_ok")
        pt_ps = sem("pt_ps")
        pt_ok = sem("pt_ok")
        at_ps = sem("at_ps")
        at_ok = sem("at_ok")
        v_ps = sem("v_ps")
        v_ok = sem("v_ok")
        turn_ps = sem("turn_ps")
        turn_ok = sem("turn_ok")
        gm_ps = sem("gm_ps")
        gm_ok = sem("gm_ok")
        ttb_ok = sem("ttb_ok")
        akv_ps = sem("akv_ps")
        akv_ok = sem("akv_ok")
        wu_ps = sem("wu_ps")
        wu_ok = sem("wu_ok")
        rm_ps = sem("rm_ps")
        rm_ok = sem("rm_ok")
        diag_ok = sem("diag_ok")
        st_ps = sem("st_ps")
        st_ok = sem("st_ok")
        y_ps = sem("y_ps")
        y_ok = sem("y_ok")
        ln_ps = sem("ln_ps")
        ln_sq = sem("ln_sq")
        ln_root = sem("ln_root")
        rw_ok = sem("rw_ok")
        wo_used = sem("wo_used")
        res_ok = sem("res_ok")
        masked_ok = sem("masked_ok")
        wo_slot = sem("wo_slot")
        moe_consts = sem("moe_consts")
        moe_in = sem("moe_in")
        n2_root = sem("n2_root")
        xn_ok = sem("xn_ok")
        xnt_ps = sem("xnt_ps")
        xnt_ok = sem("xnt_ok")
        lgt_ps = sem("lgt_ps")
        lgt_ok = sem("lgt_ok")
        logit_ps = sem("logit_ps")
        top_ok = sem("top_ok")
        top_exp = sem("top_exp")
        member_ok = sem("member_ok")
        place_ps = sem("place_ps")
        routed = sem("routed")
        acc_x = sem("acc_x")
        expert_in = [sem(f"expert_in{i}") for i in range(PRE_SLOTS, MOE_SLOTS)]
        slot_used = sem("slot_used")
        pick_ok = sem("pick_ok")
        xg_ps = sem("xg_ps")
        xg_ok = sem("xg_ok")
        xgt_ps = sem("xgt_ps")
        xgt_ok = sem("xgt_ok")
        chosen_ok = sem("chosen_ok")
        gated_ok = sem("gated_ok")
        up_ps = sem("up_ps")
        glu_ok = sem("glu_ok")
        sig_ok = sem("sig_ok")
        acts_ok = sem("acts_ok")
        actt_ps = sem("actt_ps")
        actt_ok = sem("actt_ok")
        sct_ps = sem("sct_ps")
        sct_ok = sem("sct_ok")
        down_ps = sem("down_ps")
        ye_ok = sem("ye_ok")
        combined = sem("combined")
        lin_ok = sem("lin_ok")
        gl_ok = sem("gl_ok")
        moved = sem("moved")
        out_ok = sem("out_ok")
        stored = sem("stored")

        n_proj = len(RW_GROUPS) + len(AT_GROUPS)
        n_wout = KD // 2
        w_in_v = w_in[0].rearrange("(k p) n -> p k n", p=P)
        w_out_v = w_out[0].rearrange("(k p) n -> p k n", p=P)
        cols = [3 * W + 256 * g for g in RW_GROUPS] + [256 * g for g in AT_GROUPS]

        def slot(s):
            return ring[:, s * SLOT:(s + 1) * SLOT]

        def expert_slot(j):
            t_, a0_ = slot_at[j]
            return t_[:, a0_:a0_ + SLOT]

        full = slot_full + expert_in
        earlier = [sum(slot_of(n) == j for n in range(n_proj + n_wout)) for j in range(PRE_SLOTS)]
        earlier += [0] * (MOE_SLOTS - PRE_SLOTS)
        PASSES = T // CAP

        def rows_of(h):
            return slice(HD * (h % 2), HD * (h % 2) + HD)

        block = ctx.enter_context(nc.Block())

        @block.sync
        def _(sp):
            for tt in range(TT):
                sp.dma_start(xs[:, tt, :], x[0, tt * P:(tt + 1) * P, :]).then_inc(x_in[tt], 16)
            for n in range(n_proj + n_wout):
                if n >= PRE_SLOTS:
                    sp.wait_ge(proj_ps, n - PRE_SLOTS + 1)
                if n < n_proj:
                    dst = slot(slot_of(n)).rearrange("p (k n) -> p k n", k=KD)
                    src = w_in_v[:, :, cols[n]:cols[n] + 256]
                else:
                    j = n - n_proj
                    dst = slot(slot_of(n)).rearrange("p (k n) -> p k n", k=2)
                    src = w_out_v[:, 2 * j:2 * j + 2, :]
                sp.dma_start(dst, src).then_inc(slot_full[slot_of(n)], 16)

            def load_expert(e, j):
                if j < KD:
                    src = w_up[0, e, P * j:P * (j + 1), :]
                    dst = expert_slot(j)
                else:
                    r0 = 2 * P * (j - KD)
                    src = w_down[0, e, r0:r0 + 2 * P, :].rearrange("(k p) n -> p k n", p=P)
                    dst = expert_slot(j).rearrange("p (k n) -> p k n", k=2)
                return sp.dma_start(dst, src).then_inc(full[j], 16)

            for j in (3, 4, 5):
                sp.wait_ge(proj_ps, PRE_SLOTS + j + 1)
                load_expert(0, j)
            sp.wait_ge(at_ok, 2)
            for j in (7, 8, 9):
                load_expert(0, j)
            for i, j in enumerate((6, 0)):
                sp.wait_ge(wo_slot, i + 1)
                load_expert(0, j)
            sp.wait_ge(rw_ok, 1)
            for j in (10, 11):
                load_expert(0, j)
            sp.wait_ge(wo_slot, 3)
            load_expert(0, 1)
            sp.wait_ge(wo_used, 4)
            load_expert(0, 2)

            def stream(e, i):
                for j in range(MOE_SLOTS):
                    sp.wait_ge(slot_used, MOE_SLOTS * i + (j + 1 - MOE_SLOTS))
                    load_expert(e, j)

            with sp.Fori(1, E) as e:
                stream(e, e)
            sp.wait_ge(routed, 1)
            crowd = sp.value_load(most_u[0:1, 0:1])
            with sp.If(crowd > CAP):
                with sp.Fori(1, PASSES) as p_:
                    with sp.Fori(0, E) as e:
                        stream(e, p_ * E + e)
            for i in range(4):
                sp.wait_ge(out_ok, i + 1)
                tt, j = i // 2, i % 2
                sp.dma_start(out[0, P * tt:P * (tt + 1), 512 * j:512 * (j + 1)],
                             xs[:, tt, 512 * j:512 * (j + 1)]).then_inc(stored, 16)
            sp.wait_ge(stored, 64)

        @block.gpsimd
        def _(pool):
            n_own = [0]

            def own(ins):
                n_own[0] += 1
                ins.then_inc(pool_chain, 1)
                pool.wait_ge(pool_chain, n_own[0])

            g = nc.gpsimd
            own(g.memset(cst[:, 0:zeroed], 0.0))
            own(g.memset(half_ones[0:HD, 0:HD], 1.0))
            own(g.memset(half_ones[HD:P, HD:P], 1.0))
            for q in range(NQ):
                own(g.memset(blk[NC * q:NC * (q + 1), q, :], 1.0))
            own(g.memset(keep, 1.0))
            own(g.memset(keep.rearrange("p (c t) -> p c t", t=NC)[:, :, 0:1], 0.0))
            own(g.memset(eps[:, 0:1], 1e-6))
            own(g.memset(eps[:, 1:2], 64e-5))
            own(g.affine_select(out=ident, in_=ident, compare_op=ALU.not_equal, fill=1.0, base=0,
                                pattern=[[-1, P]], channel_multiplier=1))
            for half in range(2):
                part = id64[HD * half:HD * (half + 1), :]
                own(g.affine_select(out=part, in_=part, compare_op=ALU.not_equal, fill=1.0, base=0,
                                    pattern=[[-1, HD]], channel_multiplier=1))
            bf = blk.rearrange("p q t -> p (q t)")
            own(g.affine_select(out=gmask[:, 0, :], in_=bf, compare_op=ALU.is_gt, fill=0.0, base=0,
                                pattern=[[1, P]], channel_multiplier=-1))
            g.affine_select(out=gmask[:, 1, :], in_=bf, compare_op=ALU.is_ge, fill=0.0, base=0,
                            pattern=[[1, P]], channel_multiplier=-1).then_inc(consts, 1)
            pool.wait_ge(consts, 1)
            g.memset(lora_w[HD:P, :], 0.0).then_inc(consts, 1)
            pool.wait_ge(consts, 2)
            g.memset(lora_a[0:HD, :], 0.0).then_inc(consts, 1)
            pool.wait_ge(consts, 3)
            g.memset(raw[:, :, 0:1], 0.0).then_inc(consts, 1)
            pool.wait_ge(consts, 4)
            own(g.memset(eb[0:H, 0:2, :], 0.0))
            ext = eb[0:H, 0:2, :].rearrange("p a b -> p (a b)")
            g.dma_start(ext[:, 127:319], rel_bias[0]).then_inc(bias_in, 16)
            pool.wait_ge(bias_in, 16)
            g.tensor_scalar(ext[:, 0:127], ext[:, 0:127], ext[:, 127:128], None,
                            ALU.add).then_inc(bias_ext, 1)
            pool.wait_ge(bias_ext, 1)
            g.dma_start(bias_d, ext[:, 0:384]).then_inc(bias_dram, 16)
            pool.wait_ge(bias_dram, 16)
            g.dma_start(skew_d, bass.AP(bias_d.tensor, 0, [[0, P], [1, H * 384]])).then_inc(bias_dram, 16)
            pool.wait_ge(bias_dram, 32)
            toeplitz = bass.AP(skew_d.tensor, P - 1, [[H * 384 - 1, P], [384, H], [1, T]])
            g.dma_start(eb[:, :, :], toeplitz).then_inc(bias_in, 16)
            pool.wait_ge(bias_in, 32)
            g.memset(eb[0:HD, :, P + HD:T], NEG).then_inc(bias_ok, 1)
            pool.wait_ge(bias_ok, 1)

            pool.wait_ge(kk_ok, 1)
            g.tensor_tensor(kend, kk, kk, ALU.mult).then_inc(kk_sq, 1)
            pool.wait_ge(ls_ok, 1)
            g.tensor_tensor(tmp, ls, sg, ALU.subtract).then_inc(shifted, 1)
            pool.wait_ge(proj_out, len(RW_GROUPS) + 4)
            qkf = qk.rearrange("p t a w -> p (t a w)")
            g.tensor_tensor(qk_sq, qkf, qkf, ALU.mult).then_inc(qk_sqd, 1)
            pool.wait_ge(exps, 4)
            own(g.memset(xt, 0.0))
            for half in range(2):
                part = xt[HD * half:HD * (half + 1), :, :]
                g.affine_select(out=part, in_=part, compare_op=ALU.not_equal, fill=1.0,
                                base=16 * half, pattern=[[1, NC // 2], [-1, NC]],
                                channel_multiplier=0).then_inc(xt_zero, 1)
                pool.wait_ge(xt_zero, half + 1)
            pool.wait_ge(acol_ok, 2)
            g.dma_start(acol_d, acol.rearrange("p s i -> p (s i)")).then_inc(acol_dram, 16)
            pool.wait_ge(acol_dram, 16)
            av = acol_d.rearrange("(q t) (s i) -> q s t i", t=NC, i=NC)
            for half in range(2):
                for q in range(NQ):
                    p0 = HD * half + NS * q
                    g.dma_start(prob[p0:p0 + NS, :, :], av[q]).then_inc(prob_in, 16)
            pool.wait_ge(inv_ok, 1)
            g.dma_start(inv_d, xt.rearrange("p j t -> p (j t)")).then_inc(inv_dram, 16)
            pool.wait_ge(inv_dram, 16)
            iv = inv_d.rearrange("(f q s) (j t) -> q f j s t", f=2, q=NQ, j=NC // 2)
            for half in range(2):
                for q in range(NQ):
                    p0 = NC * q + NC // 2 * half
                    g.dma_start(dt[p0:p0 + NC // 2, :, :], iv[q, half]).then_inc(dt_in, 16)
            for tt in range(TT):
                if tt:
                    pool.wait_ge(st_ps, 4 * NQ)
                pool.wait_ge(qk_sum, 1)
                for b in range(NP):
                    ins = g.tensor_tensor(
                        mt[:, b, :, :],
                        id64.unsqueeze(1).broadcast_to([P, NQ, HD]),
                        pend[:, b, NQ * tt:NQ * (tt + 1)].unsqueeze(2).broadcast_to([P, NQ, HD]),
                        ALU.mult)
                    ins.then_inc(diag_ok, 1)
            pool.wait_ge(diag_ok, NP * TT)
            pool.wait_ge(y_ps, TT)
            own(g.memset(arena[:, 2 * D:5 * D], 0.0))
            g.dma_start(eb_up[0:E, :], b_up[0]).then_inc(moe_in, 16)
            g.dma_start(eb_dn[0:E, :], b_down[0]).then_inc(moe_in, 16)
            g.dma_start(g2, norm2_g[0:1, :].broadcast_to([P, D])).then_inc(moe_in, 16)
            g.dma_start(wr, w_router[0].rearrange("(k p) e -> p k e", p=P)).then_inc(moe_in, 16)
            g.dma_start(br[0:E, :], b_router[0].rearrange("(e o) -> e o", o=1)).then_inc(moe_in, 16)
            pool.wait_ge(rw_ok, 1)
            own(g.iota(iota_i[:, :], pattern=[[1, CAP]], base=0, channel_multiplier=0))
            own(g.tensor_copy(iota, iota_i[:, :]))
            own(g.memset(ones, 1.0))
            own(g.memset(place, 1000.0))
            own(g.affine_select(out=before, in_=ones, compare_op=ALU.is_gt, fill=0.0, base=0,
                                pattern=[[1, P]], channel_multiplier=-1))
            g.memset(gated, 0.0).then_inc(moe_consts, 1)

        @block.scalar
        def _(act):
            n_own = [0]

            def own(ins):
                n_own[0] += 1
                ins.then_inc(act_chain, 1)
                act.wait_ge(act_chain, n_own[0])

            s = nc.scalar
            srcs = [(norm1_g[0], V_G1), (tshift_mu[0], V_MU), (w0[0], V_W0), (a0[0], V_A0),
                    (k_k[0].rearrange("h k -> (h k)"), V_KK), (k_a[0].rearrange("h k -> (h k)"), V_KA),
                    (r_k[0].rearrange("h k -> (h k)"), V_RK), (ln_x_g[0], V_LG), (ln_x_b[0], V_LB)]
            for src, r0 in srcs:
                n = src.shape[0] // P
                act.dma_start(rows[r0:r0 + n, :], src.rearrange("(r c) -> r c", c=P)).then_inc(rows_in, 16)
            for src, r0 in ((q_norm_g, V_QG), (k_norm_g, V_KG)):
                for half in range(2):
                    act.dma_start(rows[r0:r0 + 1, HD * half:HD * (half + 1)], src).then_inc(rows_in, 16)
            act.dma_start(wup[0:HD, :], w_decay_up[0]).then_inc(lora_in, 16)
            act.dma_start(wup[HD:P, :], w_aaa_up[0]).then_inc(lora_in, 16)
            act.dma_start(wgu, w_gate_up[0]).then_inc(lora_in, 16)
            for tt in range(TT):
                act.wait_ge(x_in[tt], 16)
                own(s.activation(htok[:, tt, :], xs[:, tt, :], ACT.Square, accum_out=stat[:, tt:tt + 1]))
            act.wait_ge(consts, 1)
            s.activation(stat[:, 2:4], stat[:, 0:2], ACT.Sqrt, bias=eps[:, 0:1],
                         scale=1.0 / D).then_inc(rms_root, 1)

            def copy_group(gi):
                act.wait_ge(proj_ps, gi + 1)
                if gi:
                    act.wait_ge(mixed, gi)
                else:
                    act.wait_ge(consts, 4)
                ps = bank[5 + gi % 2][:, :].rearrange("p (b t) -> p b t", b=2)
                s.activation(raw[:, :, 1:T + 1], ps, ACT.Copy).then_inc(proj_out, 1)

            copy_group(0)
            act.wait_ge(mixed, 1)
            s.activation(lora_w[0:HD, :], lora[0:HD, 0, :], ACT.Tanh).then_inc(lora_act, 1)
            s.activation(lora_a[HD:P, :], lora[HD:P, 0, :], ACT.Copy).then_inc(lora_act, 1)
            s.activation(lora_g, lora[:, 1, :], ACT.Sigmoid).then_inc(lora_act, 1)
            copy_group(1)
            act.wait_ge(vec_ok, 1)
            act.wait_ge(lora_ps, 1)
            for b in range(NP):
                ps = bank[b // 2][:, T * (b % 2):T * (b % 2 + 1)]
                ins = s.activation(sg[:, b, :], ps, ACT.Sigmoid, bias=vec[:, V_W0 + b:V_W0 + b + 1])
            ins.then_inc(lora_out, 1)
            act.wait_ge(lora_ps, 2)
            for b in range(NP):
                ps = bank[2 + b // 2][:, T * (b % 2):T * (b % 2 + 1)]
                ins = s.activation(aa[:, b, :], ps, ACT.Sigmoid, bias=vec[:, V_A0 + b:V_A0 + b + 1])
            ins.then_inc(lora_out, 1)
            act.wait_ge(lora_ps, 3)
            for j, bk in enumerate((4, 7)):
                ins = s.activation(gate[:, 2 * j:2 * j + 2, :].rearrange("p b t -> p (b t)"),
                                   bank[bk][:, :], ACT.Copy)
            ins.then_inc(lora_out, 1)
            copy_group(2)
            act.wait_ge(ls_ok, 1)
            lsv = ls.rearrange("p b (c t) -> p (b c) t", t=P)
            s.activation(ar[:, :, 1, :], lsv, ACT.Exp, scale=-EXP_M05).then_inc(exps, 1)
            s.activation(be, ls, ACT.Exp, scale=EXP_M05).then_inc(exps, 1)
            ends = ls.rearrange("p b (c t) -> p b c t", t=NC)[:, :, :, NC - 1]
            s.activation(pend, ends, ACT.Exp, scale=-EXP_M05).then_inc(exps, 1)
            act.wait_ge(ls_ok, 2)
            act.wait_ge(kk_sq, 1)
            s.activation(bend, tm2, ACT.Exp, scale=EXP_M05).then_inc(exps, 1)
            act.wait_ge(shifted, 1)
            s.activation(ar[:, :, 0, :], tmp.rearrange("p b (c t) -> p (b c) t", t=P), ACT.Exp,
                         scale=-EXP_M05).then_inc(exps, 1)
            copy_group(3)
            act.wait_ge(kk_ps, 1)
            for j in range(2):
                ins = s.activation(bonus[:, 2 * j:2 * j + 2, :].rearrange("p b t -> p (b t)"),
                                   bank[j][:, :], ACT.Sqrt)
            ins.then_inc(kk_root, 1)
            for gi in range(4, 7):
                copy_group(gi)

            for j in range(len(AT_GROUPS)):
                n = len(RW_GROUPS) + j
                act.wait_ge(proj_ps, n + 1)
                ps = bank[5 + n % 2][:, :].rearrange("p (t c) -> p t c", t=TT)
                c0 = 256 * (j % 2)
                dst = (qk[:, :, j // 2, c0:c0 + 256] if j < 4 else va[:, :, c0:c0 + 256])
                s.activation(dst, ps, ACT.Copy).then_inc(proj_out, 1)
            act.wait_ge(qk_sum, 1)
            s.activation(stat[:, 40:72], stat[:, 8:40], ACT.Sqrt, bias=eps[:, 0:1],
                         scale=1.0 / HD).then_inc(qk_root, 1)
            for hb in range(2):
                act.wait_ge(sc_max, hb + 1)
                for i in range(4):
                    for half, (c0, c1) in enumerate(((0, T), (T, 3 * P))):
                        k_ = 4 * half + i
                        ins = s.activation(sc[:, i, c0:c1], sc[:, i, c0:c1], ACT.Exp,
                                           bias=stat[:, 80 + k_:81 + k_],
                                           accum_out=stat[:, 88 + k_:89 + k_])
                ins.then_inc(sc_exp, 1)
                for i in range(4):
                    h = 4 * hb + i
                    act.wait_ge(pt_ps, h + 1)
                    if h >= 2:
                        act.wait_ge(at_ps, h - 1)
                    s.activation(pt[:, h % 2, :], bank[4 if h % 2 == 0 else 7][:, 0:3 * P],
                                 ACT.Copy).then_inc(pt_ok, 1)
                act.wait_ge(at_ps, 4 * hb + 4)
                s.activation(at[:, 2 * hb:2 * hb + 2, :].rearrange("p b t -> p (b t)"),
                             bank[5 + hb][:, :], ACT.Copy).then_inc(at_ok, 1)

            for tt in range(TT):
                act.wait_ge(v_ps, tt + 1)
                act.wait_ge(qk_sum, 1)
                s.activation(vtok[:, tt, :], bank[tt][:, :], ACT.Copy).then_inc(v_ok, 1)
            for tt in range(TT):
                act.wait_ge(turn_ps, 3 * tt + 3)
                hv = bank[0][:, :].rearrange("p (h k) -> p h k", h=H)
                s.activation(rr[:, :, 0:HD], hv, ACT.Copy).then_inc(turn_ok, 1)
                act.wait_ge(akv_ps, tt + 1)
                hv = bank[0][:, :].rearrange("p (h k) -> p h k", h=H)
                s.activation(rr[:, :, HD:P], hv, ACT.Copy).then_inc(akv_ok, 1)
                for j in range(2):
                    act.wait_ge(wu_ps, 2 * tt + j + 1)
                    s.activation(wu[:, 4 * j:4 * j + 4, :].rearrange("p h c -> p (h c)"),
                                 bank[1 + j][:, :], ACT.Copy).then_inc(wu_ok, 1)
                act.wait_ge(y_ps, tt + 1)
                s.activation(yy[:, :, P * tt:P * (tt + 1)],
                             bank[0][:, :].rearrange("p (b t) -> p b t", b=NP), ACT.Copy).then_inc(y_ok, 1)
            act.wait_ge(ln_ps, 2)
            for j in range(2):
                ins = s.activation(tmpn[:, 2 * j:2 * j + 2, :].rearrange("p b t -> p (b t)"),
                                   bank[3 + j][:, :], ACT.Sqrt, bias=eps[:, 1:2], scale=1.0 / HD)
            ins.then_inc(ln_root, 1)
            for tt in range(TT):
                act.wait_ge(res_ok, 2 * tt + 2)
                own(s.activation(xn[:, tt, :], xs[:, tt, :], ACT.Square, accum_out=stat[:, tt:tt + 1]))
            s.activation(stat[:, 2:4], stat[:, 0:2], ACT.Sqrt, bias=eps[:, 0:1],
                         scale=1.0 / D).then_inc(n2_root, 1)
            act.wait_ge(top_ok, 1)
            for tt in range(TT):
                ins = s.activation(tope[:, tt, :], top[:, tt, 0:TOP_K], ACT.Exp,
                                   bias=topn[:, tt:tt + 1], accum_out=tops[:, tt:tt + 1])
            ins.then_inc(top_exp, 1)

            def gather_out(i):
                act.wait_ge(xg_ps, i + 1)
                s.activation(xg, bank[6][:, :], ACT.Copy).then_inc(xg_ok, 1)
                act.wait_ge(xgt_ps, i + 1)
                s.activation(xgt.rearrange("p j c -> p (j c)"), bank[6][:, :],
                             ACT.Copy).then_inc(xgt_ok, 1)

            def expert(i, g):
                act.wait_ge(glu_ok, i + 1)
                s.activation(sig, glu, ACT.Sigmoid, scale=ALPHA).then_inc(sig_ok, 1)
                gather_out(g + 1)
                act.wait_ge(actt_ps, i + 1)
                s.activation(actt.rearrange("p j c -> p (j c)"), bank[7][:, :],
                             ACT.Copy).then_inc(actt_ok, 1)
                act.wait_ge(down_ps, i + 1)
                s.activation(ye, bank[7][:, :], ACT.Copy).then_inc(ye_ok, 1)

            gather_out(0)
            with act.Fori(0, E) as e:
                expert(e, e)
            crowd = act.value_load(most_u[0:1, 0:1])
            with act.If(crowd > CAP):
                with act.Fori(1, PASSES) as p_:
                    gather_out(p_ * (E + 1))
                    with act.Fori(0, E) as e:
                        expert(p_ * E + e, p_ * (E + 1) + e)

        @block.tensor
        def _(pe):
            t = nc.tensor
            pe.wait_ge(consts, 1)
            pe.wait_ge(rows_in, 16 * 13)
            t.transpose(bank[0][:, 0:NVEC], rows[0:NVEC, :], ident[0:NVEC, 0:NVEC]).then_inc(rows_ps, 1)
            pe.wait_ge(h_tok, TT)
            for i in range(4):
                for j in range(4):
                    k, tt = 2 * i + j // 2, j % 2
                    ins = t.transpose(bank[1 + i][:, P * j:P * (j + 1)],
                                      htok[:, tt, P * k:P * (k + 1)], ident)
                ins.then_inc(ht_ps, 1)

            def project(n):
                pe.wait_ge(slot_full[slot_of(n)], 16 * (n // PRE_SLOTS + 1))
                if n == 0:
                    pe.wait_ge(ht_ok, 4)
                if n >= 2:
                    pe.wait_ge(proj_out, n - 1)
                w = slot(slot_of(n)).rearrange("p (k n) -> p k n", k=KD)
                ps = bank[5 + n % 2]
                for j in range(2):
                    for k in range(KD):
                        if n < len(RW_GROUPS):
                            l, r = w[:, k, P * j:P * (j + 1)], ht[:, k, :]
                        else:
                            l, r = ht[:, k, P * j:P * (j + 1)], w[:, k, :]
                        ins = t.matmul(ps[:, T * j:T * (j + 1)], l, r, start=(k == 0), stop=(k == KD - 1))
                ins.then_inc(proj_ps, 1)

            def head_sums(banks, src, sem_):
                for j in range(2):
                    ins = t.matmul(bank[banks[j]][:, :], half_ones,
                                   src[:, 2 * j:2 * j + 2, :].rearrange("p b t -> p (b t)"),
                                   start=True, stop=True)
                    ins.then_inc(sem_, 1) if sem_ is not None and j else None

            project(0)
            project(1)
            pe.wait_ge(lora_in, 48)
            pe.wait_ge(consts, 3)
            pe.wait_ge(lora_act, 3)
            pe.wait_ge(vec_ok, 1)
            for w, rhs, banks in ((wup, lora_w, (0, 1)), (wup, lora_a, (2, 3)), (wgu, lora_g, (4, 7))):
                for b in range(NP):
                    ins = t.matmul(bank[banks[b // 2]][:, T * (b % 2):T * (b % 2 + 1)],
                                   w[:, P * b:P * (b + 1)], rhs, start=True, stop=True)
                ins.then_inc(lora_ps, 1)
            project(2)
            project(3)
            pe.wait_ge(kk_sq, 1)
            pe.wait_ge(lora_out, 1)
            head_sums((0, 1), kend, kk_ps)
            for n in range(4, 9):
                project(n)
            pe.wait_ge(alpha_beta, 1)
            pe.wait_ge(kk_root, 1)
            for par in range(2):
                for b in range(NP):
                    for tt in range(TT):
                        h = 2 * b + par
                        s_ = set_of(h, tt) % (NS // 2)
                        for q in range(NQ):
                            ins = t.matmul(bank[par][NC * q:NC * (q + 1), NC * s_:NC * (s_ + 1)],
                                           ar[rows_of(h), TT * b + tt, 0, NC * q:NC * (q + 1)],
                                           be[rows_of(h), b, P * tt + NC * q:P * tt + NC * (q + 1)],
                                           start=True, stop=True, tile_position=(HD * par, NC * q))
                ins.then_inc(acol_ps, 1)
            project(9)
            project(10)
            pe.wait_ge(bonus_in, 1)
            pe.wait_ge(lora_out, 2)
            head_sums((2, 3), tmp, bonus_ps)
            project(11)
            project(12)

            pe.wait_ge(qk_ok, 1)
            pe.wait_ge(acol_ok, 2)
            pe.wait_ge(elem_ok, 1)
            for a_ in range(2):
                for i in range(2):
                    for j in range(4):
                        b, tt = 2 * i + j // 2, j % 2
                        ins = t.transpose(bank[2 * a_ + i][:, P * j:P * (j + 1)],
                                          qk[:, tt, a_, P * b:P * (b + 1)], ident)
                    ins.then_inc(qkt_ps, 1)
            for hb in range(2):
                if hb == 0:
                    pe.wait_ge(qkt_ok, 4)
                else:
                    pe.wait_ge(sc_max, 1)
                for i in range(4):
                    h = 4 * hb + i
                    b = h // 2
                    t.matmul(bank[i][:, 0:T], qt[rows_of(h), b, P:T], kt[rows_of(h), b, :],
                             start=True, stop=True)
                    t.matmul(bank[i][:, T:3 * P], qt[rows_of(h), b, 0:P], kt[rows_of(h), b, 0:P],
                             start=True, stop=True).then_inc(sc_ps, 1)
                pe.wait_ge(probs_ok, hb + 1)
                pe.wait_ge(lora_out, 3)
                pe.wait_ge(proj_out, n_proj)

                def turn_probs(h):
                    if h >= 2:
                        pe.wait_ge(pt_ok, h - 1)
                    for j in range(3):
                        ins = t.transpose(bank[4 if h % 2 == 0 else 7][:, P * j:P * (j + 1)],
                                          sc[:, h % 4, P * j:P * (j + 1)], ident)
                    ins.then_inc(pt_ps, 1)

                def attend(h):
                    pe.wait_ge(pt_ok, h + 1)
                    c0 = T * (h // 2 % 2)
                    ps = bank[5 + hb][rows_of(h), c0:c0 + T]
                    v = va[:, :, HD * h:HD * (h + 1)]
                    t.matmul(ps[:, 0:P], v[:, 0, :], pt[:, h % 2, T:3 * P], start=True, stop=True)
                    t.matmul(ps[:, P:T], v[:, 0, :], pt[:, h % 2, 0:P], start=True, stop=False)
                    t.matmul(ps[:, P:T], v[:, 1, :], pt[:, h % 2, P:T], start=False,
                             stop=True).then_inc(at_ps, 1)

                turn_probs(4 * hb)
                for i in range(4):
                    if i < 3:
                        turn_probs(4 * hb + i + 1)
                    attend(4 * hb + i)

            for tt in range(TT):
                if tt == 0:
                    pe.wait_ge(sc_max, 2)
                    pe.wait_ge(mixed, 7)
                    pe.wait_ge(ends_ok, 1)
                else:
                    pe.wait_ge(y_ok, 1)
                    pe.wait_ge(wu_ok, 2)
                    pe.wait_ge(rm_ok, 3)
                cols_ = slice(P * tt, P * (tt + 1))
                if tt == 0:
                    for u in range(TT):
                        for b in range(NP):
                            ins = t.transpose(bank[u][:, P * b:P * (b + 1)],
                                              mv[:, b, P * u:P * (u + 1)], ident)
                        ins.then_inc(v_ps, 1)
                for bk, src in ((2, bend), (3, kend)):
                    for b in range(NP):
                        ins = t.transpose(bank[bk][:, P * b:P * (b + 1)], src[:, b, cols_], ident)
                    ins.then_inc(turn_ps, 1)
                if tt == 0:
                    pe.wait_ge(v_ok, 1)
                for b in range(NP):
                    ins = t.transpose(bank[0][:, P * b:P * (b + 1)], ar[:, TT * b + tt, 0, :], ident)
                ins.then_inc(turn_ps, 1)
                if tt == 0:
                    pe.wait_ge(rank_ok, 1)
                    pe.wait_ge(pt_ok, 8)
                    pe.wait_ge(at_ok, 2)
                else:
                    pe.wait_ge(st_ok, 4 * NQ)
                for h in range(H):
                    if h >= 4:
                        pe.wait_ge(gm_ok, H * tt + h - 3)
                    b = h // 2
                    r = ar[rows_of(h), TT * b + tt, :, :].rearrange("p g t -> p (g t)")
                    ps = bank[4 + h % 4]
                    t.matmul(ps[:, 0:T], be[rows_of(h), b, cols_], r, start=True, stop=True)
                    t.matmul(ps[:, T:2 * T], ka[rows_of(h), b, cols_], r, start=True,
                             stop=True).then_inc(gm_ps, 1)
                pe.wait_ge(turn_ok, tt + 1)
                for h in range(H):
                    pe.wait_ge(gm_ok, H * tt + h + 1)
                    ins = t.matmul(bank[0][:, HD * h:HD * (h + 1)], gm[:, h, 2, :],
                                   vtok[:, tt, HD * h:HD * (h + 1)], start=True, stop=True)
                ins.then_inc(akv_ps, 1)
                pe.wait_ge(ttb_ok, tt + 1)
                pe.wait_ge(v_ok, TT)
                pe.wait_ge(akv_ok, tt + 1)
                pe.wait_ge(masked_ok, 2 * tt + 2)
                for h in range(H):
                    ins = t.matmul(bank[1 + h // 4][:, P * (h % 4):P * (h % 4 + 1)], ttb[:, h, :],
                                   rr[:, h, :], start=True, stop=True)
                    ins.then_inc(wu_ps, 1) if h % 4 == 3 else None
                pe.wait_ge(wu_ok, 2 * tt + 2)
                for h in range(H):
                    ins = t.matmul(bank[3][rows_of(h), P * (h // 2):P * (h // 2 + 1)],
                                   wu[:, h, 0:HD], gm[:, h, 1, :], start=True, stop=True)
                ins.then_inc(rm_ps, 1)
                for h in range(H):
                    b = h // 2
                    ins = t.matmul(bank[4 + b // 2][rows_of(h), T * (b % 2):T * (b % 2 + 1)],
                                   wu[:, h, 0:HD], bbd[:, h, :, :].rearrange("p q k -> p (q k)"),
                                   start=True, stop=True)
                    ins.then_inc(rm_ps, 1) if h % 4 == 3 else None
                pe.wait_ge(rm_ok, 3 * tt + 3)
                for q in range(NQ):
                    for b in range(NP):
                        n = 4 * NQ * tt + NP * q + b
                        if n >= 2:
                            pe.wait_ge(st_ok, n - 1)
                        first = tt == 0 and q == 0
                        for h in (2 * b, 2 * b + 1):
                            ps = bank[6 + b % 2][rows_of(h), 0:HD]
                            t.matmul(ps, bbd[:, h, q, :], wu[:, h, HD:P], start=True, stop=False)
                            ins = t.matmul(ps, kbd[:, h, q, :], vtok[:, tt, HD * h:HD * (h + 1)],
                                           start=False, stop=first)
                            if not first:
                                ins = t.matmul(ps, mt[rows_of(h), b, q, :], st[rows_of(h), b, q, :],
                                               start=False, stop=True)
                        ins.then_inc(st_ps, 1)
                pe.wait_ge(st_ok, 4 * NQ * tt + 3 * NP)
                for b in range(NP):
                    for h in (2 * b, 2 * b + 1):
                        ps = bank[0][rows_of(h), P * b:P * (b + 1)]
                        t.matmul(ps, wu[:, h, HD:P], gm[:, h, 1, :], start=True, stop=False)
                        t.matmul(ps, vtok[:, tt, HD * h:HD * (h + 1)], gm[:, h, 3, :], start=False,
                                 stop=False)
                        qs = [q for q in range(NQ) if tt or q]
                        for q in qs:
                            ins = t.matmul(ps[:, NC * q:NC * (q + 1)], st[rows_of(h), b, q, :],
                                           rt[rows_of(h), b, NC * q:NC * (q + 1)], start=False,
                                           stop=(q == NQ - 1))
                ins.then_inc(y_ps, 1)
            pe.wait_ge(y_ok, 2)
            pe.wait_ge(wu_ok, 4)
            head_sums((1, 2), yy, ln_ps)
            pe.wait_ge(ln_sq, 1)
            head_sums((3, 4), sqy, ln_ps)
            for k in range(KD):
                n = n_proj + k // 2
                if k % 2 == 0:
                    pe.wait_ge(slot_full[slot_of(n)], 16 * (n // PRE_SLOTS + 1))
                if k == 0:
                    pe.wait_ge(at_ok, 2)
                    pe.wait_ge(st_ok, 8 * NQ)
                    pe.wait_ge(y_ok, 2)
                if k == NP:
                    pe.wait_ge(rw_ok, 1)
                w = slot(slot_of(n)).rearrange("p (k n) -> p k n", k=2)
                mix = at if k < NP else yy
                for tt in range(TT):
                    for j in range(2):
                        ins = t.matmul(bank[(5, 6, 7, 0)[2 * tt + j]][:, :],
                                       mix[:, k % NP, P * tt:P * (tt + 1)],
                                       w[:, k % 2, 512 * j:512 * (j + 1)],
                                       start=(k == 0), stop=(k == KD - 1))
                        ins.then_inc(wo_used, 1) if k == KD - 1 else None
                if k % 2 and k < KD - 1:
                    ins.then_inc(wo_slot, 1)
            pe.wait_ge(xn_ok, TT)
            pe.wait_ge(ln_root, 1)
            for i in range(4):
                for j in range(4):
                    k, tt = 2 * i + j // 2, j % 2
                    ins = t.transpose(bank[1 + i][:, P * j:P * (j + 1)],
                                      xn[:, tt, P * k:P * (k + 1)], ident)
                ins.then_inc(xnt_ps, 1)
            pe.wait_ge(res_ok, 4)
            pe.wait_ge(xnt_ok, 4)
            for k in range(KD):
                ins = t.matmul(bank[5][0:E, 0:T], wr[:, k, :], xnt[:, k, :],
                               start=(k == 0), stop=(k == KD - 1))
            ins.then_inc(lgt_ps, 1)
            for i in range(4):
                ins = t.matmul(bank[i][:, :], ident, xs[:, i // 2, 512 * (i % 2):512 * (i % 2 + 1)],
                               start=True, stop=False)
            pe.wait_ge(lgt_ok, 1)
            for tt in range(TT):
                ins = t.transpose(bank[6][:, E * tt:E * (tt + 1)], lgt[0:E, P * tt:P * (tt + 1)],
                                  ident[0:E, 0:E])
            ins.then_inc(logit_ps, 1)
            pe.wait_ge(member_ok, 1)
            pe.wait_ge(moe_consts, 1)
            t.matmul(bank[7][:, 0:E], before, member[:, 0, :], start=True, stop=True)
            t.matmul(bank[7][:, E:2 * E], ones, member[:, 0, :], start=True, stop=False)
            t.matmul(bank[7][:, E:2 * E], before, member[:, 1, :], start=False, stop=True)
            t.matmul(bank[7][:, 2 * E:3 * E], ones, member[:, 0, :], start=True, stop=False)
            t.matmul(bank[7][:, 2 * E:3 * E], ones, member[:, 1, :], start=False,
                     stop=True).then_inc(place_ps, 1)

            def gather(i):
                pe.wait_ge(pick_ok, i + 1)
                for tt in range(TT):
                    for n in range(2):
                        ins = t.matmul(bank[6][CAP * n:CAP * (n + 1), :], pick[:, tt, :],
                                       xn[:, tt, 512 * n:512 * (n + 1)],
                                       start=(tt == 0), stop=(tt == TT - 1))
                ins.then_inc(xg_ps, 1)

            def gather_turn(i):
                pe.wait_ge(xg_ok, i + 1)
                for j in range(4):
                    ins = t.transpose(bank[6][:, P * j:P * (j + 1)], xg[:, P * j:P * (j + 1)], ident)
                ins.then_inc(xgt_ps, 1)

            def expert(i, g):
                pe.wait_ge(xgt_ok, g + 1)
                for k in range(KD):
                    pe.wait_ge(full[k], 16 * i + 16 * (earlier[k] + 1))
                    w = expert_slot(k)
                    for part in range(2):
                        for n in range(2):
                            c0 = D * part + 512 * n
                            ins = t.matmul(bank[4 + part][CAP * n:CAP * (n + 1), :],
                                           xgt[:, k % 4, CAP * (k // 4):CAP * (k // 4 + 1)],
                                           w[:, c0:c0 + 512], start=(k == 0), stop=False)
                    ins.then_inc(slot_used, 1)
                pe.wait_ge(chosen_ok, i + 1)
                for part in range(2):
                    for n in range(2):
                        c0 = D * part + 512 * n
                        ins = t.matmul(bank[4 + part][CAP * n:CAP * (n + 1), :], chosen,
                                       eb_up[:, c0:c0 + 512], start=False, stop=True)
                ins.then_inc(up_ps, 1)
                gather(g + 1)
                gather_turn(g + 1)
                pe.wait_ge(acts_ok, i + 1)
                for j in range(4):
                    ins = t.transpose(bank[7][:, P * j:P * (j + 1)], acts[:, P * j:P * (j + 1)], ident)
                ins.then_inc(actt_ps, 1)
                pe.wait_ge(gated_ok, i + 1)
                pe.wait_ge(xgt_ok, g + 2)
                for n in range(2):
                    for tt in range(TT):
                        j = TT * n + tt
                        ins = t.transpose(bank[6][:, P * j:P * (j + 1)],
                                          gated[:, tt, 2 * n:2 * n + 2, :].rearrange("p a c -> p (a c)"),
                                          ident)
                ins.then_inc(sct_ps, 1)
                pe.wait_ge(actt_ok, i + 1)
                for k in range(KD):
                    j = KD + k // 2
                    if k % 2 == 0:
                        pe.wait_ge(full[j], 16 * i + 16 * (earlier[j] + 1))
                    w = expert_slot(j).rearrange("p (k n) -> p k n", k=2)
                    for n in range(2):
                        ins = t.matmul(bank[7][CAP * n:CAP * (n + 1), :],
                                       actt[:, k % 4, CAP * (k // 4):CAP * (k // 4 + 1)],
                                       w[:, k % 2, 512 * n:512 * (n + 1)], start=(k == 0), stop=False)
                    ins.then_inc(slot_used, 1) if k % 2 else None
                for n in range(2):
                    ins = t.matmul(bank[7][CAP * n:CAP * (n + 1), :], chosen,
                                   eb_dn[:, 512 * n:512 * (n + 1)], start=False, stop=True)
                ins.then_inc(down_ps, 1)
                pe.wait_ge(ye_ok, i + 1)
                pe.wait_ge(sct_ok, i + 1)
                for tt in range(TT):
                    for n in range(2):
                        ins = t.matmul(bank[2 * tt + n][:, :], sct[:, n, tt, :], ye, start=False,
                                       stop=False)
                ins.then_inc(combined, 1)

            pe.wait_ge(routed, 1)
            gather(0)
            gather_turn(0)
            with pe.Fori(0, E) as e:
                expert(e, e)
            crowd = pe.value_load(most_u[0:1, 0:1])
            with pe.If(crowd > CAP):
                with pe.Fori(1, PASSES) as p_:
                    gather(p_ * (E + 1))
                    gather_turn(p_ * (E + 1))
                    with pe.Fori(0, E) as e:
                        expert(p_ * E + e, p_ * (E + 1) + e)
            for i in range(4):
                ins = t.matmul(bank[i][:, :], nought, xn[:, 0, 0:512], start=False, stop=True)
                ins.then_inc(acc_x, 1)

        @block.vector
        def _(dve):
            n_own = [0]

            def own(ins):
                n_own[0] += 1
                ins.then_inc(vec_chain, 1)
                dve.wait_ge(vec_chain, n_own[0])

            v = nc.vector
            tt_ = v.tensor_tensor

            def cols_of(r0, n, width):
                return vec[:, r0:r0 + n].unsqueeze(2).broadcast_to([P, n, width])

            dve.wait_ge(rows_ps, 1)
            v.tensor_copy(vec[:, 0:NVEC], bank[0][:, 0:NVEC]).then_inc(vec_ok, 1)
            dve.wait_ge(rms_root, 1)
            own(v.reciprocal(stat[:, 4:6], stat[:, 2:4]))
            for tt in range(TT):
                v.tensor_scalar(htok[:, tt, :], xs[:, tt, :], stat[:, 4 + tt:5 + tt], None,
                                ALU.mult).then_inc(h_tok, 1)
            dve.wait_ge(vec_ok, 1)
            for i in range(4):
                dve.wait_ge(ht_ps, i + 1)
                tt_(ht[:, 2 * i:2 * i + 2, :], bank[1 + i][:, :].rearrange("p (k t) -> p k t", k=2),
                    cols_of(V_G1 + 2 * i, 2, T), ALU.mult).then_inc(ht_ok, 1)

            def mix(gi):
                g = RW_GROUPS[gi]
                dve.wait_ge(proj_out, gi + 1)
                own(tt_(dd, raw[:, :, 0:T], raw[:, :, 1:T + 1], ALU.subtract))
                for j in range(2):
                    dst = lora[:, j, :] if g == 6 else (mr, mk, mv)[g // 2][:, 2 * (g % 2) + j, :]
                    ins = v.scalar_tensor_tensor(
                        out=dst, in0=dd[:, j, :], scalar=vec[:, V_MU + 2 * g + j:V_MU + 2 * g + j + 1],
                        in1=raw[:, j, 1:T + 1], op0=ALU.mult, op1=ALU.add)
                ins.then_inc(mixed, 1)

            mix(0)
            mix(1)
            dve.wait_ge(lora_out, 1)
            for b in range(NP):
                ins = v.tensor_tensor_scan(ls[:, b, :], keep, sg[:, b, :], 0.0, ALU.mult, ALU.add)
            ins.then_inc(ls_ok, 1)
            dve.wait_ge(ls_ok, 1)
            lc = ls.rearrange("p b (c t) -> p (b c) t", t=NC)
            tt_(tm2.rearrange("p b (c t) -> p (b c) t", t=NC), lc,
                lc[:, :, NC - 1:NC].broadcast_to([P, NP * T // NC, NC]), ALU.subtract).then_inc(ls_ok, 1)
            mix(2)
            dve.wait_ge(mixed, 3)
            tt_(kk, mk, cols_of(V_KK, NP, T), ALU.mult).then_inc(kk_ok, 1)
            mix(3)
            dve.wait_ge(kk_root, 1)
            own(v.tensor_scalar(bonus, bonus, 1e-12, None, ALU.max))
            own(v.reciprocal(bonus, bonus))
            own(tt_(kk, kk, bonus, ALU.mult))
            dve.wait_ge(lora_out, 2)
            own(v.tensor_scalar(stat[:, 72:76], vec[:, V_KA:V_KA + NP], -1.0, 1.0, ALU.mult, ALU.add))
            for b in range(NP):
                ins = v.tensor_scalar(kend[:, b, :], aa[:, b, :], vec[:, V_KA + b:V_KA + b + 1],
                                      stat[:, 72 + b:73 + b], ALU.mult, ALU.add)
            own(ins)
            own(tt_(mk, mk, kend, ALU.mult))
            own(tt_(aa, aa, kk, ALU.mult))
            dve.wait_ge(exps, 5)
            v.scalar_tensor_tensor(out=ar[:, :, 0, :], in0=kk.rearrange("p b (c t) -> p (b c) t", t=P),
                                   scalar=-1.0, in1=ar[:, :, 0, :], op0=ALU.mult, op1=ALU.mult)
            tt_(ka, mk, be, ALU.mult)
            tt_(be, aa, be, ALU.mult).then_inc(alpha_beta, 1)
            tt_(kend, mk, bend, ALU.mult)
            tt_(bend, aa, bend, ALU.mult).then_inc(ends_ok, 1)
            mix(4)
            dve.wait_ge(mixed, 5)
            tt_(ar[:, :, 1, :], mr.rearrange("p b (c t) -> p (b c) t", t=P), ar[:, :, 1, :],
                ALU.mult).then_inc(rank_ok, 1)
            own(tt_(tmp, mr, mk, ALU.mult))
            tt_(tmp, tmp, cols_of(V_RK, NP, T), ALU.mult).then_inc(bonus_in, 1)
            mix(5)
            mix(6)
            for par in range(2):
                dve.wait_ge(acol_ps, par + 1)
                v.tensor_copy(acol[:, NS // 2 * par:NS // 2 * (par + 1), :].rearrange("p s i -> p (s i)"),
                              bank[par][:, 0:T]).then_inc(acol_ok, 1)
            dve.wait_ge(bonus_ps, 1)
            dve.wait_ge(mixed, 7)
            for j in range(2):
                ins = tt_(bonus[:, 2 * j:2 * j + 2, :].rearrange("p b t -> p (b t)"), bank[2 + j][:, :],
                          mv[:, 2 * j:2 * j + 2, :].rearrange("p b t -> p (b t)"), ALU.mult)
            ins.then_inc(elem_ok, 1)
            dve.wait_ge(qk_sqd, 1)
            v.tensor_reduce(stat[:, 8:40], qk_sq.rearrange("p (g c) -> p g c", c=HD), AX.X,
                            ALU.add).then_inc(qk_sum, 1)
            dve.wait_ge(qk_root, 1)
            own(v.reciprocal(stat[:, 40:72], stat[:, 40:72]))
            qkg = qk.rearrange("p t a (h c) -> p (t a h) c", c=HD)
            tt_(qkg, qkg, stat[:, 40:72].unsqueeze(2).broadcast_to([P, 32, HD]),
                ALU.mult).then_inc(qk_ok, 1)
            for a_ in range(2):
                col = (V_QG, V_KG)[a_]
                for i in range(2):
                    dve.wait_ge(qkt_ps, 2 * a_ + i + 1)
                    dst = (qt, kt)[a_][:, 2 * i:2 * i + 2, :].rearrange("p b t -> p (b t)")
                    v.tensor_scalar(dst, bank[2 * a_ + i][:, :], vec[:, col:col + 1],
                                    (HD ** -0.5, 1.0)[a_], ALU.mult, ALU.mult).then_inc(qkt_ok, 1)

            def biased_scores(hb):
                if hb:
                    dve.wait_ge(pt_ps, 4)
                else:
                    dve.wait_ge(bias_ok, 1)
                for i in range(4):
                    h = 4 * hb + i
                    dve.wait_ge(sc_ps, h + 1)
                    tt_(sc[:, i, 0:T], bank[i][:, 0:T], eb[:, h, :], ALU.add)
                    ins = tt_(sc[:, i, T:3 * P], bank[i][:, T:3 * P], eb[:, h, P:T], ALU.add)
                own(ins)
                v.tensor_reduce(stat[:, 76:80], sc[:, :, 0:T], AX.X, ALU.max)
                own(v.tensor_reduce(stat[:, 96:100], sc[:, :, T:3 * P], AX.X, ALU.max))
                v.tensor_scalar(stat[:, 80:84], stat[:, 76:80], -1.0, None, ALU.mult)
                v.tensor_scalar(stat[:, 84:88], stat[:, 96:100], -1.0, None, ALU.mult).then_inc(sc_max, 1)

            def scaled_probs(hb):
                dve.wait_ge(sc_exp, hb + 1)
                own(v.reciprocal(stat[:, 88:96], stat[:, 88:96]))
                tt_(sc[:, :, 0:T], sc[:, :, 0:T],
                    stat[:, 88:92].unsqueeze(2).broadcast_to([P, 4, T]), ALU.mult)
                tt_(sc[:, :, T:3 * P], sc[:, :, T:3 * P],
                    stat[:, 92:96].unsqueeze(2).broadcast_to([P, 4, P]), ALU.mult).then_inc(probs_ok, 1)

            def substitute(i0, i1):
                for i in range(i0, i1):
                    n = NC - 1 - i
                    if i == 0:
                        dve.wait_ge(prob_in, 16 * 8)
                        dve.wait_ge(xt_zero, 2)
                    u = xtmp[:, :, 0:n]
                    own(tt_(u, xt[:, :, i:i + 1].broadcast_to([P, NC // 2, n]),
                            prob[:, i + 1:NC, i].unsqueeze(1).broadcast_to([P, NC // 2, n]), ALU.mult))
                    ins = tt_(xt[:, :, i + 1:NC], xt[:, :, i + 1:NC], u, ALU.add)
                    if i == NC - 2:
                        ins.then_inc(inv_ok, 1)
                    else:
                        own(ins)

            biased_scores(0)
            substitute(0, 8)
            scaled_probs(0)
            substitute(8, 16)
            biased_scores(1)
            substitute(16, 22)
            scaled_probs(1)
            substitute(22, NC - 1)

            blkc = blk[:, :, 0:1]
            for tt in range(TT):
                for i, dst in enumerate((bbd, kbd)):
                    dve.wait_ge(turn_ps, 3 * tt + 1 + i)
                    if tt == 0 and i == 0:
                        dve.wait_ge(inv_dram, 16)
                    ps = bank[2 + i][:, :].rearrange("p (h k) -> p h k", h=H)
                    for q in range(NQ):
                        ins = v.tensor_scalar(dst[:, :, q, :], ps, blkc[:, q, :], None, ALU.mult)
                    ins.then_inc(masked_ok, 1)
                if tt:
                    dve.wait_ge(y_ps, tt)
                for h in range(H):
                    dve.wait_ge(gm_ps, H * tt + h + 1)
                    tt_(gm[:, h, :, :].rearrange("p (a g) t -> p a (g t)", a=2),
                        bank[4 + h % 4][:, :].rearrange("p (a t) -> p a t", a=2),
                        gmask.rearrange("p g t -> p (g t)").unsqueeze(1).broadcast_to([P, 2, T]),
                        ALU.mult).then_inc(gm_ok, 1)
                if tt == 0:
                    dve.wait_ge(dt_in, 16 * 8)
                dts = dt.rearrange("p (r b t) i -> p r b t i", r=2, t=TT)
                for par in range(2):
                    for q in range(NQ):
                        tv = ttb.rearrange("p (b r) c -> p r b c", r=2)[:, par, :, NC * q:NC * (q + 1)]
                        ins = v.tensor_scalar(tv, dts[:, par, :, tt, :], blkc[:, q, :], None, ALU.mult)
                ins.then_inc(ttb_ok, 1)
                dve.wait_ge(rm_ps, 3 * tt + 1)
                tt_(rt, bank[3][:, :].rearrange("p (b t) -> p b t", b=NP),
                    ar.rearrange("p (b u) g t -> p u b g t", u=TT)[:, tt, :, 1, :], ALU.add).then_inc(rm_ok, 1)
                dve.wait_ge(diag_ok, NP * (tt + 1))
                for j in range(2):
                    dve.wait_ge(rm_ps, 3 * tt + 2 + j)
                    mv_ = mt[:, 2 * j:2 * j + 2, :, :].rearrange("p b q k -> p (b q k)")
                    tt_(mv_, bank[4 + j][:, :], mv_, ALU.add).then_inc(rm_ok, 1)
                if tt:
                    dve.wait_ge(y_ps, tt)
                for q in range(NQ):
                    for b in range(NP):
                        dve.wait_ge(st_ps, 4 * NQ * tt + NP * q + b + 1)
                        v.tensor_copy(st[:, b, q + 1, :], bank[6 + b % 2][:, 0:HD]).then_inc(st_ok, 1)
                if tt == 0:
                    dve.wait_ge(st_ok, 4 * NQ)
                    own(v.tensor_copy(st[:, :, 0, :], st[:, :, NQ, :]))
            dve.wait_ge(ln_ps, 1)
            yf = yy.rearrange("p b t -> p (b t)")
            for j in range(2):
                ins = v.scalar_tensor_tensor(out=yf[:, 512 * j:512 * (j + 1)], in0=bank[1 + j][:, :],
                                             scalar=-1.0 / HD, in1=yf[:, 512 * j:512 * (j + 1)],
                                             op0=ALU.mult, op1=ALU.add)
            own(ins)
            tt_(sqy, yy, yy, ALU.mult).then_inc(ln_sq, 1)
            dve.wait_ge(ln_root, 1)
            own(v.reciprocal(tmpn, tmpn))
            own(tt_(yy, yy, tmpn, ALU.mult))
            for b in range(NP):
                ins = v.tensor_scalar(yy[:, b, :], yy[:, b, :], vec[:, V_LG + b:V_LG + b + 1],
                                      vec[:, V_LB + b:V_LB + b + 1], ALU.mult, ALU.add)
            own(ins)
            own(tt_(yy, yy, bonus, ALU.add))
            tt_(yy, yy, gate, ALU.mult).then_inc(rw_ok, 1)
            for i in range(4):
                dve.wait_ge(wo_used, i + 1)
                xv = xs[:, i // 2, 512 * (i % 2):512 * (i % 2 + 1)]
                tt_(xv, bank[(5, 6, 7, 0)[i]][:, :], xv, ALU.add).then_inc(res_ok, 1)
            dve.wait_ge(n2_root, 1)
            dve.wait_ge(moe_in, 80)
            own(v.reciprocal(stat[:, 4:6], stat[:, 2:4]))
            for tt in range(TT):
                v.scalar_tensor_tensor(out=xn[:, tt, :], in0=xs[:, tt, :], scalar=stat[:, 4 + tt:5 + tt],
                                       in1=g2, op0=ALU.mult, op1=ALU.mult).then_inc(xn_ok, 1)
            for i in range(4):
                dve.wait_ge(xnt_ps, i + 1)
                v.tensor_copy(xnt[:, 2 * i:2 * i + 2, :].rearrange("p k t -> p (k t)"),
                              bank[1 + i][:, :]).then_inc(xnt_ok, 1)
            dve.wait_ge(moe_consts, 1)
            dve.wait_ge(lgt_ps, 1)
            v.tensor_scalar(lgt[0:E, :], bank[5][0:E, 0:T], br[0:E, 0:1], None, ALU.add).then_inc(lgt_ok, 1)
            dve.wait_ge(logit_ps, 1)
            own(v.tensor_copy(logits.rearrange("p t e -> p (t e)"), bank[6][:, 0:TT * E]))
            for tt in range(TT):
                own(v.max(top[:, tt, :], logits[:, tt, :]))
                ins = v.max_index(topi_u[:, tt, :], top[:, tt, :], logits[:, tt, :])
            own(ins)
            v.tensor_scalar(topn, top[:, :, 0], -1.0, None, ALU.mult).then_inc(top_ok, 1)
            own(v.tensor_copy(topi, topi_u[:, :, 0:TOP_K]))
            own(tt_(hot, iota[:, 0:E].unsqueeze(1).broadcast_to([P, TT * TOP_K, E]),
                    topi.rearrange("p t k -> p (t k)").unsqueeze(2).broadcast_to([P, TT * TOP_K, E]),
                    ALU.is_equal))
            v.tensor_reduce(member, hot.rearrange("p (t k) e -> p t e k", t=TT), AX.X,
                            ALU.add).then_inc(member_ok, 1)
            dve.wait_ge(top_exp, 1)
            own(v.reciprocal(tops, tops))
            own(tt_(tope, tope, tops.unsqueeze(2).broadcast_to([P, TT, TOP_K]), ALU.mult))
            own(tt_(hotg, hot,
                    tope.rearrange("p t k -> p (t k)").unsqueeze(2).broadcast_to([P, TT * TOP_K, E]),
                    ALU.mult))
            own(v.tensor_reduce(gates, hotg.rearrange("p (t k) e -> p t e k", t=TT), AX.X, ALU.add))
            dve.wait_ge(place_ps, 1)
            dve.wait_ge(member_ok, 1)
            own(v.scalar_tensor_tensor(out=place[:, :, 0:E], in0=member, scalar=-1000.0,
                                       in1=place[:, :, 0:E], op0=ALU.mult, op1=ALU.add))
            own(tt_(place[:, :, 0:E], bank[7][:, 0:2 * E].rearrange("p (t e) -> p t e", t=TT),
                    place[:, :, 0:E], ALU.add))
            own(v.tensor_reduce(most, bank[7][:, 2 * E:3 * E], AX.X, ALU.max))

            def picks(e):
                for tt in range(TT):
                    ins = v.tensor_scalar(pick[:, tt, :], iota, place[:, tt, bass.ds(e, 1)], None,
                                          ALU.is_equal)
                ins.then_inc(pick_ok, 1)

            def expert(e, i, g):
                v.tensor_scalar(chosen, ones[:, 0:CAP], ident[:, bass.ds(e, 1)], None,
                                ALU.mult).then_inc(chosen_ok, 1)
                for tt in range(TT):
                    ins = v.tensor_scalar(gated[:, tt, 0::3, :],
                                          iota.unsqueeze(1).broadcast_to([P, 2, CAP]),
                                          place[:, tt, bass.ds(e, 1)], gates[:, tt, bass.ds(e, 1)],
                                          ALU.is_equal, ALU.mult)
                ins.then_inc(gated_ok, 1)
                dve.wait_ge(xg_ps, g + 1)
                picks(e + 1)
                dve.wait_ge(up_ps, i + 1)
                v.tensor_scalar(glu, bank[4][:, :], LIMIT, None, ALU.min).then_inc(glu_ok, 1)
                v.tensor_scalar(lin, bank[5][:, :], -LIMIT, LIMIT, ALU.max, ALU.min).then_inc(lin_ok, 1)
                dve.wait_ge(lin_ok, i + 1)
                v.scalar_tensor_tensor(out=lin, in0=lin, scalar=1.0, in1=glu, op0=ALU.add,
                                       op1=ALU.mult).then_inc(gl_ok, 1)
                dve.wait_ge(gl_ok, i + 1)
                dve.wait_ge(sig_ok, i + 1)
                tt_(acts, lin, sig, ALU.mult).then_inc(acts_ok, 1)
                dve.wait_ge(sct_ps, i + 1)
                v.tensor_copy(sct.rearrange("p n t c -> p (n t c)"), bank[6][:, :]).then_inc(sct_ok, 1)
                dve.wait_ge(down_ps, i + 1)

            v.tensor_copy(most_u[:, :], most).then_inc(routed, 1)
            picks(0)
            with dve.Fori(0, E) as e:
                expert(e, e, e)
            crowd = dve.value_load(most_u[0:1, 0:1])
            with dve.If(crowd > CAP):
                with dve.Fori(1, PASSES) as p_:
                    v.tensor_scalar(place, place, -float(CAP), None, ALU.add).then_inc(moved, 1)
                    dve.wait_ge(moved, p_)
                    dve.wait_ge(xg_ps, p_ * (E + 1))
                    picks(0)
                    with dve.Fori(0, E) as e:
                        expert(e, p_ * E + e, p_ * (E + 1) + e)
            for i in range(4):
                dve.wait_ge(acc_x, i + 1)
                v.tensor_copy(xs[:, i // 2, 512 * (i % 2):512 * (i % 2 + 1)],
                              bank[i][:, :]).then_inc(out_ok, 1)


_INS = ["x", "norm1_g", "w_in", "tshift_mu", "q_norm_g", "k_norm_g", "rel_bias", "w0", "w_decay_up",
        "a0", "w_aaa_up", "w_gate_up", "k_k", "k_a", "r_k", "ln_x_g", "ln_x_b", "w_out", "norm2_g",
        "w_router", "b_router", "w_up", "b_up", "w_down", "b_down"]
_OUTS = [((1, T, D), "float32")]


def kernel(**inputs):
    import numpy as _np
    import concourse.bacc as _bacc
    from concourse import mybir as _mybir
    from concourse.bass_utils import run_bass_kernel_spmd as _run

    nc = _bacc.Bacc("TRN2", target_bir_lowering=False, num_devices=1)
    arrays, args = {}, []
    for name in _INS:
        a = _np.ascontiguousarray(inputs[name])
        arrays[f"in_{name}_dram"] = a
        args.append(nc.dram_tensor(f"in_{name}_dram", a.shape, _mybir.dt.from_np(a.dtype), kind="ExternalInput").ap())
    for i, (shape, dtype) in enumerate(_OUTS):
        dt = _mybir.dt.from_np(_np.dtype(dtype))
        args.append(nc.dram_tensor(f"out_{i}_dram", shape, dt, kind="ExternalOutput").ap())
    hybrid_block(nc, *args)
    r = _run(nc, [arrays], core_ids=[0])
    return r.results[0]["out_0_dram"]
```

```python
from contextlib import ExitStack

import concourse.bass as bass
from concourse import mybir

P = 128
F32 = mybir.dt.float32
U32 = mybir.dt.uint32
I32 = mybir.dt.int32
ALU = mybir.AluOpType
ACT = mybir.ActivationFunctionType
AX = mybir.AxisListType

D = 1024
T = 256
TT = T // P
KD = D // P
H = 8
NP = H // 2
HD = 64
W = H * HD
NRW = 14
NC = 32
NQ = P // NC
NS = H * TT
E = 32
CAP = 64
EXP_M05 = 0.6065306597126334
NEG = -3.0e38
CST = 1328
SLOT = 2048
PRE_SLOTS = 7
UNITS = 12
MOE_SLOTS = 16
GROUP = 4

TOP_K = 4
ALPHA, LIMIT = 1.702, 7.0
RW_GROUPS = [6, 2, 3, 0, 1, 4, 5]
AT_GROUPS = [0, 1, 2, 3, 4, 5]


def slot_of(n):
    return n % PRE_SLOTS


def set_of(h, tt):
    return (h % 2) * NS // 2 + (h // 2) * TT + tt


def hybrid_block(nc, x, norm1_g, w_in, tshift_mu, q_norm_g, k_norm_g, rel_bias, w0, w_decay_up,
                 a0, w_aaa_up, w_gate_up, k_k, k_a, r_k, ln_x_g, ln_x_b, w_out, norm2_g,
                 w_router, b_router, w_up, b_up, w_down, b_down, out):
    with ExitStack() as ctx:
        def sb(name, shape, dt=F32):
            return ctx.enter_context(nc.sbuf_tensor(name, shape, dt))

        def sem(name):
            return ctx.enter_context(nc.semaphore(name))

        ring = sb("ring", [P, PRE_SLOTS * SLOT])
        xs = sb("xs", [P, TT, D])
        cst = sb("cst", [P, CST])
        arena_cols = 34850
        arena = sb("arena", [P, arena_cols])
        bank = [ctx.enter_context(nc.psum_tensor(f"bank{i}", [P, 512], F32)) for i in range(8)]

        class Area:
            def __init__(self, t, start, end):
                self.t, self.at, self.end = t, start, end

            def take(self, *dims):
                n = 1
                for d in dims:
                    n *= d
                a = self.t[:, self.at:self.at + n]
                self.at += n
                assert self.at <= self.end, (self.at, self.end)
                if len(dims) > 1:
                    names = "abcde"[:len(dims)]
                    a = a.rearrange(f"p ({' '.join(names)}) -> p {' '.join(names)}",
                                    **{n_: d_ for n_, d_ in zip(names[1:], dims[1:])})
                return a

        c = Area(cst, 0, CST)
        ident = c.take(P)
        half_ones = c.take(P)
        gmask = c.take(2, P)
        blk = c.take(NQ, NC)
        id64 = c.take(HD)
        keep = c.take(T)
        eps = c.take(4)
        nought = c.take(P)
        zeroed = c.at
        vec = c.take(60)
        stat = c.take(100)
        (V_G1, V_MU, V_W0, V_A0, V_KK, V_KA, V_RK, V_LG, V_LB, V_QG, V_KG) = (
            0, 8, 22, 26, 30, 34, 38, 42, 46, 50, 51)
        NVEC = 52

        a = Area(arena, 0, arena_cols)
        ar = a.take(NP * TT, 2, P)
        be = a.take(NP, T)
        ka = a.take(NP, T)
        bend = a.take(NP, T)
        kend = a.take(NP, T)
        gate = a.take(NP, T)
        bonus = a.take(NP, T)
        lora = a.take(2, T)
        pend = a.take(NP, T // NC)
        ht_at = a.at
        wu = a.take(H, P)
        rr = a.take(H, P)
        ht = Area(arena, ht_at, a.at).take(KD, T)
        vtok_at = a.at
        vtok = a.take(TT, W)
        rt = a.take(NP, P)
        st = a.take(NP, NQ + 1, HD)
        mt = a.take(NP, NQ, HD)
        qk_sq = Area(arena, vtok_at, a.at).take(4 * W)
        yy_at = a.at
        yy = a.take(NP, T)
        z = Area(arena, yy_at, a.at)
        lora_w = z.take(T)
        lora_a = z.take(T)
        lora_g = z.take(T)
        rows = z.take(P)
        e0 = a.at
        sg = a.take(NP, T)
        ls = a.take(NP, T)
        tm2 = a.take(NP, T)
        aa = a.take(NP, T)
        kk = a.take(NP, T)
        tmp = a.take(NP, T)
        mr = a.take(NP, T)
        mk = a.take(NP, T)
        mv = a.take(NP, T)
        raw = a.take(2, T + 1)
        dd = a.take(2, T)
        z = Area(arena, e0, e0 + 3 * NP * T)
        prob = z.take(NC, NC)
        xt = z.take(NC // 2, NC)
        xtmp = z.take(NC // 2, NC)
        acol = z.take(NS, NC)
        dt = z.take(NS, NC)
        bbd = Area(arena, e0, e0 + 2048).take(H, NQ, HD)
        z = Area(arena, e0 + 3 * NP * T, a.at)
        gm0 = z.take(H, 4, P)
        ttb = z.take(H, P)
        kbd = z.take(H, NQ, HD)
        tmpn = gm0[:, 4:6, :, :].rearrange("p h g t -> p (h g t)").rearrange("p (b t) -> p b t", b=NP)
        sqy = gm0[:, 6:8, :, :].rearrange("p h g t -> p (h g t)").rearrange("p (b t) -> p b t", b=NP)
        qk_at = a.at
        qk = a.take(TT, 2, W)
        htok = Area(arena, qk_at, a.at).take(TT, D)
        sc = Area(arena, qk_at, a.at).take(4, 3 * P)
        pt = a.take(2, 3 * P)
        qt = a.take(NP, T)
        kt = a.take(NP, T)
        va = a.take(TT, W)
        eb = a.take(H, T)
        at_at = a.at
        at = a.take(NP, T)
        gm1 = Area(arena, qk_at, at_at).take(H, 4, P)
        gm = (gm0, gm1)
        z = Area(arena, at_at, a.at)
        wup = z.take(W)
        wgu = z.take(W)

        z = Area(arena, 0, NP * TT * 2 * P + 4 * NP * T)
        xn = z.take(TT, D)
        eb_up = z.take(2 * D)
        eb_dn = z.take(D)
        g2 = z.take(D)
        moe_at = z.at
        z = Area(arena, yy_at - KD * E - 4, yy_at)
        wr = z.take(KD, E)
        br = z.take(1)
        z = Area(arena, moe_at, yy_at - KD * E - 4)
        xnt = z.take(KD, T)
        z = Area(arena, moe_at, z.end)
        xg = z.take(512)
        xgt = z.take(4, P)
        glu = z.take(512)
        sig = z.take(512)
        z.take(2)
        lin = z.take(512)
        acts = z.take(512)
        actt = z.take(4, P)
        ye = z.take(512)
        sct = z.take(2, TT, P)
        pick = z.take(TT, CAP)
        gated = z.take(TT, 4, CAP)
        chosen = z.take(CAP)
        lgt = z.take(T)
        logits = z.take(TT, E)
        top = z.take(TT, 8)
        topn = z.take(TT)
        tope = z.take(TT, TOP_K)
        tops = z.take(TT)
        topi = z.take(TT, TOP_K)
        hot = z.take(TT * TOP_K, E)
        hotg = z.take(TT * TOP_K, E)
        member = z.take(TT, E)
        gates = z.take(TT, E)
        place = z.take(TT, E + 1)
        counts = z.take(E)
        most = z.take(1)
        iota = z.take(CAP)
        before = z.take(P)
        ones = z.take(P)
        ring_slots = {0: 3, 1: 4, 2: 5, 6: 6, 7: 0, 14: 1, 15: 2}
        slot_at = [(arena, qk_at + 2 * SLOT), (arena, qk_at), (arena, qk_at + SLOT),
                   (arena, qk_at + 3 * SLOT)] + [(arena, e0 + j * SLOT) for j in range(5)]
        for j, r_ in ring_slots.items():
            slot_at.insert(j, (ring, r_ * SLOT))
        assert len(slot_at) == MOE_SLOTS and e0 + 5 * SLOT <= qk_at
        topi_u = sb("topi_u", [P, TT, 8], U32)
        most_u = sb("most_u", [P, 1], U32)
        iota_i = sb("iota_i", [P, CAP], I32)

        bias_d = nc.dram_tensor("bias_scratch", (H, 384), F32, kind="Internal").ap()
        skew_d = nc.dram_tensor("skew_scratch", (P, H * 384), F32, kind="Internal").ap()
        acol_d = nc.dram_tensor("acol_scratch", (P, NS * NC), F32, kind="Internal").ap()
        inv_d = nc.dram_tensor("inv_scratch", (P, NC * NC // 2), F32, kind="Internal").ap()

        x_in = [sem(f"x_in{i}") for i in range(TT)]
        rows_in = sem("rows_in")
        lora_in = sem("lora_in")
        slot_full = [sem(f"slot_full{i}") for i in range(PRE_SLOTS)]
        act_chain = sem("act_chain")
        vec_chain = sem("vec_chain")
        pool_chain = sem("pool_chain")
        consts = sem("consts")
        bias_ext = sem("bias_ext")
        bias_dram = sem("bias_dram")
        bias_in = sem("bias_in")
        bias_ok = sem("bias_ok")
        rms_root = sem("rms_root")
        h_tok = sem("h_tok")
        rows_ps = sem("rows_ps")
        vec_ok = sem("vec_ok")
        ht_ps = sem("ht_ps")
        ht_ok = sem("ht_ok")
        proj_ps = sem("proj_ps")
        proj_out = sem("proj_out")
        mixed = sem("mixed")
        lora_act = sem("lora_act")
        lora_ps = sem("lora_ps")
        lora_out = sem("lora_out")
        kk_ok = sem("kk_ok")
        kk_sq = sem("kk_sq")
        kk_ps = sem("kk_ps")
        kk_root = sem("kk_root")
        ls_ok = sem("ls_ok")
        shifted = sem("shifted")
        exps = sem("exps")
        alpha_beta = sem("alpha_beta")
        rank_ok = sem("rank_ok")
        bonus_in = sem("bonus_in")
        bonus_ps = sem("bonus_ps")
        elem_ok = sem("elem_ok")
        ends_ok = sem("ends_ok")
        acol_ps = sem("acol_ps")
        acol_ok = sem("acol_ok")
        acol_dram = sem("acol_dram")
        prob_in = sem("prob_in")
        xt_zero = sem("xt_zero")
        inv_ok = sem("inv_ok")
        inv_dram = sem("inv_dram")
        dt_in = sem("dt_in")
        qk_sqd = sem("qk_sqd")
        qk_sum = sem("qk_sum")
        qk_root = sem("qk_root")
        qk_ok = sem("qk_ok")
        qkt_ps = sem("qkt_ps")
        qkt_ok = sem("qkt_ok")
        sc_ps = sem("sc_ps")
        sc_max = sem("sc_max")
        sc_exp = sem("sc_exp")
        probs_ok = sem("probs_ok")
        pt_ps = sem("pt_ps")
        pt_ok = sem("pt_ok")
        at_ps = sem("at_ps")
        at_ok = sem("at_ok")
        v_ps = sem("v_ps")
        v_ok = sem("v_ok")
        ends_ps = sem("ends_ps")
        turn_ps = sem("turn_ps")
        turn_ok = sem("turn_ok")
        gm_ps = sem("gm_ps")
        gm_ok = sem("gm_ok")
        ttb_ok = sem("ttb_ok")
        akv_ps = sem("akv_ps")
        akv_ok = sem("akv_ok")
        wu_ps = sem("wu_ps")
        wu_ok = sem("wu_ok")
        rm_ps = sem("rm_ps")
        rm_ok = sem("rm_ok")
        diag_ok = sem("diag_ok")
        st_ps = sem("st_ps")
        st_ok = sem("st_ok")
        st_first = sem("st_first")
        y_ps = sem("y_ps")
        y_ok = sem("y_ok")
        ln_ps = sem("ln_ps")
        ln_sq = sem("ln_sq")
        ln_root = sem("ln_root")
        rw_ok = sem("rw_ok")
        wo_used = sem("wo_used")
        res_ok = sem("res_ok")
        bbd_ok = sem("bbd_ok")
        kbd_ok = sem("kbd_ok")
        wo_slot = sem("wo_slot")
        moe_consts = sem("moe_consts")
        moe_in = sem("moe_in")
        n2_root = sem("n2_root")
        xn_ok = sem("xn_ok")
        xnt_ps = sem("xnt_ps")
        xnt_ok = sem("xnt_ok")
        lgt_ps = sem("lgt_ps")
        lgt_ok = sem("lgt_ok")
        logit_ps = sem("logit_ps")
        top_ok = sem("top_ok")
        top_exp = sem("top_exp")
        member_ok = sem("member_ok")
        place_ps = sem("place_ps")
        routed = sem("routed")
        acc_x = sem("acc_x")
        expert_in = [sem(f"expert_in{i}") for i in range(MOE_SLOTS)]
        slot_used = sem("slot_used")
        pick_ok = sem("pick_ok")
        xg_ps = sem("xg_ps")
        xg_ok = sem("xg_ok")
        xgt_ps = sem("xgt_ps")
        xgt_ok = sem("xgt_ok")
        chosen_ok = sem("chosen_ok")
        gated_ok = sem("gated_ok")
        up_ps = sem("up_ps")
        glu_ok = sem("glu_ok")
        sig_ok = sem("sig_ok")
        acts_ok = sem("acts_ok")
        actt_ps = sem("actt_ps")
        actt_ok = sem("actt_ok")
        sct_ps = sem("sct_ps")
        sct_ok = sem("sct_ok")
        down_ps = sem("down_ps")
        ye_ok = sem("ye_ok")
        combined = sem("combined")
        lin_ok = sem("lin_ok")
        gl_ok = sem("gl_ok")
        moved = sem("moved")
        out_ok = sem("out_ok")
        stored = sem("stored")

        SUB0, SUB1, SUB2 = 16, 23, 27
        n_proj = len(RW_GROUPS) + len(AT_GROUPS)
        n_wout = KD // 2
        w_in_v = w_in[0].rearrange("(k p) n -> p k n", p=P)
        w_out_v = w_out[0].rearrange("(k p) n -> p k n", p=P)
        cols = [3 * W + 256 * g for g in RW_GROUPS] + [256 * g for g in AT_GROUPS]

        def slot(s):
            return ring[:, s * SLOT:(s + 1) * SLOT]

        def expert_slot(j):
            t_, a0_ = slot_at[j]
            return t_[:, a0_:a0_ + SLOT]

        full = [slot_full[ring_slots[j]] if j in ring_slots else expert_in[j] for j in range(MOE_SLOTS)]
        earlier = [sum(slot_of(n) == ring_slots.get(j) for n in range(n_proj + n_wout))
                   for j in range(MOE_SLOTS)]
        PASSES = T // CAP

        def rows_of(h):
            return slice(HD * (h % 2), HD * (h % 2) + HD)

        block = ctx.enter_context(nc.Block())

        @block.sync
        def _(sp):
            for tt in range(TT):
                sp.dma_start(xs[:, tt, :], x[0, tt * P:(tt + 1) * P, :]).then_inc(x_in[tt], 16)
            for src, r0 in ((q_norm_g, V_QG), (k_norm_g, V_KG)):
                for half in range(2):
                    sp.dma_start(rows[r0:r0 + 1, HD * half:HD * (half + 1)], src).then_inc(rows_in, 16)
            for n in range(n_proj + n_wout):
                if n == 2:
                    sp.wait_ge(lora_in, 48)
                    sp.wait_ge(rows_in, 16 * 13)
                if n >= PRE_SLOTS:
                    sp.wait_ge(proj_ps, n - PRE_SLOTS + 1)
                if n < n_proj:
                    dst = slot(slot_of(n)).rearrange("p (k n) -> p k n", k=KD)
                    src = w_in_v[:, :, cols[n]:cols[n] + 256]
                else:
                    j = n - n_proj
                    dst = slot(slot_of(n)).rearrange("p (k n) -> p k n", k=2)
                    src = w_out_v[:, 2 * j:2 * j + 2, :]
                sp.dma_start(dst, src).then_inc(slot_full[slot_of(n)], 16)

            def load_expert(e, r, j):
                s_ = (UNITS * r + j) % MOE_SLOTS
                if j < KD:
                    src = w_up[0, e, P * j:P * (j + 1), :]
                    dst = expert_slot(s_)
                else:
                    r0 = 2 * P * (j - KD)
                    src = w_down[0, e, r0:r0 + 2 * P, :].rearrange("(k p) n -> p k n", p=P)
                    dst = expert_slot(s_).rearrange("p (k n) -> p k n", k=2)
                return sp.dma_start(dst, src).then_inc(full[s_], 16)

            def load_unit(u):
                load_expert(u // UNITS, u // UNITS, u % UNITS)

            for u in (0, 1, 2):
                sp.wait_ge(proj_ps, PRE_SLOTS + ring_slots[u] + 1)
                load_unit(u)
            sp.wait_ge(at_ok, 2)
            sp.wait_ge(ttb_ok, 1)
            load_unit(3)
            sp.wait_ge(y_ps, TT)
            for u in (4, 5):
                load_unit(u)
            sp.wait_ge(wo_slot, 1)
            load_unit(6)
            sp.wait_ge(wo_slot, 2)
            for u in (7, 8):
                load_unit(u)
            sp.wait_ge(rw_ok, TT)
            for u in range(9, 14):
                load_unit(u)
            sp.wait_ge(wo_slot, 3)
            load_unit(14)
            sp.wait_ge(wo_used, 4)
            load_unit(15)

            def stream(e, n, r, j0=0):
                for j in range(j0, UNITS):
                    sp.wait_ge(slot_used, UNITS * GROUP * n + (UNITS * r + j + 1 - MOE_SLOTS))
                    load_expert(e, r, j)

            stream(1, 0, 1, MOE_SLOTS - UNITS)
            for r in (2, 3):
                stream(r, 0, r)
            with sp.Fori(1, E // GROUP) as n:
                for r in range(GROUP):
                    stream(GROUP * n + r, n, r)
            sp.wait_ge(routed, 1)
            crowd = sp.value_load(most_u[0:1, 0:1])
            with sp.If(crowd > CAP):
                with sp.Fori(1, PASSES) as p_:
                    with sp.Fori(0, E // GROUP) as n:
                        for r in range(GROUP):
                            stream(GROUP * n + r, p_ * (E // GROUP) + n, r)
            for i in range(4):
                sp.wait_ge(out_ok, i + 1)
                tt, j = i // 2, i % 2
                sp.dma_start(out[0, P * tt:P * (tt + 1), 512 * j:512 * (j + 1)],
                             xs[:, tt, 512 * j:512 * (j + 1)]).then_inc(stored, 16)
            sp.wait_ge(stored, 64)

        @block.gpsimd
        def _(pool):
            n_own = [0]

            def own(ins):
                n_own[0] += 1
                ins.then_inc(pool_chain, 1)
                pool.wait_ge(pool_chain, n_own[0])

            g = nc.gpsimd
            own(g.memset(cst[:, 0:zeroed], 0.0))
            own(g.memset(half_ones[0:HD, 0:HD], 1.0))
            own(g.memset(half_ones[HD:P, HD:P], 1.0))
            for q in range(NQ):
                own(g.memset(blk[NC * q:NC * (q + 1), q, :], 1.0))
            own(g.memset(keep, 1.0))
            own(g.memset(keep.rearrange("p (c t) -> p c t", t=NC)[:, :, 0:1], 0.0))
            own(g.memset(eps[:, 0:1], 1e-6))
            own(g.memset(eps[:, 1:2], 64e-5))
            own(g.affine_select(out=ident, in_=ident, compare_op=ALU.not_equal, fill=1.0, base=0,
                                pattern=[[-1, P]], channel_multiplier=1))
            for half in range(2):
                part = id64[HD * half:HD * (half + 1), :]
                own(g.affine_select(out=part, in_=part, compare_op=ALU.not_equal, fill=1.0, base=0,
                                    pattern=[[-1, HD]], channel_multiplier=1))
            bf = blk.rearrange("p q t -> p (q t)")
            own(g.affine_select(out=gmask[:, 0, :], in_=bf, compare_op=ALU.is_gt, fill=0.0, base=0,
                                pattern=[[1, P]], channel_multiplier=-1))
            g.affine_select(out=gmask[:, 1, :], in_=bf, compare_op=ALU.is_ge, fill=0.0, base=0,
                            pattern=[[1, P]], channel_multiplier=-1).then_inc(consts, 1)
            pool.wait_ge(consts, 1)
            g.memset(lora_w[HD:P, :], 0.0).then_inc(consts, 1)
            pool.wait_ge(consts, 2)
            g.memset(lora_a[0:HD, :], 0.0).then_inc(consts, 1)
            pool.wait_ge(consts, 3)
            g.memset(raw[:, :, 0:1], 0.0).then_inc(consts, 1)
            pool.wait_ge(consts, 4)
            own(g.memset(eb[0:H, 0:2, :], 0.0))
            ext = eb[0:H, 0:2, :].rearrange("p a b -> p (a b)")
            g.dma_start(ext[:, 127:319], rel_bias[0]).then_inc(bias_in, 16)
            pool.wait_ge(bias_in, 16)
            g.tensor_scalar(ext[:, 0:127], ext[:, 0:127], ext[:, 127:128], None,
                            ALU.add).then_inc(bias_ext, 1)
            pool.wait_ge(bias_ext, 1)
            g.dma_start(bias_d, ext[:, 0:384]).then_inc(bias_dram, 16)
            pool.wait_ge(bias_dram, 16)
            g.dma_start(skew_d, bass.AP(bias_d.tensor, 0, [[0, P], [1, H * 384]])).then_inc(bias_dram, 16)
            pool.wait_ge(bias_dram, 32)
            toeplitz = bass.AP(skew_d.tensor, P - 1, [[H * 384 - 1, P], [384, H], [1, T]])
            g.dma_start(eb[:, :, :], toeplitz).then_inc(bias_in, 16)
            pool.wait_ge(bias_in, 32)
            g.memset(eb[0:HD, :, P + HD:T], NEG).then_inc(bias_ok, 1)
            pool.wait_ge(bias_ok, 1)

            pool.wait_ge(ls_ok, 1)
            g.tensor_tensor(tmp, ls, sg, ALU.subtract).then_inc(shifted, 1)
            pool.wait_ge(exps, 5)
            own(g.memset(xt, 0.0))
            for half in range(2):
                part = xt[HD * half:HD * (half + 1), :, :]
                g.affine_select(out=part, in_=part, compare_op=ALU.not_equal, fill=1.0,
                                base=16 * half, pattern=[[1, NC // 2], [-1, NC]],
                                channel_multiplier=0).then_inc(xt_zero, 1)
                pool.wait_ge(xt_zero, half + 1)
            pool.wait_ge(acol_ok, 2)
            g.dma_start(acol_d, acol.rearrange("p s i -> p (s i)")).then_inc(acol_dram, 16)
            pool.wait_ge(acol_dram, 16)
            av = acol_d.rearrange("(q t) (s i) -> q s t i", t=NC, i=NC)
            for half in range(2):
                for q in range(NQ):
                    p0 = HD * half + NS * q
                    g.dma_start(prob[p0:p0 + NS, :, :], av[q]).then_inc(prob_in, 16)
            sqv = qk_sq.rearrange("p (t a w) -> p t a w", t=TT, a=2)
            for j in range(4):
                pool.wait_ge(proj_out, len(RW_GROUPS) + j + 1)
                qv = qk[:, :, j // 2, 256 * (j % 2):256 * (j % 2 + 1)]
                g.tensor_tensor(sqv[:, :, j // 2, 256 * (j % 2):256 * (j % 2 + 1)], qv, qv,
                                ALU.mult).then_inc(qk_sqd, 1)
            pool.wait_ge(inv_ok, 1)
            g.dma_start(inv_d, xt.rearrange("p j t -> p (j t)")).then_inc(inv_dram, 16)
            pool.wait_ge(inv_dram, 16)
            iv = inv_d.rearrange("(f q s) (j t) -> q f j s t", f=2, q=NQ, j=NC // 2)
            for half in range(2):
                for q in range(NQ):
                    p0 = NC * q + NC // 2 * half
                    g.dma_start(dt[p0:p0 + NC // 2, :, :], iv[q, half]).then_inc(dt_in, 16)
            for tt in range(TT):
                if tt:
                    pool.wait_ge(st_ps, 4 * NQ)
                    pool.wait_ge(rm_ok, 3)
                pool.wait_ge(qk_sum, 4)
                for b in range(NP):
                    ins = g.tensor_tensor(
                        mt[:, b, :, :],
                        id64.unsqueeze(1).broadcast_to([P, NQ, HD]),
                        pend[:, b, NQ * tt:NQ * (tt + 1)].unsqueeze(2).broadcast_to([P, NQ, HD]),
                        ALU.mult)
                    ins.then_inc(diag_ok, 1)
            pool.wait_ge(diag_ok, NP * TT)
            pool.wait_ge(y_ps, TT)
            own(g.memset(arena[:, 2 * D:5 * D], 0.0))
            g.dma_start(eb_up[0:E, :], b_up[0]).then_inc(moe_in, 16)
            g.dma_start(eb_dn[0:E, :], b_down[0]).then_inc(moe_in, 16)
            g.dma_start(g2, norm2_g[0:1, :].broadcast_to([P, D])).then_inc(moe_in, 16)
            g.dma_start(wr, w_router[0].rearrange("(k p) e -> p k e", p=P)).then_inc(moe_in, 16)
            g.dma_start(br[0:E, :], b_router[0].rearrange("(e o) -> e o", o=1)).then_inc(moe_in, 16)
            pool.wait_ge(rw_ok, TT)
            own(g.iota(iota_i[:, :], pattern=[[1, CAP]], base=0, channel_multiplier=0))
            own(g.tensor_copy(iota, iota_i[:, :]))
            own(g.memset(ones, 1.0))
            own(g.memset(place, 1000.0))
            own(g.affine_select(out=before, in_=ones, compare_op=ALU.is_gt, fill=0.0, base=0,
                                pattern=[[1, P]], channel_multiplier=-1))
            g.memset(gated, 0.0).then_inc(moe_consts, 1)

        @block.scalar
        def _(act):
            n_own = [0]

            def own(ins):
                n_own[0] += 1
                ins.then_inc(act_chain, 1)
                act.wait_ge(act_chain, n_own[0])

            s = nc.scalar
            srcs = [(norm1_g[0], V_G1), (tshift_mu[0], V_MU), (w0[0], V_W0), (a0[0], V_A0),
                    (k_k[0].rearrange("h k -> (h k)"), V_KK), (k_a[0].rearrange("h k -> (h k)"), V_KA),
                    (r_k[0].rearrange("h k -> (h k)"), V_RK), (ln_x_g[0], V_LG), (ln_x_b[0], V_LB)]
            for src, r0 in srcs:
                n = src.shape[0] // P
                act.dma_start(rows[r0:r0 + n, :], src.rearrange("(r c) -> r c", c=P)).then_inc(rows_in, 16)
            for tt in range(TT):
                act.wait_ge(x_in[tt], 16)
                own(s.activation(htok[:, tt, :], xs[:, tt, :], ACT.Square, accum_out=stat[:, tt:tt + 1]))
            act.wait_ge(consts, 1)
            s.activation(stat[:, 2:4], stat[:, 0:2], ACT.Sqrt, bias=eps[:, 0:1],
                         scale=1.0 / D).then_inc(rms_root, 1)
            act.dma_start(wup[0:HD, :], w_decay_up[0]).then_inc(lora_in, 16)
            act.dma_start(wup[HD:P, :], w_aaa_up[0]).then_inc(lora_in, 16)
            act.dma_start(wgu, w_gate_up[0]).then_inc(lora_in, 16)

            def copy_group(gi):
                act.wait_ge(proj_ps, gi + 1)
                if gi:
                    act.wait_ge(mixed, gi)
                else:
                    act.wait_ge(consts, 4)
                ps = bank[5 + gi % 2][:, :].rearrange("p (b t) -> p b t", b=2)
                s.activation(raw[:, :, 1:T + 1], ps, ACT.Copy).then_inc(proj_out, 1)

            copy_group(0)
            act.wait_ge(mixed, 1)
            s.activation(lora_w[0:HD, :], lora[0:HD, 0, :], ACT.Tanh).then_inc(lora_act, 1)
            s.activation(lora_a[HD:P, :], lora[HD:P, 0, :], ACT.Copy).then_inc(lora_act, 1)
            s.activation(lora_g, lora[:, 1, :], ACT.Sigmoid).then_inc(lora_act, 1)
            copy_group(1)
            act.wait_ge(vec_ok, 1)
            act.wait_ge(lora_ps, 1)
            for b in range(NP):
                ps = bank[b // 2][:, T * (b % 2):T * (b % 2 + 1)]
                ins = s.activation(sg[:, b, :], ps, ACT.Sigmoid, bias=vec[:, V_W0 + b:V_W0 + b + 1])
            ins.then_inc(lora_out, 1)
            act.wait_ge(lora_ps, 2)
            for b in range(NP):
                ps = bank[2 + b // 2][:, T * (b % 2):T * (b % 2 + 1)]
                ins = s.activation(aa[:, b, :], ps, ACT.Sigmoid, bias=vec[:, V_A0 + b:V_A0 + b + 1])
            ins.then_inc(lora_out, 1)
            act.wait_ge(lora_ps, 3)
            for j, bk in enumerate((4, 7)):
                ins = s.activation(gate[:, 2 * j:2 * j + 2, :].rearrange("p b t -> p (b t)"),
                                   bank[bk][:, :], ACT.Copy)
            ins.then_inc(lora_out, 1)
            copy_group(2)
            act.wait_ge(ls_ok, 1)
            lsv = ls.rearrange("p b (c t) -> p (b c) t", t=P)
            s.activation(ar[:, :, 1, :], lsv, ACT.Exp, scale=-EXP_M05).then_inc(exps, 1)
            s.activation(be, ls, ACT.Exp, scale=EXP_M05).then_inc(exps, 1)
            ends = ls.rearrange("p b (c t) -> p b c t", t=NC)[:, :, :, NC - 1]
            s.activation(pend, ends, ACT.Exp, scale=-EXP_M05).then_inc(exps, 1)
            act.wait_ge(ls_ok, 2)
            s.activation(bend, tm2, ACT.Exp, scale=EXP_M05).then_inc(exps, 1)
            act.wait_ge(shifted, 1)
            s.activation(ar[:, :, 0, :], tmp.rearrange("p b (c t) -> p (b c) t", t=P), ACT.Exp,
                         scale=-EXP_M05).then_inc(exps, 1)
            act.wait_ge(kk_ps, 1)
            for j in range(2):
                ins = s.activation(bonus[:, 2 * j:2 * j + 2, :].rearrange("p b t -> p (b t)"),
                                   bank[j][:, :], ACT.Sqrt)
            ins.then_inc(kk_root, 1)
            for gi in range(3, 7):
                copy_group(gi)
            for par in range(2):
                act.wait_ge(acol_ps, par + 1)
                s.activation(acol[:, NS // 2 * par:NS // 2 * (par + 1), :].rearrange("p s i -> p (s i)"),
                             bank[par][:, 0:T], ACT.Copy).then_inc(acol_ok, 1)

            for j in range(len(AT_GROUPS)):
                if j == len(AT_GROUPS) - 1:
                    act.wait_ge(qk_sum, 4)
                    s.activation(stat[:, 40:72], stat[:, 8:40], ACT.Sqrt, bias=eps[:, 0:1],
                                 scale=1.0 / HD).then_inc(qk_root, 1)
                n = len(RW_GROUPS) + j
                act.wait_ge(proj_ps, n + 1)
                ps = bank[5 + n % 2][:, :].rearrange("p (t c) -> p t c", t=TT)
                c0 = 256 * (j % 2)
                dst = (qk[:, :, j // 2, c0:c0 + 256] if j < 4 else va[:, :, c0:c0 + 256])
                s.activation(dst, ps, ACT.Copy).then_inc(proj_out, 1)
            for a_ in range(2):
                col = (V_QG, V_KG)[a_]
                for i in range(2):
                    act.wait_ge(qkt_ps, 2 * a_ + i + 1)
                    dst = (qt, kt)[a_][:, 2 * i:2 * i + 2, :].rearrange("p b t -> p (b t)")
                    s.activation(dst, bank[2 * a_ + i][:, :], ACT.Copy,
                                 scale=vec[:, col:col + 1]).then_inc(qkt_ok, 1)

            def exp_scores(b):
                act.wait_ge(sc_max, b + 1)
                at0 = 76 + 12 * (b % 2)
                for i in range(2):
                    for half, (c0, c1) in enumerate(((0, T), (T, 3 * P))):
                        k_ = 2 * half + i
                        sv = sc[:, 2 * (b % 2) + i, c0:c1]
                        ins = s.activation(sv, sv, ACT.Exp, bias=stat[:, at0 + 4 + k_:at0 + 5 + k_],
                                           accum_out=stat[:, at0 + 8 + k_:at0 + 9 + k_])
                ins.then_inc(sc_exp, 1)

            exp_scores(0)
            for b in range(NP):
                if b < NP - 1:
                    exp_scores(b + 1)
                for h in (2 * b, 2 * b + 1):
                    act.wait_ge(pt_ps, h + 1)
                    if h >= 2:
                        act.wait_ge(at_ps, h - 1)
                    s.activation(pt[:, h % 2, :], bank[4 if h % 2 == 0 else 7][:, 0:3 * P],
                                 ACT.Copy).then_inc(pt_ok, 1)
                if b == NP - 2:
                    act.wait_ge(qk_sum, 4)
                    for tt in range(TT):
                        act.wait_ge(v_ps, tt + 1)
                        s.activation(vtok[:, tt, :], bank[tt][:, :], ACT.Copy).then_inc(v_ok, 1)
                if b % 2:
                    act.wait_ge(at_ps, 2 * b + 2)
                    s.activation(at[:, b - 1:b + 1, :].rearrange("p b t -> p (b t)"),
                                 bank[5 + b // 2][:, :], ACT.Copy).then_inc(at_ok, 1)

            def token_alpha(tt):
                act.wait_ge(turn_ps, tt + 1)
                if tt:
                    act.wait_ge(wu_ps, 2)
                hv = bank[0][:, :].rearrange("p (h k) -> p h k", h=H)
                s.activation(rr[:, :, 0:HD], hv, ACT.Copy).then_inc(turn_ok, 1)

            def kappa_ends(tt):
                act.wait_ge(ends_ps, 2 * tt + 2)
                if tt:
                    act.wait_ge(st_ps, 4 * NQ)
                ps = bank[3][:, :].rearrange("p (h k) -> p h k", h=H)
                for q in range(NQ):
                    ins = s.activation(kbd[:, :, q, :], ps, ACT.Copy, scale=blk[:, q, 0:1])
                ins.then_inc(kbd_ok, 1)

            def solved(tt):
                act.wait_ge(akv_ps, tt + 1)
                hv = bank[0][:, :].rearrange("p (h k) -> p h k", h=H)
                s.activation(rr[:, :, HD:P], hv, ACT.Copy).then_inc(akv_ok, 1)
                for j in range(2):
                    act.wait_ge(wu_ps, 2 * tt + j + 1)
                    s.activation(wu[:, 4 * j:4 * j + 4, :].rearrange("p h c -> p (h c)"),
                                 bank[1 + j][:, :], ACT.Copy).then_inc(wu_ok, 1)

            def states_out(tt):
                if tt:
                    act.wait_ge(y_ps, tt)
                for q in range(NQ):
                    for b in range(NP):
                        act.wait_ge(st_ps, 4 * NQ * tt + NP * q + b + 1)
                        s.activation(st[:, b, q + 1, :], bank[6 + b % 2][:, 0:HD],
                                     ACT.Copy).then_inc(st_ok, 1)

            def result_out(tt):
                act.wait_ge(y_ps, tt + 1)
                s.activation(yy[:, :, P * tt:P * (tt + 1)],
                             bank[0][:, :].rearrange("p (b t) -> p b t", b=NP), ACT.Copy).then_inc(y_ok, 1)

            def group_root(tt):
                act.wait_ge(ln_ps, 2 * tt + 2)
                s.activation(tmpn[:, :, P * tt:P * (tt + 1)],
                             bank[7][:, :].rearrange("p (b t) -> p b t", b=NP), ACT.Sqrt,
                             bias=eps[:, 1:2], scale=1.0 / HD).then_inc(ln_root, 1)

            token_alpha(0)
            kappa_ends(0)
            solved(0)
            states_out(0)
            act.wait_ge(st_ok, 4 * NQ)
            act.wait_ge(y_ps, 1)
            s.activation(st[:, :, 0, :], st[:, :, NQ, :], ACT.Copy).then_inc(st_first, 1)
            result_out(0)
            token_alpha(1)
            kappa_ends(1)
            group_root(0)
            solved(1)
            states_out(1)
            result_out(1)
            group_root(1)
            for tt in range(TT):
                act.wait_ge(res_ok, 2 * tt + 2)
                own(s.activation(xn[:, tt, :], xs[:, tt, :], ACT.Square, accum_out=stat[:, tt:tt + 1]))
                s.activation(stat[:, 2 + tt:3 + tt], stat[:, tt:tt + 1], ACT.Sqrt, bias=eps[:, 0:1],
                             scale=1.0 / D).then_inc(n2_root, 1)
            for tt in range(TT):
                act.wait_ge(top_ok, tt + 1)
                s.activation(tope[:, tt, :], top[:, tt, 0:TOP_K], ACT.Exp, bias=topn[:, tt:tt + 1],
                             accum_out=tops[:, tt:tt + 1]).then_inc(top_exp, 1)

            def gather_out(i):
                act.wait_ge(xg_ps, i + 1)
                s.activation(xg, bank[6][:, :], ACT.Copy).then_inc(xg_ok, 1)
                act.wait_ge(xgt_ps, i + 1)
                s.activation(xgt.rearrange("p j c -> p (j c)"), bank[6][:, :],
                             ACT.Copy).then_inc(xgt_ok, 1)

            def expert(i, g):
                act.wait_ge(glu_ok, i + 1)
                s.activation(sig, glu, ACT.Sigmoid, scale=ALPHA).then_inc(sig_ok, 1)
                gather_out(g + 1)
                act.wait_ge(actt_ps, i + 1)
                s.activation(actt.rearrange("p j c -> p (j c)"), bank[7][:, :],
                             ACT.Copy).then_inc(actt_ok, 1)
                act.wait_ge(down_ps, i + 1)
                s.activation(ye, bank[7][:, :], ACT.Copy).then_inc(ye_ok, 1)

            gather_out(0)
            with act.Fori(0, E // GROUP) as n:
                for r in range(GROUP):
                    expert(GROUP * n + r, GROUP * n + r)
            crowd = act.value_load(most_u[0:1, 0:1])
            with act.If(crowd > CAP):
                with act.Fori(1, PASSES) as p_:
                    gather_out(p_ * (E + 1))
                    with act.Fori(0, E // GROUP) as n:
                        for r in range(GROUP):
                            expert(p_ * E + GROUP * n + r, p_ * (E + 1) + GROUP * n + r)

        @block.tensor
        def _(pe):
            t = nc.tensor
            pe.wait_ge(consts, 1)
            for tt in range(TT):
                pe.wait_ge(h_tok, tt + 1)
                if tt:
                    pe.wait_ge(rows_in, 16 * 13)
                    t.transpose(bank[0][:, 0:NVEC], rows[0:NVEC, :],
                                ident[0:NVEC, 0:NVEC]).then_inc(rows_ps, 1)
                for k in range(KD):
                    ins = t.transpose(bank[1 + k // 2][:, T * (k % 2) + P * tt:T * (k % 2) + P * (tt + 1)],
                                      htok[:, tt, P * k:P * (k + 1)], ident)
                    ins.then_inc(ht_ps, 1) if tt and k % 2 else None

            def project(n):
                pe.wait_ge(slot_full[slot_of(n)], 16 * (n // PRE_SLOTS + 1))
                if n == 0:
                    pe.wait_ge(ht_ok, 4)
                if n >= 2:
                    pe.wait_ge(proj_out, n - 1)
                w = slot(slot_of(n)).rearrange("p (k n) -> p k n", k=KD)
                ps = bank[5 + n % 2]
                for j in range(2):
                    for k in range(KD):
                        if n < len(RW_GROUPS):
                            l, r = w[:, k, P * j:P * (j + 1)], ht[:, k, :]
                        else:
                            l, r = ht[:, k, P * j:P * (j + 1)], w[:, k, :]
                        ins = t.matmul(ps[:, T * j:T * (j + 1)], l, r, start=(k == 0), stop=(k == KD - 1))
                ins.then_inc(proj_ps, 1)

            def head_sums(banks, src, sem_):
                for j in range(2):
                    ins = t.matmul(bank[banks[j]][:, :], half_ones,
                                   src[:, 2 * j:2 * j + 2, :].rearrange("p b t -> p (b t)"),
                                   start=True, stop=True)
                    ins.then_inc(sem_, 1) if sem_ is not None and j else None

            project(0)
            project(1)
            pe.wait_ge(lora_in, 48)
            pe.wait_ge(consts, 3)
            pe.wait_ge(lora_act, 3)
            pe.wait_ge(vec_ok, 1)
            for w, rhs, banks in ((wup, lora_w, (0, 1)), (wup, lora_a, (2, 3)), (wgu, lora_g, (4, 7))):
                for b in range(NP):
                    ins = t.matmul(bank[banks[b // 2]][:, T * (b % 2):T * (b % 2 + 1)],
                                   w[:, P * b:P * (b + 1)], rhs, start=True, stop=True)
                ins.then_inc(lora_ps, 1)
            project(2)
            project(3)
            pe.wait_ge(kk_sq, 1)
            pe.wait_ge(lora_out, 1)
            head_sums((0, 1), bonus, kk_ps)
            for n in range(4, 7):
                project(n)
            pe.wait_ge(alpha_beta, 1)
            pe.wait_ge(kk_root, 1)
            for par in range(2):
                for b in range(NP):
                    for tt in range(TT):
                        h = 2 * b + par
                        s_ = set_of(h, tt) % (NS // 2)
                        for q in range(NQ):
                            ins = t.matmul(bank[par][NC * q:NC * (q + 1), NC * s_:NC * (s_ + 1)],
                                           ar[rows_of(h), TT * b + tt, 0, NC * q:NC * (q + 1)],
                                           be[rows_of(h), b, P * tt + NC * q:P * tt + NC * (q + 1)],
                                           start=True, stop=True, tile_position=(HD * par, NC * q))
                ins.then_inc(acol_ps, 1)
            project(7)
            project(8)
            pe.wait_ge(bonus_in, 1)
            pe.wait_ge(lora_out, 2)
            head_sums((2, 3), tmp, bonus_ps)
            for n in range(9, n_proj):
                project(n)

            pe.wait_ge(qk_ok, 1)
            pe.wait_ge(acol_ok, 2)
            pe.wait_ge(elem_ok, 1)
            for a_ in range(2):
                for i in range(2):
                    for j in range(4):
                        b, tt = 2 * i + j // 2, j % 2
                        ins = t.transpose(bank[2 * a_ + i][:, P * j:P * (j + 1)],
                                          qk[:, tt, a_, P * b:P * (b + 1)], ident)
                    ins.then_inc(qkt_ps, 1)
            pe.wait_ge(qkt_ok, 4)

            def scores(b):
                if b >= 2:
                    pe.wait_ge(sc_max, b - 1)
                for r_ in range(2):
                    rows_ = rows_of(r_)
                    ps = bank[2 * (b % 2) + r_]
                    t.matmul(ps[:, 0:T], qt[rows_, b, P:T], kt[rows_, b, :], start=True, stop=True)
                    t.matmul(ps[:, T:3 * P], qt[rows_, b, 0:P], kt[rows_, b, 0:P],
                             start=True, stop=True).then_inc(sc_ps, 1)

            def attend(b):
                pe.wait_ge(probs_ok, b + 1)
                for h in (2 * b, 2 * b + 1):
                    if h >= 2:
                        pe.wait_ge(pt_ok, h - 1)
                    for j in range(3):
                        ins = t.transpose(bank[4 if h % 2 == 0 else 7][:, P * j:P * (j + 1)],
                                          sc[:, 2 * (b % 2) + h % 2, P * j:P * (j + 1)], ident)
                    ins.then_inc(pt_ps, 1)
                for h in (2 * b, 2 * b + 1):
                    pe.wait_ge(pt_ok, h + 1)
                    c0 = T * (b % 2)
                    ps = bank[5 + b // 2][rows_of(h), c0:c0 + T]
                    v = va[:, :, HD * h:HD * (h + 1)]
                    t.matmul(ps[:, 0:P], v[:, 0, :], pt[:, h % 2, T:3 * P], start=True, stop=True)
                    t.matmul(ps[:, P:T], v[:, 0, :], pt[:, h % 2, 0:P], start=True, stop=False)
                    t.matmul(ps[:, P:T], v[:, 1, :], pt[:, h % 2, P:T], start=False,
                             stop=True).then_inc(at_ps, 1)

            def turn_v():
                pe.wait_ge(sc_max, NP)
                for u in range(TT):
                    for b in range(NP):
                        ins = t.transpose(bank[u][:, P * b:P * (b + 1)],
                                          mv[:, b, P * u:P * (u + 1)], ident)
                    ins.then_inc(v_ps, 1)

            def turn_ends(tt):
                if tt:
                    pe.wait_ge(wu_ok, 2)
                    pe.wait_ge(rm_ok, 1)
                for bk, src in ((2, bend), (3, kend)):
                    for b in range(NP):
                        ins = t.transpose(bank[bk][:, P * b:P * (b + 1)],
                                          src[:, b, P * tt:P * (tt + 1)], ident)
                    ins.then_inc(ends_ps, 1)

            def turn_alpha(tt):
                if tt:
                    pe.wait_ge(y_ok, 1)
                else:
                    pe.wait_ge(v_ok, 1)
                for b in range(NP):
                    ins = t.transpose(bank[0][:, P * b:P * (b + 1)], ar[:, TT * b + tt, 0, :], ident)
                ins.then_inc(turn_ps, 1)

            def pair_products(tt, par, qs):
                for q in qs:
                    for b in range(NP):
                        rows_ = rows_of(par)
                        r = ar[rows_, TT * b + tt, :, NC * q:NC * (q + 1)]
                        for i, src in enumerate((be, ka)):
                            c0 = P * b + 2 * NC * i
                            ins = t.matmul(bank[4 + par][NC * q:NC * (q + 1), c0:c0 + 2 * NC],
                                           src[rows_, b, P * tt + NC * q:P * tt + NC * (q + 1)], r,
                                           start=True, stop=True, tile_position=(HD * par, NC * q))
                ins.then_inc(gm_ps, 1) if NQ - 1 in qs else None

            def a_k_v(tt):
                pe.wait_ge(turn_ok, tt + 1)
                for par in range(2):
                    pe.wait_ge(gm_ok, 2 * tt + par + 1)
                    for h in range(par, H, 2):
                        ins = t.matmul(bank[0][:, HD * h:HD * (h + 1)], gm[tt][:, h, 2, :],
                                       vtok[:, tt, HD * h:HD * (h + 1)], start=True, stop=True)
                ins.then_inc(akv_ps, 1)

            def solve(tt):
                pe.wait_ge(ttb_ok, tt + 1)
                pe.wait_ge(v_ok, TT)
                pe.wait_ge(akv_ok, tt + 1)
                pe.wait_ge(bbd_ok, tt + 1)
                for h in range(H):
                    ins = t.matmul(bank[1 + h // 4][:, P * (h % 4):P * (h % 4 + 1)], ttb[:, h, :],
                                   rr[:, h, :], start=True, stop=True)
                    ins.then_inc(wu_ps, 1) if h % 4 == 3 else None
                pe.wait_ge(kbd_ok, tt + 1)
                pe.wait_ge(wu_ok, 2 * tt + 2)
                for h in range(H):
                    ins = t.matmul(bank[3][rows_of(h), P * (h // 2):P * (h // 2 + 1)],
                                   wu[:, h, 0:HD], gm[tt][:, h, 1, :], start=True, stop=True)
                ins.then_inc(rm_ps, 1)
                for h in range(H):
                    b = h // 2
                    ins = t.matmul(bank[4 + b // 2][rows_of(h), T * (b % 2):T * (b % 2 + 1)],
                                   wu[:, h, 0:HD], bbd[:, h, :, :].rearrange("p q k -> p (q k)"),
                                   start=True, stop=True)
                    ins.then_inc(rm_ps, 1) if h % 4 == 3 else None
                pe.wait_ge(rm_ok, 3 * tt + 3)
                if tt:
                    pe.wait_ge(st_first, 1)

            def states(tt, q):
                for b in range(NP):
                    n = 4 * NQ * tt + NP * q + b
                    if n >= 2:
                        pe.wait_ge(st_ok, n - 1)
                    first = tt == 0 and q == 0
                    for h in (2 * b, 2 * b + 1):
                        ps = bank[6 + b % 2][rows_of(h), 0:HD]
                        t.matmul(ps, bbd[:, h, q, :], wu[:, h, HD:P], start=True, stop=False)
                        ins = t.matmul(ps, kbd[:, h, q, :], vtok[:, tt, HD * h:HD * (h + 1)],
                                       start=False, stop=first)
                        if not first:
                            ins = t.matmul(ps, mt[rows_of(h), b, q, :], st[rows_of(h), b, q, :],
                                           start=False, stop=True)
                    ins.then_inc(st_ps, 1)

            def read_out(tt):
                pe.wait_ge(st_ok, 4 * NQ * tt + 3 * NP)
                for b in range(NP):
                    for h in (2 * b, 2 * b + 1):
                        ps = bank[0][rows_of(h), P * b:P * (b + 1)]
                        t.matmul(ps, wu[:, h, HD:P], gm[tt][:, h, 1, :], start=True, stop=False)
                        t.matmul(ps, vtok[:, tt, HD * h:HD * (h + 1)], gm[tt][:, h, 3, :], start=False,
                                 stop=False)
                        for q in range(0 if tt else 1, NQ):
                            ins = t.matmul(ps[:, NC * q:NC * (q + 1)], st[rows_of(h), b, q, :],
                                           rt[rows_of(h), b, NC * q:NC * (q + 1)], start=False,
                                           stop=(q == NQ - 1))
                ins.then_inc(y_ps, 1)

            def tile_sums(tt, bk, src):
                t.matmul(bank[bk][:, :], half_ones, src[:, :, P * tt:P * (tt + 1)],
                         start=True, stop=True).then_inc(ln_ps, 1)

            def mix_out(tt, k):
                n = n_proj + k // 2
                pe.wait_ge(slot_full[slot_of(n)], 16 * (n // PRE_SLOTS + 1))
                w = slot(slot_of(n)).rearrange("p (k n) -> p k n", k=2)
                for j in range(2):
                    ins = t.matmul(bank[((1, 2), (3, 4))[tt][j]][:, :],
                                   (at if k < NP else yy)[:, k % NP, P * tt:P * (tt + 1)],
                                   w[:, k % 2, 512 * j:512 * (j + 1)],
                                   start=(k == 0), stop=(k == KD - 1))
                    ins.then_inc(wo_used, 1) if k == KD - 1 else None
                ins.then_inc(wo_slot, 1) if tt and k % 2 and k < KD - 1 else None

            scores(0)
            scores(1)
            pe.wait_ge(lora_out, 3)
            pe.wait_ge(proj_out, n_proj)
            for b in range(NP):
                if b + 2 < NP:
                    scores(b + 2)
                if b == NP - 1:
                    turn_v()
                attend(b)

            pe.wait_ge(ends_ok, 1)
            pe.wait_ge(rank_ok, 1)
            turn_ends(0)
            turn_alpha(0)
            pe.wait_ge(pt_ok, 8)
            pe.wait_ge(at_ok, 2)
            pair_products(0, 0, range(NQ))
            pair_products(0, 1, range(NQ))
            a_k_v(0)
            solve(0)
            for q in range(NQ):
                states(0, q)
                if q == 0:
                    turn_ends(1)
                    pair_products(1, 0, range(2))
                elif q < 3:
                    pair_products(1, q - 1, range(2, NQ)) if q == 1 else pair_products(1, 1, range(NQ))
            read_out(0)
            turn_alpha(1)
            tile_sums(0, 6, yy)
            a_k_v(1)
            pe.wait_ge(ln_sq, 1)
            tile_sums(0, 7, sqy)
            solve(1)
            pe.wait_ge(ln_root, 1)
            for q in range(NQ):
                states(1, q)
                mix_out(0, q)
            read_out(1)
            for k in (0, 1):
                mix_out(1, k)
            pe.wait_ge(y_ok, 2)
            pe.wait_ge(st_ok, 8 * NQ)
            tile_sums(1, 6, yy)
            for k in (2, 3):
                mix_out(1, k)
            pe.wait_ge(ln_sq, 2)
            tile_sums(1, 7, sqy)
            pe.wait_ge(rw_ok, 1)
            for k in range(NP, KD):
                mix_out(0, k)
            pe.wait_ge(rw_ok, 2)
            for k in range(NP, KD):
                mix_out(1, k)
            def logits_of(tt):
                cols_ = slice(P * tt, P * (tt + 1))
                for k in range(KD):
                    if k % 4 == 0:
                        pe.wait_ge(xnt_ok, 2 * tt + k // 4 + 1)
                    ins = t.matmul(bank[7 - 3 * tt][0:E, cols_], wr[:, k, :], xnt[:, k, cols_],
                                   start=(k == 0), stop=(k == KD - 1))
                ins.then_inc(lgt_ps, 1)

            for tt in range(TT):
                pe.wait_ge(xn_ok, tt + 1)
                pe.wait_ge(ln_root, 2)
                for i in range(2):
                    if tt:
                        pe.wait_ge(xnt_ok, i + 1)
                    for j in range(4):
                        k = 4 * i + j
                        ins = t.transpose(bank[5 + i][:, P * j:P * (j + 1)],
                                          xn[:, tt, P * k:P * (k + 1)], ident)
                    ins.then_inc(xnt_ps, 1)
            for tt in range(TT):
                logits_of(tt)
            for tt in range(TT):
                pe.wait_ge(xnt_ok, 4)
                pe.wait_ge(lgt_ok, tt + 1)
                t.transpose(bank[5 + tt][:, 0:E], lgt[0:E, P * tt:P * (tt + 1)],
                            ident[0:E, 0:E]).then_inc(logit_ps, 1)
            pe.wait_ge(res_ok, 4)
            for i in range(4):
                ins = t.matmul(bank[i][:, :], ident, xs[:, i // 2, 512 * (i % 2):512 * (i % 2 + 1)],
                               start=True, stop=False)
            pe.wait_ge(member_ok, 1)
            pe.wait_ge(moe_consts, 1)
            t.matmul(bank[7][:, 0:E], before, member[:, 0, :], start=True, stop=True)
            t.matmul(bank[7][:, E:2 * E], ones, member[:, 0, :], start=True, stop=False)
            t.matmul(bank[7][:, E:2 * E], before, member[:, 1, :], start=False, stop=True)
            t.matmul(bank[7][:, 2 * E:3 * E], ones, member[:, 0, :], start=True, stop=False)
            t.matmul(bank[7][:, 2 * E:3 * E], ones, member[:, 1, :], start=False,
                     stop=True).then_inc(place_ps, 1)

            def gather(i):
                pe.wait_ge(pick_ok, i + 1)
                for tt in range(TT):
                    for n in range(2):
                        ins = t.matmul(bank[6][CAP * n:CAP * (n + 1), :], pick[:, tt, :],
                                       xn[:, tt, 512 * n:512 * (n + 1)],
                                       start=(tt == 0), stop=(tt == TT - 1))
                ins.then_inc(xg_ps, 1)

            def gather_turn(i):
                pe.wait_ge(xg_ok, i + 1)
                for j in range(4):
                    ins = t.transpose(bank[6][:, P * j:P * (j + 1)], xg[:, P * j:P * (j + 1)], ident)
                ins.then_inc(xgt_ps, 1)

            def expert(step, r, i, g):

                def unit(j):
                    u = UNITS * r + j
                    s_ = u % MOE_SLOTS
                    rounds = UNITS * GROUP // MOE_SLOTS
                    pe.wait_ge(full[s_], 16 * rounds * step + 16 * (earlier[s_] + u // MOE_SLOTS + 1))
                    return expert_slot(s_)

                pe.wait_ge(xgt_ok, g + 1)
                for k in range(KD):
                    w = unit(k)
                    for part in range(2):
                        for n in range(2):
                            c0 = D * part + 512 * n
                            ins = t.matmul(bank[4 + part][CAP * n:CAP * (n + 1), :],
                                           xgt[:, k % 4, CAP * (k // 4):CAP * (k // 4 + 1)],
                                           w[:, c0:c0 + 512], start=(k == 0), stop=False)
                    ins.then_inc(slot_used, 1)
                pe.wait_ge(chosen_ok, i + 1)
                for part in range(2):
                    for n in range(2):
                        c0 = D * part + 512 * n
                        ins = t.matmul(bank[4 + part][CAP * n:CAP * (n + 1), :], chosen,
                                       eb_up[:, c0:c0 + 512], start=False, stop=True)
                ins.then_inc(up_ps, 1)
                gather(g + 1)
                gather_turn(g + 1)
                pe.wait_ge(acts_ok, i + 1)
                for j in range(4):
                    ins = t.transpose(bank[7][:, P * j:P * (j + 1)], acts[:, P * j:P * (j + 1)], ident)
                ins.then_inc(actt_ps, 1)
                pe.wait_ge(gated_ok, i + 1)
                pe.wait_ge(xgt_ok, g + 2)
                for n in range(2):
                    for tt in range(TT):
                        j = TT * n + tt
                        ins = t.transpose(bank[6][:, P * j:P * (j + 1)],
                                          gated[:, tt, 2 * n:2 * n + 2, :].rearrange("p a c -> p (a c)"),
                                          ident)
                ins.then_inc(sct_ps, 1)
                pe.wait_ge(actt_ok, i + 1)
                for k in range(KD):
                    if k % 2 == 0:
                        w = unit(KD + k // 2).rearrange("p (k n) -> p k n", k=2)
                    for n in range(2):
                        ins = t.matmul(bank[7][CAP * n:CAP * (n + 1), :],
                                       actt[:, k % 4, CAP * (k // 4):CAP * (k // 4 + 1)],
                                       w[:, k % 2, 512 * n:512 * (n + 1)], start=(k == 0), stop=False)
                    ins.then_inc(slot_used, 1) if k % 2 else None
                for n in range(2):
                    ins = t.matmul(bank[7][CAP * n:CAP * (n + 1), :], chosen,
                                   eb_dn[:, 512 * n:512 * (n + 1)], start=False, stop=True)
                ins.then_inc(down_ps, 1)
                pe.wait_ge(ye_ok, i + 1)
                pe.wait_ge(sct_ok, i + 1)
                for tt in range(TT):
                    for n in range(2):
                        ins = t.matmul(bank[2 * tt + n][:, :], sct[:, n, tt, :], ye, start=False,
                                       stop=False)
                ins.then_inc(combined, 1)

            pe.wait_ge(routed, 1)
            gather(0)
            gather_turn(0)
            with pe.Fori(0, E // GROUP) as n:
                for r in range(GROUP):
                    expert(n, r, GROUP * n + r, GROUP * n + r)
            crowd = pe.value_load(most_u[0:1, 0:1])
            with pe.If(crowd > CAP):
                with pe.Fori(1, PASSES) as p_:
                    gather(p_ * (E + 1))
                    gather_turn(p_ * (E + 1))
                    with pe.Fori(0, E // GROUP) as n:
                        for r in range(GROUP):
                            expert(p_ * (E // GROUP) + n, r, p_ * E + GROUP * n + r,
                                   p_ * (E + 1) + GROUP * n + r)
            for i in range(4):
                ins = t.matmul(bank[i][:, :], nought, xn[:, 0, 0:512], start=False, stop=True)
                ins.then_inc(acc_x, 1)

        @block.vector
        def _(dve):
            n_own = [0]

            def own(ins):
                n_own[0] += 1
                ins.then_inc(vec_chain, 1)
                dve.wait_ge(vec_chain, n_own[0])

            v = nc.vector
            tt_ = v.tensor_tensor

            def cols_of(r0, n, width):
                return vec[:, r0:r0 + n].unsqueeze(2).broadcast_to([P, n, width])

            dve.wait_ge(rms_root, 1)
            own(v.reciprocal(stat[:, 4:6], stat[:, 2:4]))
            for tt in range(TT):
                v.tensor_scalar(htok[:, tt, :], xs[:, tt, :], stat[:, 4 + tt:5 + tt], None,
                                ALU.mult).then_inc(h_tok, 1)
            dve.wait_ge(rows_ps, 1)
            v.tensor_copy(vec[:, 0:NVEC], bank[0][:, 0:NVEC]).then_inc(vec_ok, 1)
            dve.wait_ge(vec_ok, 1)
            for i in range(4):
                dve.wait_ge(ht_ps, i + 1)
                tt_(ht[:, 2 * i:2 * i + 2, :], bank[1 + i][:, :].rearrange("p (k t) -> p k t", k=2),
                    cols_of(V_G1 + 2 * i, 2, T), ALU.mult).then_inc(ht_ok, 1)

            def mix(gi):
                g = RW_GROUPS[gi]
                dve.wait_ge(proj_out, gi + 1)
                own(tt_(dd, raw[:, :, 0:T], raw[:, :, 1:T + 1], ALU.subtract))
                for j in range(2):
                    dst = lora[:, j, :] if g == 6 else (mr, mk, mv)[g // 2][:, 2 * (g % 2) + j, :]
                    ins = v.scalar_tensor_tensor(
                        out=dst, in0=dd[:, j, :], scalar=vec[:, V_MU + 2 * g + j:V_MU + 2 * g + j + 1],
                        in1=raw[:, j, 1:T + 1], op0=ALU.mult, op1=ALU.add)
                ins.then_inc(mixed, 1)

            mix(0)
            mix(1)
            dve.wait_ge(lora_out, 1)
            for b in range(NP):
                ins = v.tensor_tensor_scan(ls[:, b, :], keep, sg[:, b, :], 0.0, ALU.mult, ALU.add)
            ins.then_inc(ls_ok, 1)
            dve.wait_ge(ls_ok, 1)
            lc = ls.rearrange("p b (c t) -> p (b c) t", t=NC)
            tt_(tm2.rearrange("p b (c t) -> p (b c) t", t=NC), lc,
                lc[:, :, NC - 1:NC].broadcast_to([P, NP * T // NC, NC]), ALU.subtract).then_inc(ls_ok, 1)
            mix(2)
            dve.wait_ge(mixed, 3)
            tt_(kk, mk, cols_of(V_KK, NP, T), ALU.mult).then_inc(kk_ok, 1)
            dve.wait_ge(kk_ok, 1)
            tt_(bonus, kk, kk, ALU.mult).then_inc(kk_sq, 1)
            dve.wait_ge(lora_out, 2)
            own(v.tensor_scalar(stat[:, 72:76], vec[:, V_KA:V_KA + NP], -1.0, 1.0, ALU.mult, ALU.add))
            for b in range(NP):
                ins = v.tensor_scalar(kend[:, b, :], aa[:, b, :], vec[:, V_KA + b:V_KA + b + 1],
                                      stat[:, 72 + b:73 + b], ALU.mult, ALU.add)
            own(ins)
            own(tt_(mk, mk, kend, ALU.mult))
            dve.wait_ge(exps, 4)
            tt_(ka, mk, be, ALU.mult)
            own(tt_(kend, mk, bend, ALU.mult))
            dve.wait_ge(kk_root, 1)
            own(v.tensor_scalar(bonus, bonus, 1e-12, None, ALU.max))
            own(v.reciprocal(bonus, bonus))
            own(tt_(kk, kk, bonus, ALU.mult))
            own(tt_(aa, aa, kk, ALU.mult))
            dve.wait_ge(exps, 5)
            v.scalar_tensor_tensor(out=ar[:, :, 0, :], in0=kk.rearrange("p b (c t) -> p (b c) t", t=P),
                                   scalar=-1.0, in1=ar[:, :, 0, :], op0=ALU.mult, op1=ALU.mult)
            tt_(be, aa, be, ALU.mult).then_inc(alpha_beta, 1)
            tt_(bend, aa, bend, ALU.mult).then_inc(ends_ok, 1)
            mix(3)
            mix(4)
            dve.wait_ge(mixed, 5)
            tt_(ar[:, :, 1, :], mr.rearrange("p b (c t) -> p (b c) t", t=P), ar[:, :, 1, :],
                ALU.mult).then_inc(rank_ok, 1)
            own(tt_(tmp, mr, mk, ALU.mult))
            tt_(tmp, tmp, cols_of(V_RK, NP, T), ALU.mult).then_inc(bonus_in, 1)
            mix(5)
            mix(6)

            def substitute(i0, i1):
                for i in range(i0, i1):
                    n = NC - 1 - i
                    if i == 0:
                        dve.wait_ge(prob_in, 16 * 8)
                        dve.wait_ge(xt_zero, 2)
                    u = xtmp[:, :, 0:n]
                    own(tt_(u, xt[:, :, i:i + 1].broadcast_to([P, NC // 2, n]),
                            prob[:, i + 1:NC, i].unsqueeze(1).broadcast_to([P, NC // 2, n]), ALU.mult))
                    ins = tt_(xt[:, :, i + 1:NC], xt[:, :, i + 1:NC], u, ALU.add)
                    if i == NC - 2:
                        ins.then_inc(inv_ok, 1)
                    else:
                        own(ins)

            substitute(0, SUB0)
            dve.wait_ge(bonus_ps, 1)
            dve.wait_ge(mixed, 7)
            for j in range(2):
                ins = tt_(bonus[:, 2 * j:2 * j + 2, :].rearrange("p b t -> p (b t)"), bank[2 + j][:, :],
                          mv[:, 2 * j:2 * j + 2, :].rearrange("p b t -> p (b t)"), ALU.mult)
            ins.then_inc(elem_ok, 1)
            for j in range(4):
                dve.wait_ge(qk_sqd, j + 1)
                v.tensor_reduce(
                    stat[:, 8:40].rearrange("p (t a h) -> p t a h", t=TT, a=2)[
                        :, :, j // 2, 4 * (j % 2):4 * (j % 2) + 4],
                    qk_sq.rearrange("p (t a h c) -> p t a h c", t=TT, a=2, h=H)[
                        :, :, j // 2, 4 * (j % 2):4 * (j % 2) + 4, :],
                    AX.X, ALU.add).then_inc(qk_sum, 1)
            v.tensor_scalar(vec[:, V_QG:V_QG + 1], vec[:, V_QG:V_QG + 1], HD ** -0.5, None, ALU.mult)
            dve.wait_ge(qk_root, 1)
            own(v.reciprocal(stat[:, 40:72], stat[:, 40:72]))
            qkg = qk.rearrange("p t a (h c) -> p (t a h) c", c=HD)
            tt_(qkg, qkg, stat[:, 40:72].unsqueeze(2).broadcast_to([P, 32, HD]),
                ALU.mult).then_inc(qk_ok, 1)
            substitute(SUB0, SUB1)

            def biased_scores(b):
                if b >= 2:
                    dve.wait_ge(pt_ps, 2 * b - 2)
                else:
                    dve.wait_ge(bias_ok, 1)
                c0, at0 = 2 * (b % 2), 76 + 12 * (b % 2)
                for i in range(2):
                    h = 2 * b + i
                    dve.wait_ge(sc_ps, h + 1)
                    tt_(sc[:, c0 + i, 0:T], bank[c0 + i][:, 0:T], eb[:, h, :], ALU.add)
                    ins = tt_(sc[:, c0 + i, T:3 * P], bank[c0 + i][:, T:3 * P], eb[:, h, P:T], ALU.add)
                own(ins)
                v.tensor_reduce(stat[:, at0:at0 + 2], sc[:, c0:c0 + 2, 0:T], AX.X, ALU.max)
                own(v.tensor_reduce(stat[:, at0 + 2:at0 + 4], sc[:, c0:c0 + 2, T:3 * P], AX.X, ALU.max))
                v.tensor_scalar(stat[:, at0 + 4:at0 + 8], stat[:, at0:at0 + 4], -1.0, None,
                                ALU.mult).then_inc(sc_max, 1)

            def scaled_probs(b):
                dve.wait_ge(sc_exp, b + 1)
                c0, at0 = 2 * (b % 2), 76 + 12 * (b % 2)
                sums = stat[:, at0 + 8:at0 + 12]
                own(v.reciprocal(sums, sums))
                tt_(sc[:, c0:c0 + 2, 0:T], sc[:, c0:c0 + 2, 0:T],
                    sums[:, 0:2].unsqueeze(2).broadcast_to([P, 2, T]), ALU.mult)
                tt_(sc[:, c0:c0 + 2, T:3 * P], sc[:, c0:c0 + 2, T:3 * P],
                    sums[:, 2:4].unsqueeze(2).broadcast_to([P, 2, P]), ALU.mult).then_inc(probs_ok, 1)

            biased_scores(0)
            for b in range(NP):
                if b == 0:
                    biased_scores(1)
                scaled_probs(b)
                if b + 2 < NP:
                    biased_scores(b + 2)
                    substitute((SUB1, SUB2)[b], (SUB2, NC - 1)[b])

            blkc = blk[:, :, 0:1]

            def beta_ends(tt):
                dve.wait_ge(ends_ps, 2 * tt + 1)
                if tt:
                    dve.wait_ge(st_ps, 4 * NQ)
                else:
                    dve.wait_ge(inv_dram, 16)
                ps = bank[2][:, :].rearrange("p (h k) -> p h k", h=H)
                for q in range(NQ):
                    ins = v.tensor_scalar(bbd[:, :, q, :], ps, blkc[:, q, :], None, ALU.mult)
                ins.then_inc(bbd_ok, 1)

            def chunk_matrices(tt):
                for par in range(2):
                    dve.wait_ge(gm_ps, 2 * tt + par + 1)
                    for b in range(NP):
                        for i in range(2):
                            c0 = P * b + 2 * NC * i
                            ins = tt_(
                                gm[tt][:, 2 * b + par, 2 * i:2 * i + 2, :].rearrange(
                                    "p g (q t) -> p g q t", t=NC),
                                bank[4 + par][:, c0:c0 + 2 * NC].rearrange(
                                    "p (g t) -> p g t", t=NC).unsqueeze(2).broadcast_to([P, 2, NQ, NC]),
                                gmask.rearrange("p g (q t) -> p g q t", t=NC), ALU.mult)
                    ins.then_inc(gm_ok, 1)

            def inverses(tt):
                if tt:
                    dve.wait_ge(wu_ps, 2)
                else:
                    dve.wait_ge(dt_in, 16 * 8)
                dts = dt.rearrange("p (r b t) i -> p r b t i", r=2, t=TT)
                for par in range(2):
                    for q in range(NQ):
                        tv = ttb.rearrange("p (b r) c -> p r b c", r=2)[:, par, :, NC * q:NC * (q + 1)]
                        ins = v.tensor_scalar(tv, dts[:, par, :, tt, :], blkc[:, q, :], None, ALU.mult)
                ins.then_inc(ttb_ok, 1)

            def transitions(tt):
                dve.wait_ge(rm_ps, 3 * tt + 1)
                if tt:
                    dve.wait_ge(y_ps, 1)
                tt_(rt, bank[3][:, :].rearrange("p (b t) -> p b t", b=NP),
                    ar.rearrange("p (b u) g t -> p u b g t", u=TT)[:, tt, :, 1, :], ALU.add).then_inc(rm_ok, 1)
                dve.wait_ge(diag_ok, NP * (tt + 1))
                for j in range(2):
                    dve.wait_ge(rm_ps, 3 * tt + 2 + j)
                    mv_ = mt[:, 2 * j:2 * j + 2, :, :].rearrange("p b q k -> p (b q k)")
                    tt_(mv_, bank[4 + j][:, :], mv_, ALU.add).then_inc(rm_ok, 1)

            def centred(tt):
                dve.wait_ge(ln_ps, 2 * tt + 1)
                yv = yy[:, :, P * tt:P * (tt + 1)]
                own(v.scalar_tensor_tensor(out=yv, in0=bank[6][:, :].rearrange("p (b t) -> p b t", b=NP),
                                           scalar=-1.0 / HD, in1=yv, op0=ALU.mult, op1=ALU.add))
                tt_(sqy[:, :, P * tt:P * (tt + 1)], yv, yv, ALU.mult).then_inc(ln_sq, 1)

            def gated_result(tt):
                dve.wait_ge(ln_root, tt + 1)
                cols_ = slice(P * tt, P * (tt + 1))
                yv, rv = yy[:, :, cols_], tmpn[:, :, cols_]
                own(v.reciprocal(rv, rv))
                own(tt_(yv, yv, rv, ALU.mult))
                for b in range(NP):
                    ins = v.tensor_scalar(yy[:, b, cols_], yy[:, b, cols_], vec[:, V_LG + b:V_LG + b + 1],
                                          vec[:, V_LB + b:V_LB + b + 1], ALU.mult, ALU.add)
                own(ins)
                own(tt_(yv, yv, bonus[:, :, cols_], ALU.add))
                tt_(yv, yv, gate[:, :, cols_], ALU.mult).then_inc(rw_ok, 1)

            beta_ends(0)
            chunk_matrices(0)
            inverses(0)
            transitions(0)
            chunk_matrices(1)
            inverses(1)
            beta_ends(1)
            centred(0)
            transitions(1)
            gated_result(0)
            centred(1)
            gated_result(1)
            for i in range(4):
                dve.wait_ge(wo_used, i + 1)
                xv = xs[:, i // 2, 512 * (i % 2):512 * (i % 2 + 1)]
                tt_(xv, bank[1 + i][:, :], xv, ALU.add).then_inc(res_ok, 1)
            dve.wait_ge(moe_in, 80)
            for tt in range(TT):
                dve.wait_ge(n2_root, tt + 1)
                own(v.reciprocal(stat[:, 4 + tt:5 + tt], stat[:, 2 + tt:3 + tt]))
                v.scalar_tensor_tensor(out=xn[:, tt, :], in0=xs[:, tt, :], scalar=stat[:, 4 + tt:5 + tt],
                                       in1=g2, op0=ALU.mult, op1=ALU.mult).then_inc(xn_ok, 1)
            dve.wait_ge(moe_consts, 1)
            for tt in range(TT):
                for i in range(2):
                    dve.wait_ge(xnt_ps, 2 * tt + i + 1)
                    v.tensor_copy(xnt[:, 4 * i:4 * i + 4, P * tt:P * (tt + 1)],
                                  bank[5 + i][:, :].rearrange("p (k t) -> p k t", k=4)).then_inc(xnt_ok, 1)
            for tt in range(TT):
                lt = lgt[0:E, P * tt:P * (tt + 1)]
                dve.wait_ge(lgt_ps, tt + 1)
                v.tensor_scalar(lt, bank[7 - 3 * tt][0:E, P * tt:P * (tt + 1)], br[0:E, 0:1], None,
                                ALU.add).then_inc(lgt_ok, 1)
            for tt in range(TT):
                dve.wait_ge(logit_ps, tt + 1)
                own(v.tensor_copy(logits[:, tt, :], bank[5 + tt][:, 0:E]))
                own(v.max(top[:, tt, :], logits[:, tt, :]))
                v.tensor_scalar(topn[:, tt:tt + 1], top[:, tt, 0:1], -1.0, None, ALU.mult).then_inc(top_ok, 1)
                own(v.max_index(topi_u[:, tt, :], top[:, tt, :], logits[:, tt, :]))
            own(v.tensor_copy(topi, topi_u[:, :, 0:TOP_K]))
            own(tt_(hot, iota[:, 0:E].unsqueeze(1).broadcast_to([P, TT * TOP_K, E]),
                    topi.rearrange("p t k -> p (t k)").unsqueeze(2).broadcast_to([P, TT * TOP_K, E]),
                    ALU.is_equal))
            v.tensor_reduce(member, hot.rearrange("p (t k) e -> p t e k", t=TT), AX.X,
                            ALU.add).then_inc(member_ok, 1)
            dve.wait_ge(top_exp, TT)
            own(v.reciprocal(tops, tops))
            own(tt_(tope, tope, tops.unsqueeze(2).broadcast_to([P, TT, TOP_K]), ALU.mult))
            own(tt_(hotg, hot,
                    tope.rearrange("p t k -> p (t k)").unsqueeze(2).broadcast_to([P, TT * TOP_K, E]),
                    ALU.mult))
            own(v.tensor_reduce(gates, hotg.rearrange("p (t k) e -> p t e k", t=TT), AX.X, ALU.add))
            dve.wait_ge(member_ok, 1)
            own(v.scalar_tensor_tensor(out=place[:, :, 0:E], in0=member, scalar=-1000.0,
                                       in1=place[:, :, 0:E], op0=ALU.mult, op1=ALU.add))
            dve.wait_ge(place_ps, 1)
            own(tt_(place[:, :, 0:E], bank[7][:, 0:2 * E].rearrange("p (t e) -> p t e", t=TT),
                    place[:, :, 0:E], ALU.add))
            own(v.tensor_reduce(most, bank[7][:, 2 * E:3 * E], AX.X, ALU.max))

            def picks(e):
                for tt in range(TT):
                    ins = v.tensor_scalar(pick[:, tt, :], iota, place[:, tt, bass.ds(e, 1)], None,
                                          ALU.is_equal)
                ins.then_inc(pick_ok, 1)

            def expert(e, i, g):
                v.tensor_scalar(chosen, ones[:, 0:CAP], ident[:, bass.ds(e, 1)], None,
                                ALU.mult).then_inc(chosen_ok, 1)
                for tt in range(TT):
                    ins = v.tensor_scalar(gated[:, tt, 0::3, :],
                                          iota.unsqueeze(1).broadcast_to([P, 2, CAP]),
                                          place[:, tt, bass.ds(e, 1)], gates[:, tt, bass.ds(e, 1)],
                                          ALU.is_equal, ALU.mult)
                ins.then_inc(gated_ok, 1)
                dve.wait_ge(xg_ps, g + 1)
                picks(e + 1)
                dve.wait_ge(up_ps, i + 1)
                v.tensor_scalar(glu, bank[4][:, :], LIMIT, None, ALU.min).then_inc(glu_ok, 1)
                v.tensor_scalar(lin, bank[5][:, :], -LIMIT, LIMIT, ALU.max, ALU.min).then_inc(lin_ok, 1)
                dve.wait_ge(lin_ok, i + 1)
                v.scalar_tensor_tensor(out=lin, in0=lin, scalar=1.0, in1=glu, op0=ALU.add,
                                       op1=ALU.mult).then_inc(gl_ok, 1)
                dve.wait_ge(gl_ok, i + 1)
                dve.wait_ge(sig_ok, i + 1)
                tt_(acts, lin, sig, ALU.mult).then_inc(acts_ok, 1)
                dve.wait_ge(sct_ps, i + 1)
                v.tensor_copy(sct.rearrange("p n t c -> p (n t c)"), bank[6][:, :]).then_inc(sct_ok, 1)
                dve.wait_ge(down_ps, i + 1)

            v.tensor_copy(most_u[:, :], most).then_inc(routed, 1)
            picks(0)
            with dve.Fori(0, E // GROUP) as n:
                for r in range(GROUP):
                    expert(GROUP * n + r, GROUP * n + r, GROUP * n + r)
            crowd = dve.value_load(most_u[0:1, 0:1])
            with dve.If(crowd > CAP):
                with dve.Fori(1, PASSES) as p_:
                    v.tensor_scalar(place, place, -float(CAP), None, ALU.add).then_inc(moved, 1)
                    dve.wait_ge(moved, p_)
                    dve.wait_ge(xg_ps, p_ * (E + 1))
                    picks(0)
                    with dve.Fori(0, E // GROUP) as n:
                        for r in range(GROUP):
                            expert(GROUP * n + r, p_ * E + GROUP * n + r, p_ * (E + 1) + GROUP * n + r)
            for i in range(4):
                dve.wait_ge(acc_x, i + 1)
                v.tensor_copy(xs[:, i // 2, 512 * (i % 2):512 * (i % 2 + 1)],
                              bank[i][:, :]).then_inc(out_ok, 1)


_INS = ["x", "norm1_g", "w_in", "tshift_mu", "q_norm_g", "k_norm_g", "rel_bias", "w0", "w_decay_up",
        "a0", "w_aaa_up", "w_gate_up", "k_k", "k_a", "r_k", "ln_x_g", "ln_x_b", "w_out", "norm2_g",
        "w_router", "b_router", "w_up", "b_up", "w_down", "b_down"]
_OUTS = [((1, T, D), "float32")]


def kernel(**inputs):
    import numpy as _np
    import concourse.bacc as _bacc
    from concourse import mybir as _mybir
    from concourse.bass_utils import run_bass_kernel_spmd as _run

    nc = _bacc.Bacc("TRN2", target_bir_lowering=False, num_devices=1)
    arrays, args = {}, []
    for name in _INS:
        a = _np.ascontiguousarray(inputs[name])
        arrays[f"in_{name}_dram"] = a
        args.append(nc.dram_tensor(f"in_{name}_dram", a.shape, _mybir.dt.from_np(a.dtype), kind="ExternalInput").ap())
    for i, (shape, dtype) in enumerate(_OUTS):
        dt = _mybir.dt.from_np(_np.dtype(dtype))
        args.append(nc.dram_tensor(f"out_{i}_dram", shape, dt, kind="ExternalOutput").ap())
    hybrid_block(nc, *args)
    r = _run(nc, [arrays], core_ids=[0])
    return r.results[0]["out_0_dram"]
```

```python
from contextlib import ExitStack

import concourse.bass as bass
from concourse import mybir

P = 128
F32 = mybir.dt.float32
BF16 = mybir.dt.bfloat16
U32 = mybir.dt.uint32
I32 = mybir.dt.int32
ALU = mybir.AluOpType
ACT = mybir.ActivationFunctionType
AX = mybir.AxisListType

D = 1024
T = 256
TT = T // P
KD = D // P
H = 8
NP = H // 2
HD = 64
W = H * HD
NRW = 14
NC = 32
NQ = P // NC
NS = H * TT
E = 32
CAP = 64
EXP_M05 = 0.6065306597126334
NEG = -3.0e38
CST = 1328
SLOT = 2048
PRE_SLOTS = 7
UNITS = 12
MOE_SLOTS = 18
GROUP = 3
STEPS = E // GROUP
LEFT = E % GROUP

TOP_K = 4
ALPHA, LIMIT = 1.702, 7.0
RW_GROUPS = [6, 2, 3, 0, 1, 4, 5]
AT_GROUPS = [0, 1, 2, 3, 4, 5]


def slot_of(n):
    return n % PRE_SLOTS


def set_of(h, tt):
    return (h % 2) * NS // 2 + (h // 2) * TT + tt


def hybrid_block(nc, x, norm1_g, w_in, tshift_mu, q_norm_g, k_norm_g, rel_bias, w0, w_decay_up,
                 a0, w_aaa_up, w_gate_up, k_k, k_a, r_k, ln_x_g, ln_x_b, w_out, norm2_g,
                 w_router, b_router, w_up, b_up, w_down, b_down, out):
    with ExitStack() as ctx:
        def sb(name, shape, dt=F32):
            return ctx.enter_context(nc.sbuf_tensor(name, shape, dt))

        def sem(name):
            return ctx.enter_context(nc.semaphore(name))

        ring = sb("ring", [P, PRE_SLOTS * SLOT])
        xs = sb("xs", [P, TT, D])
        cst = sb("cst", [P, CST])
        arena_cols = 34850
        arena = sb("arena", [P, arena_cols])
        bank = [ctx.enter_context(nc.psum_tensor(f"bank{i}", [P, 512], F32)) for i in range(8)]

        class Area:
            def __init__(self, t, start, end):
                self.t, self.at, self.end = t, start, end

            def take(self, *dims):
                n = 1
                for d in dims:
                    n *= d
                a = self.t[:, self.at:self.at + n]
                self.at += n
                assert self.at <= self.end, (self.at, self.end)
                if len(dims) > 1:
                    names = "abcde"[:len(dims)]
                    a = a.rearrange(f"p ({' '.join(names)}) -> p {' '.join(names)}",
                                    **{n_: d_ for n_, d_ in zip(names[1:], dims[1:])})
                return a

        c = Area(cst, 0, CST)
        ident = c.take(P)
        half_ones = c.take(P)
        gmask = c.take(2, P)
        blk = c.take(NQ, NC)
        id64 = c.take(HD)
        keep = c.take(T)
        eps = c.take(4)
        nought = c.take(P)
        zeroed = c.at
        vec = c.take(60)
        stat = c.take(100)
        (V_G1, V_MU, V_W0, V_A0, V_KK, V_KA, V_RK, V_LG, V_LB, V_QG, V_KG) = (
            0, 8, 22, 26, 30, 34, 38, 42, 46, 50, 51)
        NVEC = 52

        a = Area(arena, 0, arena_cols)
        ar = a.take(NP * TT, 2, P)
        be_at = a.at
        be = a.take(NP, T)
        ka = a.take(NP, T)
        bend = a.take(NP, T)
        kend = a.take(NP, T)
        gate = a.take(NP, T)
        bonus = a.take(NP, T)
        lora = a.take(2, T)
        pend = a.take(NP, T // NC)
        ht_at = a.at
        wu = a.take(H, P)
        rr = a.take(H, P)
        ht = Area(arena, ht_at, a.at).take(KD, T)
        vtok_at = a.at
        vtok = a.take(TT, W)
        rt = a.take(NP, P)
        st_at = a.at
        st = a.take(NP, NQ + 1, HD)
        mt = a.take(NP, NQ, HD)
        qk_sq = Area(arena, vtok_at, a.at).take(4 * W)
        yy_at = a.at
        yy = a.take(NP, T)
        z = Area(arena, yy_at, a.at)
        lora_w = z.take(T)
        lora_a = z.take(T)
        lora_g = z.take(T)
        rows = z.take(P)
        e0 = a.at
        sg = a.take(NP, T)
        ls = a.take(NP, T)
        tm2 = a.take(NP, T)
        aa = a.take(NP, T)
        kk = a.take(NP, T)
        tmp = a.take(NP, T)
        mr = a.take(NP, T)
        mk = a.take(NP, T)
        mv = a.take(NP, T)
        raw = a.take(2, T + 1)
        dd = a.take(2, T)
        z = Area(arena, e0, e0 + 3 * NP * T)
        prob = z.take(NC, NC)
        xt = z.take(NC // 2, NC)
        xtmp = z.take(NC // 2, NC)
        acol = z.take(NS, NC)
        dt = z.take(NS, NC)
        bbd = Area(arena, e0, e0 + 2048).take(H, NQ, HD)
        z = Area(arena, e0 + 3 * NP * T, a.at)
        gm0_at = z.at
        gm0 = z.take(H, 3, P)
        z.take(H, P)
        ttb = z.take(H, P)
        kbd = z.take(H, NQ, HD)
        z = Area(arena, gm0_at, a.at)
        kt = (z.take(NP, T), z.take(NP, T))
        tmpn = z.take(NP, T)
        sqy = z.take(NP, T)
        qk_at = a.at
        qk = a.take(TT, 2, W)
        htok = Area(arena, qk_at, a.at).take(TT, D)
        sc = Area(arena, qk_at, a.at).take(4, 3 * P)
        pt = a.take(2, 3 * P)
        qt = a.take(NP, T)
        va = a.take(TT, W)
        eb = a.take(H, T)
        at_at = a.at
        at = a.take(NP, T)
        gm1 = Area(arena, qk_at, at_at).take(H, 3, P)
        gm = (gm0, gm1)
        z = Area(arena, at_at, a.at)
        wup = z.take(W)
        wgu = z.take(W)

        xn_at = e0 + SLOT // 2
        xn = Area(arena, xn_at, a.at).take(TT, D)
        out_s = xn
        eb_dn = Area(arena, gm0_at + 4096, a.at).take(D)
        eb_up = Area(arena, gm0_at + 5120, a.at).take(2 * D)
        moe_at = be_at + 4 * NP * T
        z = Area(arena, yy_at - KD * E - 4, yy_at)
        wr = z.take(KD, E)
        br = z.take(1)
        z = Area(arena, moe_at, yy_at - KD * E - 4)
        xnt = z.take(KD, T)
        z = Area(arena, moe_at, z.end)
        xg = z.take(512)
        xgt = z.take(4, P)
        glu = z.take(512)
        sig = z.take(512)
        z.take(2)
        lin = z.take(512)
        acts = z.take(512)
        actt = z.take(4, P)
        ye = z.take(512)
        sct = z.take(2, TT, P)
        pick = z.take(TT, CAP)
        gated = z.take(TT, 4, CAP)
        chosen = z.take(CAP)
        lgt = z.take(T)
        logits = z.take(TT, E)
        top = z.take(TT, 8)
        topn = z.take(TT)
        tope = z.take(TT, TOP_K)
        tops = z.take(TT)
        topi = z.take(TT, TOP_K)
        hot = z.take(TT * TOP_K, E)
        hotg = z.take(TT * TOP_K, E)
        member = z.take(TT, E)
        gates = z.take(TT, E)
        place = z.take(TT, E + 1)
        counts = z.take(E)
        most = z.take(1)
        iota = z.take(CAP)
        ones = z.take(CAP)
        g2 = z.take(D)
        assert z.at - D >= st_at
        ring_slots = {0: 3, 1: 4, 2: 5, 10: 6, 11: 0, 14: 1, 15: 2}
        slot_at = [(arena, at_) for at_ in (
            qk_at + 2 * SLOT,
            be_at, be_at + SLOT,
            gm0_at,
            0,
            qk_at, qk_at + SLOT,
            qk_at + 3 * SLOT,
            gm0_at + SLOT)]
        for j, r_ in ring_slots.items():
            slot_at.insert(j, (ring, r_ * SLOT))
        assert yy_at + NP * T == e0
        slot_at += [(arena, yy_at), (xs[:, :, :].rearrange("p t d -> p (t d)"), 0)]
        assert len(slot_at) == MOE_SLOTS and UNITS * GROUP % MOE_SLOTS == 0
        topi_u = sb("topi_u", [P, TT, 8], U32)
        before = sb("before", [P, P], BF16)
        ones16 = sb("ones16", [P, P], BF16)
        member16 = sb("member16", [P, TT, E], BF16)
        nought16 = sb("nought16", [P, 512], BF16)
        most_u = sb("most_u", [P, 1], U32)
        iota_i = sb("iota_i", [P, CAP], I32)

        bias_d = nc.dram_tensor("bias_scratch", (H, 384), F32, kind="Internal").ap()
        skew_d = nc.dram_tensor("skew_scratch", (P, H * 384), F32, kind="Internal").ap()
        acol_d = nc.dram_tensor("acol_scratch", (P, NS * NC), F32, kind="Internal").ap()
        inv_d = nc.dram_tensor("inv_scratch", (P, NC * NC // 2), F32, kind="Internal").ap()

        x_in = [sem(f"x_in{i}") for i in range(TT)]
        rows_in = sem("rows_in")
        lora_in = sem("lora_in")
        slot_full = [sem(f"slot_full{i}") for i in range(PRE_SLOTS)]
        act_chain = sem("act_chain")
        vec_chain = sem("vec_chain")
        pool_chain = sem("pool_chain")
        consts = sem("consts")
        bias_ext = sem("bias_ext")
        bias_dram = sem("bias_dram")
        bias_in = sem("bias_in")
        bias_ok = sem("bias_ok")
        rms_root = sem("rms_root")
        h_tok = sem("h_tok")
        rows_ps = sem("rows_ps")
        vec_ok = sem("vec_ok")
        ht_ps = sem("ht_ps")
        ht_ok = sem("ht_ok")
        proj_ps = sem("proj_ps")
        proj_out = sem("proj_out")
        mixed = sem("mixed")
        lora_act = sem("lora_act")
        lora_ps = sem("lora_ps")
        lora_out = sem("lora_out")
        kk_ok = sem("kk_ok")
        kk_sq = sem("kk_sq")
        kk_ps = sem("kk_ps")
        kk_root = sem("kk_root")
        ls_ok = sem("ls_ok")
        shifted = sem("shifted")
        exps = sem("exps")
        alpha_beta = sem("alpha_beta")
        rank_ok = sem("rank_ok")
        bonus_in = sem("bonus_in")
        bonus_ps = sem("bonus_ps")
        elem_ok = sem("elem_ok")
        ends_ok = sem("ends_ok")
        acol_ps = sem("acol_ps")
        acol_ok = sem("acol_ok")
        acol_dram = sem("acol_dram")
        prob_in = sem("prob_in")
        xt_zero = sem("xt_zero")
        inv_ok = sem("inv_ok")
        inv_dram = sem("inv_dram")
        kt_zero = sem("kt_zero")
        dt_in = sem("dt_in")
        qk_sqd = sem("qk_sqd")
        qk_sum = sem("qk_sum")
        qk_root = sem("qk_root")
        qk_ok = sem("qk_ok")
        qkt_ps = sem("qkt_ps")
        qkt_ok = sem("qkt_ok")
        sc_ps = sem("sc_ps")
        sc_max = sem("sc_max")
        sc_exp = sem("sc_exp")
        probs_ok = sem("probs_ok")
        pt_ps = sem("pt_ps")
        pt_ok = sem("pt_ok")
        at_ps = sem("at_ps")
        at_ok = sem("at_ok")
        v_ps = sem("v_ps")
        v_ok = sem("v_ok")
        ends_ps = sem("ends_ps")
        turn_ps = sem("turn_ps")
        turn_ok = sem("turn_ok")
        gm_ps = sem("gm_ps")
        gm_ok = sem("gm_ok")
        ttb_ok = sem("ttb_ok")
        akv_ps = sem("akv_ps")
        akv_ok = sem("akv_ok")
        wu_ps = sem("wu_ps")
        wu_ok = sem("wu_ok")
        rm_ps = sem("rm_ps")
        rm_ok = sem("rm_ok")
        diag_ok = sem("diag_ok")
        st_ps = sem("st_ps")
        st_ok = sem("st_ok")
        st_first = sem("st_first")
        y_ps = sem("y_ps")
        y_ok = sem("y_ok")
        ln_ps = sem("ln_ps")
        ln_sq = sem("ln_sq")
        ln_root = sem("ln_root")
        rw_ok = sem("rw_ok")
        wo_used = sem("wo_used")
        res_ok = sem("res_ok")
        bbd_ok = sem("bbd_ok")
        kbd_ok = sem("kbd_ok")
        wo_slot = sem("wo_slot")
        moe_consts = sem("moe_consts")
        moe_in = sem("moe_in")
        n2_root = sem("n2_root")
        xn_ok = sem("xn_ok")
        xnt_ps = sem("xnt_ps")
        xnt_ok = sem("xnt_ok")
        lgt_ps = sem("lgt_ps")
        lgt_ok = sem("lgt_ok")
        logit_ps = sem("logit_ps")
        top_ok = sem("top_ok")
        top_exp = sem("top_exp")
        member_ok = sem("member_ok")
        place_ps = sem("place_ps")
        routed = sem("routed")
        acc_x = sem("acc_x")
        acc_open = sem("acc_open")
        expert_in = [sem(f"expert_in{i}") for i in range(MOE_SLOTS)]
        slot_used = sem("slot_used")
        pick_ok = sem("pick_ok")
        xg_ps = sem("xg_ps")
        xg_ok = sem("xg_ok")
        xgt_ps = sem("xgt_ps")
        xgt_ok = sem("xgt_ok")
        chosen_ok = sem("chosen_ok")
        gated_ok = sem("gated_ok")
        glu_ok = sem("glu_ok")
        sig_ok = sem("sig_ok")
        acts_ok = sem("acts_ok")
        actt_ps = sem("actt_ps")
        actt_ok = sem("actt_ok")
        sct_ps = sem("sct_ps")
        sct_ok = sem("sct_ok")
        ye_ok = sem("ye_ok")
        lin_ok = sem("lin_ok")
        gl_ok = sem("gl_ok")
        moved = sem("moved")
        out_ok = sem("out_ok")
        out_ok_act = sem("out_ok_act")
        stored = sem("stored")

        SUB0, SUB1, SUB2 = 22, 31, 31
        n_proj = len(RW_GROUPS) + len(AT_GROUPS)
        n_wout = KD // 2
        w_in_v = w_in[0].rearrange("(k p) n -> p k n", p=P)
        w_out_v = w_out[0].rearrange("(k p) n -> p k n", p=P)
        cols = [3 * W + 256 * g for g in RW_GROUPS] + [256 * g for g in AT_GROUPS]

        ROWS = [(norm1_g[0], V_G1), (tshift_mu[0], V_MU), (w0[0], V_W0), (a0[0], V_A0),
                (k_k[0].rearrange("h k -> (h k)"), V_KK), (k_a[0].rearrange("h k -> (h k)"), V_KA),
                (r_k[0].rearrange("h k -> (h k)"), V_RK), (ln_x_g[0], V_LG), (ln_x_b[0], V_LB)]
        WARM = 8
        ACT_ROWS = 3

        def slot(s):
            return ring[:, s * SLOT:(s + 1) * SLOT]

        def expert_slot(j):
            t_, a0_ = slot_at[j]
            return t_[:, a0_:a0_ + SLOT]

        full = [slot_full[ring_slots[j]] if j in ring_slots else expert_in[j]
                for j in range(MOE_SLOTS)]
        earlier = [sum(slot_of(n) == ring_slots.get(j) for n in range(n_proj + n_wout))
                   for j in range(MOE_SLOTS)]
        ROUNDS = UNITS * GROUP // MOE_SLOTS
        pass_loads = [len(range(j, UNITS * E, MOE_SLOTS)) for j in range(MOE_SLOTS)]
        PASSES = T // CAP

        def rows_of(h):
            return slice(HD * (h % 2), HD * (h % 2) + HD)

        block = ctx.enter_context(nc.Block())

        @block.sync
        def _(sp):
            for tt in range(TT):
                sp.dma_start(xs[:, tt, :], x[0, tt * P:(tt + 1) * P, :]).then_inc(x_in[tt], 16)
            for n in range(n_proj + n_wout):
                if n == 1:
                    for src, r0 in ROWS[ACT_ROWS:]:
                        rows_n = src.shape[0] // P
                        sp.dma_start(rows[r0:r0 + rows_n, :],
                                     src.rearrange("(r c) -> r c", c=P)).then_inc(rows_in, 16)
                    for src, r0 in ((q_norm_g, V_QG), (k_norm_g, V_KG)):
                        for half in range(2):
                            sp.dma_start(rows[r0:r0 + 1, HD * half:HD * (half + 1)],
                                         src).then_inc(rows_in, 16)
                if n == 2:
                    sp.wait_ge(lora_in, 48)
                    sp.wait_ge(rows_in, 16 * 13)
                if n >= PRE_SLOTS:
                    sp.wait_ge(proj_ps, n - PRE_SLOTS + 1)
                if n < n_proj:
                    dst = slot(slot_of(n)).rearrange("p (k n) -> p k n", k=KD)
                    src = w_in_v[:, :, cols[n]:cols[n] + 256]
                else:
                    j = n - n_proj
                    dst = slot(slot_of(n)).rearrange("p (k n) -> p k n", k=2)
                    src = w_out_v[:, 2 * j:2 * j + 2, :]
                sp.dma_start(dst, src).then_inc(slot_full[slot_of(n)], 16)

            def load_expert(e, j, s_):
                if j < KD:
                    src = w_up[0, e, P * j:P * (j + 1), :]
                    dst = expert_slot(s_)
                else:
                    r0 = 2 * P * (j - KD)
                    src = w_down[0, e, r0:r0 + 2 * P, :].rearrange("(k p) n -> p k n", p=P)
                    dst = expert_slot(s_).rearrange("p (k n) -> p k n", k=2)
                return sp.dma_start(dst, src).then_inc(full[s_], 16)

            def load_unit(u):
                load_expert(u // UNITS, u % UNITS, u % MOE_SLOTS)

            for u in (0, 1, 2):
                sp.wait_ge(proj_ps, PRE_SLOTS + ring_slots[u] + 1)
                load_unit(u)
            sp.wait_ge(at_ok, 2)
            sp.wait_ge(ttb_ok, 1)
            load_unit(3)
            sp.wait_ge(gm_ps, 2 * TT)
            sp.wait_ge(ends_ps, 2 * TT)
            for u in (4, 5):
                load_unit(u)
            sp.wait_ge(y_ps, 1)
            load_unit(6)
            sp.wait_ge(rm_ok, 4)
            sp.wait_ge(turn_ps, TT)
            load_unit(7)
            sp.wait_ge(y_ps, TT)
            for u in (8, 9):
                load_unit(u)
            sp.wait_ge(wo_slot, 1)
            load_unit(10)
            sp.wait_ge(wo_slot, 2)
            for u in (11, 12):
                load_unit(u)
            sp.wait_ge(rw_ok, TT)
            load_unit(13)
            sp.wait_ge(wo_slot, 3)
            load_unit(14)
            sp.wait_ge(wo_used, 4)
            load_unit(15)
            load_unit(16)
            sp.wait_ge(acc_open, 4)
            load_unit(17)

            def stream(first_e, r, base):
                for j in range(UNITS):
                    u = UNITS * r + j
                    sp.wait_ge(slot_used, UNITS * first_e + base + (u + 1 - MOE_SLOTS))
                    load_expert(first_e + r, j, u % MOE_SLOTS)

            def later_steps(base):
                with sp.Fori(1, STEPS) as n:
                    for r in range(GROUP):
                        stream(GROUP * n, r, base)
                for r in range(LEFT):
                    stream(GROUP * STEPS, r, base)

            for u in range(MOE_SLOTS, UNITS * GROUP):
                sp.wait_ge(slot_used, u + 1 - MOE_SLOTS)
                load_unit(u)
            later_steps(0)
            sp.wait_ge(routed, 1)
            crowd = sp.value_load(most_u[0:1, 0:1])
            with sp.If(crowd > CAP):
                with sp.Fori(1, PASSES) as p_:
                    base = p_ * (UNITS * E)
                    for u in range(UNITS * GROUP):
                        sp.wait_ge(slot_used, base + max(u + 1 - MOE_SLOTS, 0))
                        load_unit(u)
                    later_steps(base)
            for i in range(4):
                tt, j = i // 2, i % 2
                sp.wait_ge((out_ok, out_ok_act)[j], tt + 1)
                sp.dma_start(out[0, P * tt:P * (tt + 1), 512 * j:512 * (j + 1)],
                             out_s[:, tt, 512 * j:512 * (j + 1)]).then_inc(stored, 16)
            sp.wait_ge(stored, 64)

        @block.gpsimd
        def _(pool):
            n_own = [0]

            def own(ins):
                n_own[0] += 1
                ins.then_inc(pool_chain, 1)
                pool.wait_ge(pool_chain, n_own[0])

            g = nc.gpsimd
            own(g.memset(cst[:, 0:zeroed], 0.0))
            own(g.memset(half_ones[0:HD, 0:HD], 1.0))
            own(g.memset(half_ones[HD:P, HD:P], 1.0))
            for q in range(NQ):
                own(g.memset(blk[NC * q:NC * (q + 1), q, :], 1.0))
            own(g.memset(keep, 1.0))
            own(g.memset(keep.rearrange("p (c t) -> p c t", t=NC)[:, :, 0:1], 0.0))
            own(g.memset(eps[:, 0:1], 1e-6))
            own(g.memset(eps[:, 1:2], 64e-5))
            own(g.affine_select(out=ident, in_=ident, compare_op=ALU.not_equal, fill=1.0, base=0,
                                pattern=[[-1, P]], channel_multiplier=1))
            for half in range(2):
                part = id64[HD * half:HD * (half + 1), :]
                own(g.affine_select(out=part, in_=part, compare_op=ALU.not_equal, fill=1.0, base=0,
                                    pattern=[[-1, HD]], channel_multiplier=1))
            bf = blk.rearrange("p q t -> p (q t)")
            own(g.affine_select(out=gmask[:, 0, :], in_=bf, compare_op=ALU.is_gt, fill=0.0, base=0,
                                pattern=[[1, P]], channel_multiplier=-1))
            g.affine_select(out=gmask[:, 1, :], in_=bf, compare_op=ALU.is_ge, fill=0.0, base=0,
                            pattern=[[1, P]], channel_multiplier=-1).then_inc(consts, 1)
            pool.wait_ge(consts, 1)
            g.memset(lora_w[HD:P, :], 0.0).then_inc(consts, 1)
            pool.wait_ge(consts, 2)
            g.memset(lora_a[0:HD, :], 0.0).then_inc(consts, 1)
            pool.wait_ge(consts, 3)
            g.memset(raw[:, :, 0:1], 0.0).then_inc(consts, 1)
            pool.wait_ge(consts, 4)
            own(g.memset(eb[0:H, 0:2, :], 0.0))
            ext = eb[0:H, 0:2, :].rearrange("p a b -> p (a b)")
            g.dma_start(ext[:, 127:319], rel_bias[0]).then_inc(bias_in, 16)
            pool.wait_ge(bias_in, 16)
            g.tensor_scalar(ext[:, 0:127], ext[:, 0:127], ext[:, 127:128], None,
                            ALU.add).then_inc(bias_ext, 1)
            pool.wait_ge(bias_ext, 1)
            g.dma_start(bias_d, ext[:, 0:384]).then_inc(bias_dram, 16)
            pool.wait_ge(bias_dram, 16)
            g.dma_start(skew_d, bass.AP(bias_d.tensor, 0, [[0, P], [1, H * 384]])).then_inc(bias_dram, 16)
            pool.wait_ge(bias_dram, 32)
            toeplitz = bass.AP(skew_d.tensor, P - 1, [[H * 384 - 1, P], [384, H], [1, T]])
            g.dma_start(eb[:, :, :], toeplitz).then_inc(bias_in, 16)
            pool.wait_ge(bias_in, 32)
            g.memset(eb[0:HD, :, P + HD:T], NEG).then_inc(bias_ok, 1)
            pool.wait_ge(bias_ok, 1)

            pool.wait_ge(ls_ok, 1)
            g.tensor_tensor(tmp, ls, sg, ALU.subtract).then_inc(shifted, 1)
            pool.wait_ge(exps, 5)
            own(g.memset(xt, 0.0))
            for half in range(2):
                part = xt[HD * half:HD * (half + 1), :, :]
                g.affine_select(out=part, in_=part, compare_op=ALU.not_equal, fill=1.0,
                                base=16 * half, pattern=[[1, NC // 2], [-1, NC]],
                                channel_multiplier=0).then_inc(xt_zero, 1)
                pool.wait_ge(xt_zero, half + 1)
            pool.wait_ge(acol_ok, 2)
            g.dma_start(acol_d, acol.rearrange("p s i -> p (s i)")).then_inc(acol_dram, 16)
            pool.wait_ge(acol_dram, 16)
            av = acol_d.rearrange("(q t) (s i) -> q s t i", t=NC, i=NC)
            for half in range(2):
                for q in range(NQ):
                    p0 = HD * half + NS * q
                    g.dma_start(prob[p0:p0 + NS, :, :], av[q]).then_inc(prob_in, 16)
            pool.wait_ge(ends_ok, 1)
            for r_ in range(2):
                g.memset(kt[r_][rows_of(1 - r_), :, :], 0.0).then_inc(kt_zero, 1)
                pool.wait_ge(kt_zero, r_ + 1)
            sqv = qk_sq.rearrange("p (t a w) -> p t a w", t=TT, a=2)
            for j in range(4):
                pool.wait_ge(proj_out, len(RW_GROUPS) + j + 1)
                qv = qk[:, :, j // 2, 256 * (j % 2):256 * (j % 2 + 1)]
                g.tensor_tensor(sqv[:, :, j // 2, 256 * (j % 2):256 * (j % 2 + 1)], qv, qv,
                                ALU.mult).then_inc(qk_sqd, 1)
            pool.wait_ge(inv_ok, 1)
            g.dma_start(inv_d, xt.rearrange("p j t -> p (j t)")).then_inc(inv_dram, 16)
            pool.wait_ge(inv_dram, 16)
            iv = inv_d.rearrange("(f q s) (j t) -> q f j s t", f=2, q=NQ, j=NC // 2)
            for half in range(2):
                for q in range(NQ):
                    p0 = NC * q + NC // 2 * half
                    g.dma_start(dt[p0:p0 + NC // 2, :, :], iv[q, half]).then_inc(dt_in, 16)
            for tt in range(TT):
                if tt:
                    pool.wait_ge(st_ps, 4 * NQ)
                    pool.wait_ge(rm_ok, 3)
                pool.wait_ge(qk_sum, 4)
                for b in range(NP):
                    ins = g.tensor_tensor(
                        mt[:, b, :, :],
                        id64.unsqueeze(1).broadcast_to([P, NQ, HD]),
                        pend[:, b, NQ * tt:NQ * (tt + 1)].unsqueeze(2).broadcast_to([P, NQ, HD]),
                        ALU.mult)
                    ins.then_inc(diag_ok, 1)
            pool.wait_ge(diag_ok, NP * TT)
            pool.wait_ge(y_ps, TT)
            pool.wait_ge(st_ok, 8 * NQ)
            own(g.memset(eb_up, 0.0))
            own(g.memset(eb_dn, 0.0))
            g.dma_start(eb_up[0:E, :], b_up[0]).then_inc(moe_in, 16)
            g.dma_start(eb_dn[0:E, :], b_down[0]).then_inc(moe_in, 16)
            g.dma_start(g2, norm2_g[0:1, :].broadcast_to([P, D])).then_inc(moe_in, 16)
            g.dma_start(wr, w_router[0].rearrange("(k p) e -> p k e", p=P)).then_inc(moe_in, 16)
            g.dma_start(br[0:E, :], b_router[0].rearrange("(e o) -> e o", o=1)).then_inc(moe_in, 16)
            pool.wait_ge(rw_ok, TT)
            own(g.iota(iota_i[:, :], pattern=[[1, CAP]], base=0, channel_multiplier=0))
            own(g.tensor_copy(iota, iota_i[:, :]))
            own(g.memset(ones, 1.0))
            own(g.memset(ones16[:, :], 1.0))
            own(g.memset(nought16[:, :], 0.0))
            own(g.memset(place, 1000.0))
            own(g.affine_select(out=before[:, :], in_=ones16[:, :], compare_op=ALU.is_gt, fill=0.0, base=0,
                                pattern=[[1, P]], channel_multiplier=-1))
            g.memset(gated, 0.0).then_inc(moe_consts, 1)

        @block.scalar
        def _(act):
            n_own = [0]

            def own(ins):
                n_own[0] += 1
                ins.then_inc(act_chain, 1)
                act.wait_ge(act_chain, n_own[0])

            s = nc.scalar
            for src, r0 in ROWS[:ACT_ROWS]:
                n = src.shape[0] // P
                act.dma_start(rows[r0:r0 + n, :], src.rearrange("(r c) -> r c", c=P)).then_inc(rows_in, 16)
            for tt in range(TT):
                act.wait_ge(x_in[tt], 16)
                own(s.activation(htok[:, tt, :], xs[:, tt, :], ACT.Square, accum_out=stat[:, tt:tt + 1]))
            act.wait_ge(consts, 1)
            s.activation(stat[:, 2:4], stat[:, 0:2], ACT.Sqrt, bias=eps[:, 0:1],
                         scale=1.0 / D).then_inc(rms_root, 1)
            act.dma_start(wup[0:HD, :], w_decay_up[0]).then_inc(lora_in, 16)
            act.dma_start(wup[HD:P, :], w_aaa_up[0]).then_inc(lora_in, 16)
            act.dma_start(wgu, w_gate_up[0]).then_inc(lora_in, 16)

            def copy_group(gi):
                act.wait_ge(proj_ps, gi + 1)
                if gi:
                    act.wait_ge(mixed, gi)
                else:
                    act.wait_ge(consts, 4)
                ps = bank[5 + gi % 2][:, :].rearrange("p (b t) -> p b t", b=2)
                s.activation(raw[:, :, 1:T + 1], ps, ACT.Copy).then_inc(proj_out, 1)

            copy_group(0)
            act.wait_ge(mixed, 1)
            s.activation(lora_w[0:HD, :], lora[0:HD, 0, :], ACT.Tanh).then_inc(lora_act, 1)
            s.activation(lora_a[HD:P, :], lora[HD:P, 0, :], ACT.Copy).then_inc(lora_act, 1)
            s.activation(lora_g, lora[:, 1, :], ACT.Sigmoid).then_inc(lora_act, 1)
            copy_group(1)
            act.wait_ge(vec_ok, 1)
            act.wait_ge(lora_ps, 1)
            for b in range(NP):
                ps = bank[b // 2][:, T * (b % 2):T * (b % 2 + 1)]
                ins = s.activation(sg[:, b, :], ps, ACT.Sigmoid, bias=vec[:, V_W0 + b:V_W0 + b + 1])
            ins.then_inc(lora_out, 1)
            act.wait_ge(lora_ps, 2)
            for b in range(NP):
                ps = bank[2 + b // 2][:, T * (b % 2):T * (b % 2 + 1)]
                ins = s.activation(aa[:, b, :], ps, ACT.Sigmoid, bias=vec[:, V_A0 + b:V_A0 + b + 1])
            ins.then_inc(lora_out, 1)
            act.wait_ge(lora_ps, 3)
            for j, bk in enumerate((4, 7)):
                ins = s.activation(gate[:, 2 * j:2 * j + 2, :].rearrange("p b t -> p (b t)"),
                                   bank[bk][:, :], ACT.Copy)
            ins.then_inc(lora_out, 1)
            copy_group(2)
            act.wait_ge(ls_ok, 1)
            lsv = ls.rearrange("p b (c t) -> p (b c) t", t=P)
            s.activation(ar[:, :, 1, :], lsv, ACT.Exp, scale=-EXP_M05).then_inc(exps, 1)
            s.activation(be, ls, ACT.Exp, scale=EXP_M05).then_inc(exps, 1)
            ends = ls.rearrange("p b (c t) -> p b c t", t=NC)[:, :, :, NC - 1]
            s.activation(pend, ends, ACT.Exp, scale=-EXP_M05).then_inc(exps, 1)
            act.wait_ge(ls_ok, 2)
            s.activation(bend, tm2, ACT.Exp, scale=EXP_M05).then_inc(exps, 1)
            act.wait_ge(shifted, 1)
            s.activation(ar[:, :, 0, :], tmp.rearrange("p b (c t) -> p (b c) t", t=P), ACT.Exp,
                         scale=-EXP_M05).then_inc(exps, 1)
            copy_group(3)
            act.wait_ge(kk_ps, 1)
            for j in range(2):
                ins = s.activation(bonus[:, 2 * j:2 * j + 2, :].rearrange("p b t -> p (b t)"),
                                   bank[j][:, :], ACT.Sqrt)
            ins.then_inc(kk_root, 1)
            for gi in range(4, 6):
                copy_group(gi)
            for par in range(2):
                act.wait_ge(acol_ps, par + 1)
                s.activation(acol[:, NS // 2 * par:NS // 2 * (par + 1), :].rearrange("p s i -> p (s i)"),
                             bank[par][:, 0:T], ACT.Copy).then_inc(acol_ok, 1)
            copy_group(6)

            for j in range(len(AT_GROUPS)):
                if j == len(AT_GROUPS) - 1:
                    act.wait_ge(qk_sum, 4)
                    s.activation(stat[:, 40:72], stat[:, 8:40], ACT.Sqrt, bias=eps[:, 0:1],
                                 scale=1.0 / HD).then_inc(qk_root, 1)
                n = len(RW_GROUPS) + j
                act.wait_ge(proj_ps, n + 1)
                ps = bank[5 + n % 2][:, :].rearrange("p (t c) -> p t c", t=TT)
                c0 = 256 * (j % 2)
                dst = (qk[:, :, j // 2, c0:c0 + 256] if j < 4 else va[:, :, c0:c0 + 256])
                s.activation(dst, ps, ACT.Copy).then_inc(proj_out, 1)
            for i in range(2):
                act.wait_ge(qkt_ps, i + 1)
                s.activation(qt[:, 2 * i:2 * i + 2, :].rearrange("p b t -> p (b t)"), bank[i][:, :],
                             ACT.Copy, scale=vec[:, V_QG:V_QG + 1]).then_inc(qkt_ok, 1)
            act.wait_ge(kt_zero, 2)
            for i in range(2):
                act.wait_ge(qkt_ps, 2 + i + 1)
                for r_ in range(2):
                    ins = s.activation(
                        kt[r_][rows_of(r_), 2 * i:2 * i + 2, :].rearrange("p b t -> p (b t)"),
                        bank[2 + i][rows_of(r_), :], ACT.Copy, scale=vec[rows_of(r_), V_KG:V_KG + 1])
                ins.then_inc(qkt_ok, 1)

            def exp_scores(b):
                act.wait_ge(sc_max, b + 1)
                at0 = 76 + 12 * (b % 2)
                for i in range(2):
                    for half, (c0, c1) in enumerate(((0, T), (T, 3 * P))):
                        k_ = 2 * half + i
                        sv = sc[:, 2 * (b % 2) + i, c0:c1]
                        ins = s.activation(sv, sv, ACT.Exp, bias=stat[:, at0 + 4 + k_:at0 + 5 + k_],
                                           accum_out=stat[:, at0 + 8 + k_:at0 + 9 + k_])
                ins.then_inc(sc_exp, 1)

            exp_scores(0)
            for b in range(NP):
                if b < NP - 1:
                    exp_scores(b + 1)
                if b == NP - 2:
                    act.wait_ge(qk_sum, 4)
                    for tt in range(TT):
                        act.wait_ge(v_ps, tt + 1)
                        s.activation(vtok[:, tt, :], bank[tt][:, :], ACT.Copy).then_inc(v_ok, 1)
                for h in (2 * b, 2 * b + 1):
                    act.wait_ge(pt_ps, h + 1)
                    if h >= 2:
                        act.wait_ge(at_ps, h - 1)
                    s.activation(pt[:, h % 2, :], bank[4 if h % 2 == 0 else 7][:, 0:3 * P],
                                 ACT.Copy).then_inc(pt_ok, 1)
                if b % 2:
                    act.wait_ge(at_ps, 2 * b + 2)
                    s.activation(at[:, b - 1:b + 1, :].rearrange("p b t -> p (b t)"),
                                 bank[5 + b // 2][:, :], ACT.Copy).then_inc(at_ok, 1)

            def token_alpha(tt):
                act.wait_ge(turn_ps, tt + 1)
                if tt:
                    act.wait_ge(wu_ps, 2)
                hv = bank[0][:, :].rearrange("p (h k) -> p h k", h=H)
                s.activation(rr[:, :, 0:HD], hv, ACT.Copy).then_inc(turn_ok, 1)

            def kappa_ends(tt):
                act.wait_ge(ends_ps, 2 * tt + 2)
                if tt:
                    act.wait_ge(st_ps, 4 * NQ)
                ps = bank[3][:, :].rearrange("p (h k) -> p h k", h=H)
                for q in range(NQ):
                    ins = s.activation(kbd[:, :, q, :], ps, ACT.Copy, scale=blk[:, q, 0:1])
                ins.then_inc(kbd_ok, 1)

            def solved(tt):
                act.wait_ge(akv_ps, tt + 1)
                hv = bank[0][:, :].rearrange("p (h k) -> p h k", h=H)
                s.activation(rr[:, :, HD:P], hv, ACT.Copy).then_inc(akv_ok, 1)
                for j in range(2):
                    act.wait_ge(wu_ps, 2 * tt + j + 1)
                    s.activation(wu[:, 4 * j:4 * j + 4, :].rearrange("p h c -> p (h c)"),
                                 bank[1 + j][:, :], ACT.Copy).then_inc(wu_ok, 1)

            def states_out(tt):
                if tt:
                    act.wait_ge(y_ps, tt)
                for q in range(NQ):
                    for b in range(NP):
                        act.wait_ge(st_ps, 4 * NQ * tt + NP * q + b + 1)
                        s.activation(st[:, b, q + 1, :], bank[6 + b % 2][:, 0:HD],
                                     ACT.Copy).then_inc(st_ok, 1)

            def result_out(tt):
                act.wait_ge(y_ps, tt + 1)
                s.activation(yy[:, :, P * tt:P * (tt + 1)],
                             bank[0][:, :].rearrange("p (b t) -> p b t", b=NP), ACT.Copy).then_inc(y_ok, 1)

            def group_root(tt):
                act.wait_ge(ln_ps, 2 * tt + 2)
                s.activation(tmpn[:, :, P * tt:P * (tt + 1)],
                             bank[7][:, :].rearrange("p (b t) -> p b t", b=NP), ACT.Sqrt,
                             bias=eps[:, 1:2], scale=1.0 / HD).then_inc(ln_root, 1)

            token_alpha(0)
            kappa_ends(0)
            solved(0)
            states_out(0)
            act.wait_ge(st_ok, 4 * NQ)
            act.wait_ge(y_ps, 1)
            s.activation(st[:, :, 0, :], st[:, :, NQ, :], ACT.Copy).then_inc(st_first, 1)
            result_out(0)
            token_alpha(1)
            kappa_ends(1)
            group_root(0)
            solved(1)
            states_out(1)
            result_out(1)
            group_root(1)
            for tt in range(TT):
                act.wait_ge(res_ok, 2 * tt + 2)
                own(s.activation(xn[:, tt, :], xs[:, tt, :], ACT.Square, accum_out=stat[:, tt:tt + 1]))
                s.activation(stat[:, 2 + tt:3 + tt], stat[:, tt:tt + 1], ACT.Sqrt, bias=eps[:, 0:1],
                             scale=1.0 / D).then_inc(n2_root, 1)
            for tt in range(TT):
                act.wait_ge(top_ok, tt + 1)
                s.activation(tope[:, tt, :], top[:, tt, 0:TOP_K], ACT.Exp, bias=topn[:, tt:tt + 1],
                             accum_out=tops[:, tt:tt + 1]).then_inc(top_exp, 1)

            def gather_out(i):
                act.wait_ge(xg_ps, i + 1)
                s.activation(xg, bank[6][:, :], ACT.Copy).then_inc(xg_ok, 1)
                act.wait_ge(xgt_ps, i + 1)
                s.activation(xgt.rearrange("p j c -> p (j c)"), bank[6][:, :],
                             ACT.Copy).then_inc(xgt_ok, 1)

            def expert(i, g):
                act.wait_ge(glu_ok, i + 1)
                s.activation(sig, glu, ACT.Sigmoid, scale=ALPHA).then_inc(sig_ok, 1)
                gather_out(g + 1)
                act.wait_ge(actt_ps, i + 1)
                s.activation(actt.rearrange("p j c -> p (j c)"), bank[7][:, :],
                             ACT.Copy).then_inc(actt_ok, 1)
                act.wait_ge(slot_used, UNITS * i + UNITS)
                s.activation(ye, bank[7][:, :], ACT.Copy).then_inc(ye_ok, 1)

            gather_out(0)
            with act.Fori(0, E) as e:
                expert(e, e)
            crowd = act.value_load(most_u[0:1, 0:1])
            with act.If(crowd > CAP):
                with act.Fori(1, PASSES) as p_:
                    gather_out(p_ * (E + 1))
                    with act.Fori(0, E) as e:
                        expert(p_ * E + e, p_ * (E + 1) + e)
            for i in (1, 3):
                act.wait_ge(acc_x, i + 1)
                s.activation(out_s[:, i // 2, 512:D], bank[i][:, :], ACT.Copy).then_inc(out_ok_act, 1)

        @block.tensor
        def _(pe):
            t = nc.tensor
            pe.wait_ge(consts, 1)
            for i in range(WARM):
                t.matmul(bank[5][:, 0:P], nought, nought, start=True, stop=True)
            for tt in range(TT):
                pe.wait_ge(h_tok, tt + 1)
                if tt:
                    pe.wait_ge(rows_in, 16 * 13)
                    t.transpose(bank[0][:, 0:NVEC], rows[0:NVEC, :],
                                ident[0:NVEC, 0:NVEC]).then_inc(rows_ps, 1)
                for k in range(KD):
                    ins = t.transpose(bank[1 + k // 2][:, T * (k % 2) + P * tt:T * (k % 2) + P * (tt + 1)],
                                      htok[:, tt, P * k:P * (k + 1)], ident)
                    ins.then_inc(ht_ps, 1) if tt and k % 2 else None

            def project(n):
                pe.wait_ge(slot_full[slot_of(n)], 16 * (n // PRE_SLOTS + 1))
                if n >= 2:
                    pe.wait_ge(proj_out, n - 1)
                w = slot(slot_of(n)).rearrange("p (k n) -> p k n", k=KD)
                ps = bank[5 + n % 2]
                for j in range(2):
                    for k in range(KD):
                        if n == 0 and j == 0 and k % 2 == 0:
                            pe.wait_ge(ht_ok, k // 2 + 1)
                        if n < len(RW_GROUPS):
                            l, r = w[:, k, P * j:P * (j + 1)], ht[:, k, :]
                        else:
                            l, r = ht[:, k, P * j:P * (j + 1)], w[:, k, :]
                        ins = t.matmul(ps[:, T * j:T * (j + 1)], l, r, start=(k == 0), stop=(k == KD - 1))
                ins.then_inc(proj_ps, 1)

            def head_sums(banks, src, sem_):
                for j in range(2):
                    ins = t.matmul(bank[banks[j]][:, :], half_ones,
                                   src[:, 2 * j:2 * j + 2, :].rearrange("p b t -> p (b t)"),
                                   start=True, stop=True)
                    ins.then_inc(sem_, 1) if sem_ is not None and j else None

            project(0)
            project(1)
            pe.wait_ge(lora_in, 48)
            pe.wait_ge(consts, 3)
            pe.wait_ge(lora_act, 3)
            pe.wait_ge(vec_ok, 1)
            for w, rhs, banks in ((wup, lora_w, (0, 1)), (wup, lora_a, (2, 3)), (wgu, lora_g, (4, 7))):
                for b in range(NP):
                    ins = t.matmul(bank[banks[b // 2]][:, T * (b % 2):T * (b % 2 + 1)],
                                   w[:, P * b:P * (b + 1)], rhs, start=True, stop=True)
                ins.then_inc(lora_ps, 1)
            project(2)
            project(3)
            pe.wait_ge(kk_sq, 1)
            pe.wait_ge(lora_out, 1)
            head_sums((0, 1), bonus, kk_ps)
            project(4)
            project(5)
            pe.wait_ge(alpha_beta, 1)
            pe.wait_ge(kk_root, 1)
            for par in range(2):
                for b in range(NP):
                    for tt in range(TT):
                        h = 2 * b + par
                        s_ = set_of(h, tt) % (NS // 2)
                        for q in range(NQ):
                            ins = t.matmul(bank[par][NC * q:NC * (q + 1), NC * s_:NC * (s_ + 1)],
                                           ar[rows_of(h), TT * b + tt, 0, NC * q:NC * (q + 1)],
                                           be[rows_of(h), b, P * tt + NC * q:P * tt + NC * (q + 1)],
                                           start=True, stop=True, tile_position=(HD * par, NC * q))
                ins.then_inc(acol_ps, 1)
            project(6)
            project(7)
            project(8)
            pe.wait_ge(bonus_in, 1)
            pe.wait_ge(lora_out, 2)
            head_sums((2, 3), tmp, bonus_ps)
            for n in range(9, n_proj):
                project(n)

            pe.wait_ge(qk_ok, 1)
            pe.wait_ge(acol_ok, 2)
            pe.wait_ge(elem_ok, 1)
            for a_ in range(2):
                for i in range(2):
                    for j in range(4):
                        b, tt = 2 * i + j // 2, j % 2
                        ins = t.transpose(bank[2 * a_ + i][:, P * j:P * (j + 1)],
                                          qk[:, tt, a_, P * b:P * (b + 1)], ident)
                    ins.then_inc(qkt_ps, 1)
            pe.wait_ge(qkt_ok, 4)

            def scores(b):
                if b >= 2:
                    pe.wait_ge(sc_max, b - 1)
                for r_ in range(2):
                    ps = bank[2 * (b % 2) + r_]
                    t.matmul(ps[:, 0:T], qt[:, b, P:T], kt[r_][:, b, :], start=True, stop=True)
                    t.matmul(ps[:, T:3 * P], qt[:, b, 0:P], kt[r_][:, b, 0:P],
                             start=True, stop=True).then_inc(sc_ps, 1)

            def attend(b):
                pe.wait_ge(probs_ok, b + 1)
                for h in (2 * b, 2 * b + 1):
                    if h >= 2:
                        pe.wait_ge(pt_ok, h - 1)
                    for j in range(3):
                        ins = t.transpose(bank[4 if h % 2 == 0 else 7][:, P * j:P * (j + 1)],
                                          sc[:, 2 * (b % 2) + h % 2, P * j:P * (j + 1)], ident)
                    ins.then_inc(pt_ps, 1)
                for h in (2 * b, 2 * b + 1):
                    pe.wait_ge(pt_ok, h + 1)
                    c0 = T * (b % 2)
                    ps = bank[5 + b // 2][rows_of(h), c0:c0 + T]
                    v = va[:, :, HD * h:HD * (h + 1)]
                    t.matmul(ps[:, 0:P], v[:, 0, :], pt[:, h % 2, T:3 * P], start=True, stop=True)
                    t.matmul(ps[:, P:T], v[:, 0, :], pt[:, h % 2, 0:P], start=True, stop=False)
                    t.matmul(ps[:, P:T], v[:, 1, :], pt[:, h % 2, P:T], start=False,
                             stop=True).then_inc(at_ps, 1)

            def turn_v():
                pe.wait_ge(sc_max, NP - 1)
                for u in range(TT):
                    for b in range(NP):
                        ins = t.transpose(bank[u][:, P * b:P * (b + 1)],
                                          mv[:, b, P * u:P * (u + 1)], ident)
                    ins.then_inc(v_ps, 1)

            def turn_ends(tt):
                if tt:
                    pe.wait_ge(wu_ok, 2)
                    pe.wait_ge(rm_ok, 1)
                for bk, src in ((2, bend), (3, kend)):
                    for b in range(NP):
                        ins = t.transpose(bank[bk][:, P * b:P * (b + 1)],
                                          src[:, b, P * tt:P * (tt + 1)], ident)
                    ins.then_inc(ends_ps, 1)

            def turn_alpha(tt):
                if tt:
                    pe.wait_ge(y_ok, 1)
                else:
                    pe.wait_ge(v_ok, 1)
                for b in range(NP):
                    ins = t.transpose(bank[0][:, P * b:P * (b + 1)], ar[:, TT * b + tt, 0, :], ident)
                ins.then_inc(turn_ps, 1)

            def pair_products(tt, par, qs):
                for q in qs:
                    for b in range(NP):
                        rows_ = rows_of(par)
                        for g0, src in ((0, ka), (1, be)):
                            c0 = P * b + 2 * NC * g0
                            ins = t.matmul(bank[4 + par][NC * q:NC * (q + 1), c0:c0 + NC * (2 - g0)],
                                           src[rows_, b, P * tt + NC * q:P * tt + NC * (q + 1)],
                                           ar[rows_, TT * b + tt, g0:2, NC * q:NC * (q + 1)],
                                           start=True, stop=True, tile_position=(HD * par, NC * q))
                ins.then_inc(gm_ps, 1) if NQ - 1 in qs else None

            def a_k_v(tt):
                pe.wait_ge(turn_ok, tt + 1)
                for par in range(2):
                    pe.wait_ge(gm_ok, 2 * tt + par + 1)
                    for h in range(par, H, 2):
                        ins = t.matmul(bank[0][:, HD * h:HD * (h + 1)], gm[tt][:, h, 0, :],
                                       vtok[:, tt, HD * h:HD * (h + 1)], start=True, stop=True)
                ins.then_inc(akv_ps, 1)

            def solve(tt):
                pe.wait_ge(ttb_ok, tt + 1)
                pe.wait_ge(v_ok, TT)
                pe.wait_ge(akv_ok, tt + 1)
                pe.wait_ge(bbd_ok, tt + 1)
                for h in range(H):
                    ins = t.matmul(bank[1 + h // 4][:, P * (h % 4):P * (h % 4 + 1)], ttb[:, h, :],
                                   rr[:, h, :], start=True, stop=True)
                    ins.then_inc(wu_ps, 1) if h % 4 == 3 else None
                pe.wait_ge(kbd_ok, tt + 1)
                pe.wait_ge(wu_ok, 2 * tt + 2)
                for h in range(H):
                    ins = t.matmul(bank[3][rows_of(h), P * (h // 2):P * (h // 2 + 1)],
                                   wu[:, h, 0:HD], gm[tt][:, h, 2, :], start=True, stop=True)
                ins.then_inc(rm_ps, 1)
                for h in range(H):
                    b = h // 2
                    ins = t.matmul(bank[4 + b // 2][rows_of(h), T * (b % 2):T * (b % 2 + 1)],
                                   wu[:, h, 0:HD], bbd[:, h, :, :].rearrange("p q k -> p (q k)"),
                                   start=True, stop=True)
                    ins.then_inc(rm_ps, 1) if h % 4 == 3 else None
                pe.wait_ge(rm_ok, 3 * tt + 3)
                if tt:
                    pe.wait_ge(st_first, 1)

            def states(tt, q):
                for b in range(NP):
                    n = 4 * NQ * tt + NP * q + b
                    if n >= 2:
                        pe.wait_ge(st_ok, n - 1)
                    first = tt == 0 and q == 0
                    for h in (2 * b, 2 * b + 1):
                        ps = bank[6 + b % 2][rows_of(h), 0:HD]
                        t.matmul(ps, bbd[:, h, q, :], wu[:, h, HD:P], start=True, stop=False)
                        ins = t.matmul(ps, kbd[:, h, q, :], vtok[:, tt, HD * h:HD * (h + 1)],
                                       start=False, stop=first)
                        if not first:
                            ins = t.matmul(ps, mt[rows_of(h), b, q, :], st[rows_of(h), b, q, :],
                                           start=False, stop=True)
                    ins.then_inc(st_ps, 1)

            def read_out(tt):
                pe.wait_ge(st_ok, 4 * NQ * tt + 3 * NP)
                for b in range(NP):
                    for h in (2 * b, 2 * b + 1):
                        ps = bank[0][rows_of(h), P * b:P * (b + 1)]
                        t.matmul(ps, wu[:, h, HD:P], gm[tt][:, h, 2, :], start=True, stop=False)
                        t.matmul(ps, vtok[:, tt, HD * h:HD * (h + 1)], gm[tt][:, h, 1, :], start=False,
                                 stop=False)
                        for q in range(0 if tt else 1, NQ):
                            ins = t.matmul(ps[:, NC * q:NC * (q + 1)], st[rows_of(h), b, q, :],
                                           rt[rows_of(h), b, NC * q:NC * (q + 1)], start=False,
                                           stop=(q == NQ - 1))
                ins.then_inc(y_ps, 1)

            def tile_sums(tt, bk, src):
                t.matmul(bank[bk][:, :], half_ones, src[:, :, P * tt:P * (tt + 1)],
                         start=True, stop=True).then_inc(ln_ps, 1)

            def mix_out(tt, k):
                n = n_proj + k // 2
                pe.wait_ge(slot_full[slot_of(n)], 16 * (n // PRE_SLOTS + 1))
                w = slot(slot_of(n)).rearrange("p (k n) -> p k n", k=2)
                for j in range(2):
                    ins = t.matmul(bank[((1, 2), (3, 4))[tt][j]][:, :],
                                   (at if k < NP else yy)[:, k % NP, P * tt:P * (tt + 1)],
                                   w[:, k % 2, 512 * j:512 * (j + 1)],
                                   start=(k == 0), stop=(k == KD - 1))
                    ins.then_inc(wo_used, 1) if k == KD - 1 else None
                ins.then_inc(wo_slot, 1) if tt and k % 2 and k < KD - 1 else None

            scores(0)
            scores(1)
            pe.wait_ge(lora_out, 3)
            pe.wait_ge(proj_out, n_proj)
            for b in range(NP):
                if b + 2 < NP:
                    scores(b + 2)
                if b == NP - 2:
                    turn_v()
                if b == NP - 1:
                    pe.wait_ge(ends_ok, 1)
                    pe.wait_ge(sc_max, NP)
                    turn_ends(0)
                    turn_alpha(0)
                attend(b)

            def logits_of(tt):
                cols_ = slice(P * tt, P * (tt + 1))
                for k in range(KD):
                    if k % 4 == 0:
                        pe.wait_ge(xnt_ok, 2 * tt + k // 4 + 1)
                    ins = t.matmul(bank[7 - 3 * tt][0:E, cols_], wr[:, k, :], xnt[:, k, cols_],
                                   start=(k == 0), stop=(k == KD - 1))
                ins.then_inc(lgt_ps, 1)

            def turn_xn(tt):
                pe.wait_ge(xn_ok, tt + 1)
                pe.wait_ge(ln_root, 2)
                for i in range(2):
                    if tt:
                        pe.wait_ge(xnt_ok, i + 1)
                    for j in range(4):
                        k = 4 * i + j
                        ins = t.transpose(bank[5 + i][:, P * j:P * (j + 1)],
                                          xn[:, tt, P * k:P * (k + 1)], ident)
                    ins.then_inc(xnt_ps, 1)

            pe.wait_ge(rank_ok, 1)
            pe.wait_ge(pt_ok, 7)
            pe.wait_ge(at_ok, 1)
            pair_products(0, 0, range(NQ))
            pair_products(0, 1, range(NQ))
            a_k_v(0)
            solve(0)
            pe.wait_ge(pt_ok, 8)
            pe.wait_ge(at_ok, 2)
            for q in range(NQ):
                states(0, q)
                if q == 0:
                    turn_ends(1)
                    pair_products(1, 0, range(2))
                elif q < 3:
                    pair_products(1, q - 1, range(2, NQ)) if q == 1 else pair_products(1, 1, range(NQ))
            read_out(0)
            turn_alpha(1)
            tile_sums(0, 6, yy)
            a_k_v(1)
            pe.wait_ge(ln_sq, 1)
            tile_sums(0, 7, sqy)
            solve(1)
            pe.wait_ge(ln_root, 1)
            for q in range(NQ):
                states(1, q)
                mix_out(0, q)
            read_out(1)
            for k in (0, 1):
                mix_out(1, k)
            pe.wait_ge(y_ok, 2)
            pe.wait_ge(st_ok, 8 * NQ)
            tile_sums(1, 6, yy)
            for k in (2, 3):
                mix_out(1, k)
            pe.wait_ge(ln_sq, 2)
            tile_sums(1, 7, sqy)
            pe.wait_ge(rw_ok, 1)
            for k in range(NP, KD):
                mix_out(0, k)
            pe.wait_ge(rw_ok, 2)
            for k in (4, 5, 6):
                mix_out(1, k)
            turn_xn(0)
            mix_out(1, 7)
            logits_of(0)
            turn_xn(1)
            logits_of(1)
            for tt in range(TT):
                pe.wait_ge(xnt_ok, 4)
                pe.wait_ge(lgt_ok, tt + 1)
                t.transpose(bank[5 + tt][:, 0:E], lgt[0:E, P * tt:P * (tt + 1)],
                            ident[0:E, 0:E]).then_inc(logit_ps, 1)

            def open_sums(banks):
                for i in banks:
                    t.matmul(bank[i][:, :], ident, xs[:, i // 2, 512 * (i % 2):512 * (i % 2 + 1)],
                             start=True, stop=False).then_inc(acc_open, 1)

            pe.wait_ge(res_ok, 4)
            open_sums((0, 1))
            pe.wait_ge(member_ok, 1)
            pe.wait_ge(moe_consts, 1)
            m = [member16[:, tt, :] for tt in range(TT)]
            t.matmul(bank[7][:, 0:E], before[:, :], m[0], start=True, stop=True)
            t.matmul(bank[7][:, E:2 * E], ones16[:, :], m[0], start=True, stop=False)
            t.matmul(bank[7][:, E:2 * E], before[:, :], m[1], start=False, stop=True)
            t.matmul(bank[7][:, 2 * E:3 * E], ones16[:, :], m[0], start=True, stop=False)
            t.matmul(bank[7][:, 2 * E:3 * E], ones16[:, :], m[1], start=False,
                     stop=True).then_inc(place_ps, 1)
            open_sums((2, 3))

            def gather(i):
                pe.wait_ge(pick_ok, i + 1)
                for tt in range(TT):
                    for n in range(2):
                        ins = t.matmul(bank[6][CAP * n:CAP * (n + 1), :], pick[:, tt, :],
                                       xn[:, tt, 512 * n:512 * (n + 1)],
                                       start=(tt == 0), stop=(tt == TT - 1))
                ins.then_inc(xg_ps, 1)

            def gather_turn(i):
                pe.wait_ge(xg_ok, i + 1)
                for j in range(4):
                    ins = t.transpose(bank[6][:, P * j:P * (j + 1)], xg[:, P * j:P * (j + 1)], ident)
                ins.then_inc(xgt_ps, 1)

            def expert(step, r, i, g, p_=0):

                def unit(j):
                    u = UNITS * r + j
                    s_ = u % MOE_SLOTS
                    loads = earlier[s_] + u // MOE_SLOTS + 1
                    pe.wait_ge(full[s_], 16 * ROUNDS * step + 16 * pass_loads[s_] * p_ + 16 * loads)
                    return expert_slot(s_)

                pe.wait_ge(chosen_ok, i + 1)
                for part in range(2):
                    for n in range(2):
                        c0 = D * part + 512 * n
                        t.matmul(bank[4 + part][CAP * n:CAP * (n + 1), :], chosen,
                                 eb_up[:, c0:c0 + 512], start=True, stop=False)
                pe.wait_ge(xgt_ok, g + 1)
                for k in range(KD):
                    w = unit(k)
                    for part in range(2):
                        for n in range(2):
                            c0 = D * part + 512 * n
                            ins = t.matmul(bank[4 + part][CAP * n:CAP * (n + 1), :],
                                           xgt[:, k % 4, CAP * (k // 4):CAP * (k // 4 + 1)],
                                           w[:, c0:c0 + 512], start=False, stop=(k == KD - 1))
                    ins.then_inc(slot_used, 1)
                gather(g + 1)
                gather_turn(g + 1)
                pe.wait_ge(acts_ok, i + 1)
                for j in range(4):
                    ins = t.transpose(bank[7][:, P * j:P * (j + 1)], acts[:, P * j:P * (j + 1)], ident)
                ins.then_inc(actt_ps, 1)
                pe.wait_ge(gated_ok, i + 1)
                pe.wait_ge(xgt_ok, g + 2)
                for n in range(2):
                    for tt in range(TT):
                        j = TT * n + tt
                        ins = t.transpose(bank[6][:, P * j:P * (j + 1)],
                                          gated[:, tt, 2 * n:2 * n + 2, :].rearrange("p a c -> p (a c)"),
                                          ident)
                ins.then_inc(sct_ps, 1)
                pe.wait_ge(actt_ok, i + 1)
                for n in range(2):
                    t.matmul(bank[7][CAP * n:CAP * (n + 1), :], chosen,
                             eb_dn[:, 512 * n:512 * (n + 1)], start=True, stop=False)
                for k in range(KD):
                    if k % 2 == 0:
                        w = unit(KD + k // 2).rearrange("p (k n) -> p k n", k=2)
                    for n in range(2):
                        ins = t.matmul(bank[7][CAP * n:CAP * (n + 1), :],
                                       actt[:, k % 4, CAP * (k // 4):CAP * (k // 4 + 1)],
                                       w[:, k % 2, 512 * n:512 * (n + 1)], start=False,
                                       stop=(k == KD - 1))
                    ins.then_inc(slot_used, 1) if k % 2 else None
                pe.wait_ge(ye_ok, i + 1)
                pe.wait_ge(sct_ok, i + 1)
                for tt in range(TT):
                    for n in range(2):
                        t.matmul(bank[2 * tt + n][:, :], sct[:, n, tt, :], ye, start=False, stop=False)

            pe.wait_ge(routed, 1)
            gather(0)
            gather_turn(0)
            def experts(p_):
                with pe.Fori(0, STEPS) as n:
                    for r in range(GROUP):
                        e = GROUP * n + r
                        expert(n, r, p_ * E + e, p_ * (E + 1) + e, p_)
                for r in range(LEFT):
                    e = GROUP * STEPS + r
                    expert(STEPS, r, p_ * E + e, p_ * (E + 1) + e, p_)

            experts(0)
            crowd = pe.value_load(most_u[0:1, 0:1])
            with pe.If(crowd > CAP):
                with pe.Fori(1, PASSES) as p_:
                    gather(p_ * (E + 1))
                    gather_turn(p_ * (E + 1))
                    experts(p_)
            for i in range(4):
                t.matmul(bank[i][:, :], nought16[:, 0:P], nought16[:, :], start=False,
                         stop=True).then_inc(acc_x, 1)

        @block.vector
        def _(dve):
            n_own = [0]

            def own(ins):
                n_own[0] += 1
                ins.then_inc(vec_chain, 1)
                dve.wait_ge(vec_chain, n_own[0])

            v = nc.vector
            tt_ = v.tensor_tensor

            def cols_of(r0, n, width):
                return vec[:, r0:r0 + n].unsqueeze(2).broadcast_to([P, n, width])

            dve.wait_ge(rms_root, 1)
            own(v.reciprocal(stat[:, 4:6], stat[:, 2:4]))
            for tt in range(TT):
                v.tensor_scalar(htok[:, tt, :], xs[:, tt, :], stat[:, 4 + tt:5 + tt], None,
                                ALU.mult).then_inc(h_tok, 1)
            dve.wait_ge(rows_ps, 1)
            v.tensor_copy(vec[:, 0:NVEC], bank[0][:, 0:NVEC]).then_inc(vec_ok, 1)
            dve.wait_ge(vec_ok, 1)
            for i in range(4):
                dve.wait_ge(ht_ps, i + 1)
                tt_(ht[:, 2 * i:2 * i + 2, :], bank[1 + i][:, :].rearrange("p (k t) -> p k t", k=2),
                    cols_of(V_G1 + 2 * i, 2, T), ALU.mult).then_inc(ht_ok, 1)

            def mix(gi):
                g = RW_GROUPS[gi]
                dve.wait_ge(proj_out, gi + 1)
                own(tt_(dd, raw[:, :, 0:T], raw[:, :, 1:T + 1], ALU.subtract))
                for j in range(2):
                    dst = lora[:, j, :] if g == 6 else (mr, mk, mv)[g // 2][:, 2 * (g % 2) + j, :]
                    ins = v.scalar_tensor_tensor(
                        out=dst, in0=dd[:, j, :], scalar=vec[:, V_MU + 2 * g + j:V_MU + 2 * g + j + 1],
                        in1=raw[:, j, 1:T + 1], op0=ALU.mult, op1=ALU.add)
                ins.then_inc(mixed, 1)

            mix(0)
            mix(1)
            dve.wait_ge(lora_out, 1)
            for b in range(NP):
                ins = v.tensor_tensor_scan(ls[:, b, :], keep, sg[:, b, :], 0.0, ALU.mult, ALU.add)
            ins.then_inc(ls_ok, 1)
            dve.wait_ge(ls_ok, 1)
            lc = ls.rearrange("p b (c t) -> p (b c) t", t=NC)
            tt_(tm2.rearrange("p b (c t) -> p (b c) t", t=NC), lc,
                lc[:, :, NC - 1:NC].broadcast_to([P, NP * T // NC, NC]), ALU.subtract).then_inc(ls_ok, 1)
            mix(2)
            dve.wait_ge(mixed, 3)
            tt_(kk, mk, cols_of(V_KK, NP, T), ALU.mult).then_inc(kk_ok, 1)
            dve.wait_ge(kk_ok, 1)
            tt_(bonus, kk, kk, ALU.mult).then_inc(kk_sq, 1)
            dve.wait_ge(lora_out, 2)
            own(v.tensor_scalar(stat[:, 72:76], vec[:, V_KA:V_KA + NP], -1.0, 1.0, ALU.mult, ALU.add))
            for b in range(NP):
                ins = v.tensor_scalar(kend[:, b, :], aa[:, b, :], vec[:, V_KA + b:V_KA + b + 1],
                                      stat[:, 72 + b:73 + b], ALU.mult, ALU.add)
            own(ins)
            own(tt_(mk, mk, kend, ALU.mult))
            dve.wait_ge(exps, 4)
            tt_(ka, mk, be, ALU.mult)
            own(tt_(kend, mk, bend, ALU.mult))
            mix(3)
            dve.wait_ge(kk_root, 1)
            own(v.tensor_scalar(bonus, bonus, 1e-12, None, ALU.max))
            own(v.reciprocal(bonus, bonus))
            own(tt_(kk, kk, bonus, ALU.mult))
            own(tt_(aa, aa, kk, ALU.mult))
            dve.wait_ge(exps, 5)
            v.scalar_tensor_tensor(out=ar[:, :, 0, :], in0=kk.rearrange("p b (c t) -> p (b c) t", t=P),
                                   scalar=-1.0, in1=ar[:, :, 0, :], op0=ALU.mult, op1=ALU.mult)
            tt_(be, aa, be, ALU.mult).then_inc(alpha_beta, 1)
            tt_(bend, aa, bend, ALU.mult).then_inc(ends_ok, 1)
            mix(4)
            dve.wait_ge(mixed, 5)
            tt_(ar[:, :, 1, :], mr.rearrange("p b (c t) -> p (b c) t", t=P), ar[:, :, 1, :],
                ALU.mult).then_inc(rank_ok, 1)
            own(tt_(tmp, mr, mk, ALU.mult))
            tt_(tmp, tmp, cols_of(V_RK, NP, T), ALU.mult).then_inc(bonus_in, 1)
            mix(5)
            mix(6)

            def substitute(i0, i1):
                for i in range(i0, i1):
                    n = NC - 1 - i
                    if i == 0:
                        dve.wait_ge(prob_in, 16 * 8)
                        dve.wait_ge(xt_zero, 2)
                    u = xtmp[:, :, 0:n]
                    own(tt_(u, xt[:, :, i:i + 1].broadcast_to([P, NC // 2, n]),
                            prob[:, i + 1:NC, i].unsqueeze(1).broadcast_to([P, NC // 2, n]), ALU.mult))
                    ins = tt_(xt[:, :, i + 1:NC], xt[:, :, i + 1:NC], u, ALU.add)
                    if i == NC - 2:
                        ins.then_inc(inv_ok, 1)
                    else:
                        own(ins)

            substitute(0, SUB0)
            dve.wait_ge(bonus_ps, 1)
            dve.wait_ge(mixed, 7)
            for j in range(2):
                ins = tt_(bonus[:, 2 * j:2 * j + 2, :].rearrange("p b t -> p (b t)"), bank[2 + j][:, :],
                          mv[:, 2 * j:2 * j + 2, :].rearrange("p b t -> p (b t)"), ALU.mult)
            ins.then_inc(elem_ok, 1)
            for j in range(4):
                dve.wait_ge(qk_sqd, j + 1)
                v.tensor_reduce(
                    stat[:, 8:40].rearrange("p (t a h) -> p t a h", t=TT, a=2)[
                        :, :, j // 2, 4 * (j % 2):4 * (j % 2) + 4],
                    qk_sq.rearrange("p (t a h c) -> p t a h c", t=TT, a=2, h=H)[
                        :, :, j // 2, 4 * (j % 2):4 * (j % 2) + 4, :],
                    AX.X, ALU.add).then_inc(qk_sum, 1)
            v.tensor_scalar(vec[:, V_QG:V_QG + 1], vec[:, V_QG:V_QG + 1], HD ** -0.5, None, ALU.mult)
            dve.wait_ge(qk_root, 1)
            own(v.reciprocal(stat[:, 40:72], stat[:, 40:72]))
            qkg = qk.rearrange("p t a (h c) -> p (t a h) c", c=HD)
            tt_(qkg, qkg, stat[:, 40:72].unsqueeze(2).broadcast_to([P, 32, HD]),
                ALU.mult).then_inc(qk_ok, 1)
            substitute(SUB0, SUB1)

            def biased_scores(b):
                if b >= 2:
                    dve.wait_ge(pt_ps, 2 * b - 2)
                else:
                    dve.wait_ge(bias_ok, 1)
                c0, at0 = 2 * (b % 2), 76 + 12 * (b % 2)
                for i in range(2):
                    h = 2 * b + i
                    dve.wait_ge(sc_ps, h + 1)
                    tt_(sc[:, c0 + i, 0:T], bank[c0 + i][:, 0:T], eb[:, h, :], ALU.add)
                    ins = tt_(sc[:, c0 + i, T:3 * P], bank[c0 + i][:, T:3 * P], eb[:, h, P:T], ALU.add)
                own(ins)
                v.tensor_reduce(stat[:, at0:at0 + 2], sc[:, c0:c0 + 2, 0:T], AX.X, ALU.max)
                own(v.tensor_reduce(stat[:, at0 + 2:at0 + 4], sc[:, c0:c0 + 2, T:3 * P], AX.X, ALU.max))
                v.tensor_scalar(stat[:, at0 + 4:at0 + 8], stat[:, at0:at0 + 4], -1.0, None,
                                ALU.mult).then_inc(sc_max, 1)

            def scaled_probs(b):
                dve.wait_ge(sc_exp, b + 1)
                c0, at0 = 2 * (b % 2), 76 + 12 * (b % 2)
                sums = stat[:, at0 + 8:at0 + 12]
                own(v.reciprocal(sums, sums))
                tt_(sc[:, c0:c0 + 2, 0:T], sc[:, c0:c0 + 2, 0:T],
                    sums[:, 0:2].unsqueeze(2).broadcast_to([P, 2, T]), ALU.mult)
                tt_(sc[:, c0:c0 + 2, T:3 * P], sc[:, c0:c0 + 2, T:3 * P],
                    sums[:, 2:4].unsqueeze(2).broadcast_to([P, 2, P]), ALU.mult).then_inc(probs_ok, 1)

            biased_scores(0)
            for b in range(NP):
                if b == 0:
                    biased_scores(1)
                scaled_probs(b)
                if b + 2 < NP:
                    biased_scores(b + 2)
                    substitute((SUB1, SUB2)[b], (SUB2, NC - 1)[b])

            blkc = blk[:, :, 0:1]

            def beta_ends(tt):
                dve.wait_ge(ends_ps, 2 * tt + 1)
                if tt:
                    dve.wait_ge(st_ps, 4 * NQ)
                else:
                    dve.wait_ge(inv_dram, 16)
                ps = bank[2][:, :].rearrange("p (h k) -> p h k", h=H)
                for q in range(NQ):
                    ins = v.tensor_scalar(bbd[:, :, q, :], ps, blkc[:, q, :], None, ALU.mult)
                ins.then_inc(bbd_ok, 1)

            def chunk_matrices(tt):
                for par in range(2):
                    dve.wait_ge(gm_ps, 2 * tt + par + 1)
                    for b in range(NP):
                        for g0, g1 in ((0, 2), (2, 3)):
                            c0 = P * b + NC * g0
                            ins = tt_(
                                gm[tt][:, 2 * b + par, g0:g1, :].rearrange("p g (q t) -> p g q t", t=NC),
                                bank[4 + par][:, c0:c0 + NC * (g1 - g0)].rearrange(
                                    "p (g t) -> p g t", t=NC).unsqueeze(2).broadcast_to([P, g1 - g0, NQ, NC]),
                                gmask[:, g0 // 2:, :].rearrange("p g (q t) -> p g q t", t=NC), ALU.mult)
                    ins.then_inc(gm_ok, 1)

            def inverses(tt):
                if tt:
                    dve.wait_ge(wu_ps, 2)
                else:
                    dve.wait_ge(dt_in, 16 * 8)
                dts = dt.rearrange("p (r b t) i -> p r b t i", r=2, t=TT)
                for par in range(2):
                    for q in range(NQ):
                        tv = ttb.rearrange("p (b r) c -> p r b c", r=2)[:, par, :, NC * q:NC * (q + 1)]
                        ins = v.tensor_scalar(tv, dts[:, par, :, tt, :], blkc[:, q, :], None, ALU.mult)
                ins.then_inc(ttb_ok, 1)

            def transitions(tt):
                dve.wait_ge(rm_ps, 3 * tt + 1)
                if tt:
                    dve.wait_ge(y_ps, 1)
                tt_(rt, bank[3][:, :].rearrange("p (b t) -> p b t", b=NP),
                    ar.rearrange("p (b u) g t -> p u b g t", u=TT)[:, tt, :, 1, :], ALU.add).then_inc(rm_ok, 1)
                dve.wait_ge(diag_ok, NP * (tt + 1))
                for j in range(2):
                    dve.wait_ge(rm_ps, 3 * tt + 2 + j)
                    mv_ = mt[:, 2 * j:2 * j + 2, :, :].rearrange("p b q k -> p (b q k)")
                    tt_(mv_, bank[4 + j][:, :], mv_, ALU.add).then_inc(rm_ok, 1)

            def centred(tt):
                dve.wait_ge(ln_ps, 2 * tt + 1)
                yv = yy[:, :, P * tt:P * (tt + 1)]
                own(v.scalar_tensor_tensor(out=yv, in0=bank[6][:, :].rearrange("p (b t) -> p b t", b=NP),
                                           scalar=-1.0 / HD, in1=yv, op0=ALU.mult, op1=ALU.add))
                tt_(sqy[:, :, P * tt:P * (tt + 1)], yv, yv, ALU.mult).then_inc(ln_sq, 1)

            def gated_result(tt):
                dve.wait_ge(ln_root, tt + 1)
                cols_ = slice(P * tt, P * (tt + 1))
                yv, rv = yy[:, :, cols_], tmpn[:, :, cols_]
                own(v.reciprocal(rv, rv))
                own(tt_(yv, yv, rv, ALU.mult))
                for b in range(NP):
                    ins = v.tensor_scalar(yy[:, b, cols_], yy[:, b, cols_], vec[:, V_LG + b:V_LG + b + 1],
                                          vec[:, V_LB + b:V_LB + b + 1], ALU.mult, ALU.add)
                own(ins)
                own(tt_(yv, yv, bonus[:, :, cols_], ALU.add))
                tt_(yv, yv, gate[:, :, cols_], ALU.mult).then_inc(rw_ok, 1)

            beta_ends(0)
            chunk_matrices(0)
            inverses(0)
            transitions(0)
            chunk_matrices(1)
            inverses(1)
            beta_ends(1)
            centred(0)
            transitions(1)
            gated_result(0)
            centred(1)
            gated_result(1)
            dve.wait_ge(moe_in, 80)
            for tt in range(TT):
                for i in (2 * tt, 2 * tt + 1):
                    dve.wait_ge(wo_used, i + 1)
                    xv = xs[:, i // 2, 512 * (i % 2):512 * (i % 2 + 1)]
                    tt_(xv, bank[1 + i][:, :], xv, ALU.add).then_inc(res_ok, 1)
                dve.wait_ge(n2_root, tt + 1)
                own(v.reciprocal(stat[:, 4 + tt:5 + tt], stat[:, 2 + tt:3 + tt]))
                v.scalar_tensor_tensor(out=xn[:, tt, :], in0=xs[:, tt, :], scalar=stat[:, 4 + tt:5 + tt],
                                       in1=g2, op0=ALU.mult, op1=ALU.mult).then_inc(xn_ok, 1)
                for i in range(2):
                    dve.wait_ge(xnt_ps, 2 * tt + i + 1)
                    v.tensor_copy(xnt[:, 4 * i:4 * i + 4, P * tt:P * (tt + 1)],
                                  bank[5 + i][:, :].rearrange("p (k t) -> p k t", k=4)).then_inc(xnt_ok, 1)
            dve.wait_ge(moe_consts, 1)
            for tt in range(TT):
                lt = lgt[0:E, P * tt:P * (tt + 1)]
                dve.wait_ge(lgt_ps, tt + 1)
                v.tensor_scalar(lt, bank[7 - 3 * tt][0:E, P * tt:P * (tt + 1)], br[0:E, 0:1], None,
                                ALU.add).then_inc(lgt_ok, 1)
            for tt in range(TT):
                dve.wait_ge(logit_ps, tt + 1)
                own(v.tensor_copy(logits[:, tt, :], bank[5 + tt][:, 0:E]))
                own(v.max(top[:, tt, :], logits[:, tt, :]))
                v.tensor_scalar(topn[:, tt:tt + 1], top[:, tt, 0:1], -1.0, None, ALU.mult).then_inc(top_ok, 1)
                own(v.max_index(topi_u[:, tt, :], top[:, tt, :], logits[:, tt, :]))
            own(v.tensor_copy(topi, topi_u[:, :, 0:TOP_K]))
            own(tt_(hot, iota[:, 0:E].unsqueeze(1).broadcast_to([P, TT * TOP_K, E]),
                    topi.rearrange("p t k -> p (t k)").unsqueeze(2).broadcast_to([P, TT * TOP_K, E]),
                    ALU.is_equal))
            own(v.tensor_reduce(member, hot.rearrange("p (t k) e -> p t e k", t=TT), AX.X, ALU.add))
            v.tensor_copy(member16[:, :, :], member).then_inc(member_ok, 1)
            dve.wait_ge(top_exp, TT)
            own(v.reciprocal(tops, tops))
            own(tt_(tope, tope, tops.unsqueeze(2).broadcast_to([P, TT, TOP_K]), ALU.mult))
            own(tt_(hotg, hot,
                    tope.rearrange("p t k -> p (t k)").unsqueeze(2).broadcast_to([P, TT * TOP_K, E]),
                    ALU.mult))
            own(v.tensor_reduce(gates, hotg.rearrange("p (t k) e -> p t e k", t=TT), AX.X, ALU.add))
            dve.wait_ge(member_ok, 1)
            own(v.scalar_tensor_tensor(out=place[:, :, 0:E], in0=member, scalar=-1000.0,
                                       in1=place[:, :, 0:E], op0=ALU.mult, op1=ALU.add))
            dve.wait_ge(place_ps, 1)
            own(tt_(place[:, :, 0:E], bank[7][:, 0:2 * E].rearrange("p (t e) -> p t e", t=TT),
                    place[:, :, 0:E], ALU.add))
            own(v.tensor_reduce(most, bank[7][:, 2 * E:3 * E], AX.X, ALU.max))

            def picks(e):
                for tt in range(TT):
                    ins = v.tensor_scalar(pick[:, tt, :], iota, place[:, tt, bass.ds(e, 1)], None,
                                          ALU.is_equal)
                ins.then_inc(pick_ok, 1)

            def expert(e, i, g):
                v.tensor_scalar(chosen, ones[:, 0:CAP], ident[:, bass.ds(e, 1)], None,
                                ALU.mult).then_inc(chosen_ok, 1)
                for tt in range(TT):
                    ins = v.tensor_scalar(gated[:, tt, 0::3, :],
                                          iota.unsqueeze(1).broadcast_to([P, 2, CAP]),
                                          place[:, tt, bass.ds(e, 1)], gates[:, tt, bass.ds(e, 1)],
                                          ALU.is_equal, ALU.mult)
                ins.then_inc(gated_ok, 1)
                dve.wait_ge(xg_ps, g + 1)
                picks(e + 1)
                dve.wait_ge(slot_used, UNITS * i + KD)
                v.tensor_scalar(glu, bank[4][:, :], LIMIT, None, ALU.min).then_inc(glu_ok, 1)
                v.tensor_scalar(lin, bank[5][:, :], -LIMIT, LIMIT, ALU.max, ALU.min).then_inc(lin_ok, 1)
                dve.wait_ge(lin_ok, i + 1)
                v.scalar_tensor_tensor(out=lin, in0=lin, scalar=1.0, in1=glu, op0=ALU.add,
                                       op1=ALU.mult).then_inc(gl_ok, 1)
                dve.wait_ge(gl_ok, i + 1)
                dve.wait_ge(sig_ok, i + 1)
                tt_(acts, lin, sig, ALU.mult).then_inc(acts_ok, 1)
                dve.wait_ge(sct_ps, i + 1)
                v.tensor_copy(sct.rearrange("p n t c -> p (n t c)"), bank[6][:, :]).then_inc(sct_ok, 1)
                dve.wait_ge(slot_used, UNITS * i + UNITS)

            v.tensor_copy(most_u[:, :], most).then_inc(routed, 1)
            picks(0)
            with dve.Fori(0, E) as e:
                expert(e, e, e)
            crowd = dve.value_load(most_u[0:1, 0:1])
            with dve.If(crowd > CAP):
                with dve.Fori(1, PASSES) as p_:
                    v.tensor_scalar(place, place, -float(CAP), None, ALU.add).then_inc(moved, 1)
                    dve.wait_ge(moved, p_)
                    dve.wait_ge(xg_ps, p_ * (E + 1))
                    picks(0)
                    with dve.Fori(0, E) as e:
                        expert(e, p_ * E + e, p_ * (E + 1) + e)
            for i in (0, 2):
                dve.wait_ge(acc_x, i + 1)
                v.tensor_copy(out_s[:, i // 2, 0:512], bank[i][:, :]).then_inc(out_ok, 1)


_INS = ["x", "norm1_g", "w_in", "tshift_mu", "q_norm_g", "k_norm_g", "rel_bias", "w0", "w_decay_up",
        "a0", "w_aaa_up", "w_gate_up", "k_k", "k_a", "r_k", "ln_x_g", "ln_x_b", "w_out", "norm2_g",
        "w_router", "b_router", "w_up", "b_up", "w_down", "b_down"]
_OUTS = [((1, T, D), "float32")]


def kernel(**inputs):
    import numpy as _np
    import concourse.bacc as _bacc
    from concourse import mybir as _mybir
    from concourse.bass_utils import run_bass_kernel_spmd as _run

    nc = _bacc.Bacc("TRN2", target_bir_lowering=False, num_devices=1)
    arrays, args = {}, []
    for name in _INS:
        a = _np.ascontiguousarray(inputs[name])
        arrays[f"in_{name}_dram"] = a
        args.append(nc.dram_tensor(f"in_{name}_dram", a.shape, _mybir.dt.from_np(a.dtype), kind="ExternalInput").ap())
    for i, (shape, dtype) in enumerate(_OUTS):
        dt = _mybir.dt.from_np(_np.dtype(dtype))
        args.append(nc.dram_tensor(f"out_{i}_dram", shape, dt, kind="ExternalOutput").ap())
    hybrid_block(nc, *args)
    r = _run(nc, [arrays], core_ids=[0])
    return r.results[0]["out_0_dram"]
```
